# Optimizing a Trainium2 kernel written in Bass

```python
import jax, jax.numpy as jnp
from jax import lax
import numpy as np

D_MODEL = 1024
BATCH = 1
SEQ = 512
DEPTH = 1

N_HEADS = 8
HEAD_DIM = 64
ATTN_WIDTH = N_HEADS * HEAD_DIM
MOBA_BLOCK = 256
MOBA_TOPK = 3
Q_CHUNK = 128
POOL_WINDOWS = (2, 4, 8, 16)
N_POOL_GROUPS = len(POOL_WINDOWS)
POOL_WIDTH = D_MODEL // 2
POOL_GROUP_IN = POOL_WIDTH // N_POOL_GROUPS
POOL_GROUP_OUT = D_MODEL // N_POOL_GROUPS
N_BRANCHES = 2
IN_PROJ_WIDTH = 3 * ATTN_WIDTH + POOL_WIDTH + N_BRANCHES * D_MODEL
N_EXPERT_GROUPS = 4
EXPERTS_PER_GROUP = 8
N_EXPERTS = N_EXPERT_GROUPS * EXPERTS_PER_GROUP
TOP_K_INNER = 2
EXPERT_HIDDEN = 256
N_ADA = 6
EPS = 1e-6

kernel_name = "hybrid_moba_pool_hiermoe_adaln"

def rmsnorm(x, g):
    xf = x.astype(jnp.float32)
    xf = xf * lax.rsqrt(jnp.mean(xf * xf, axis=-1, keepdims=True) + EPS)
    return (xf * g.astype(jnp.float32)).astype(x.dtype)

def modulate(h, shift, scale):
    return h * (1.0 + scale[:, None, :]) + shift[:, None, :]

def moba_attention(q, k, v):
    B, H, S, Dh = q.shape
    nb = -(-S // MOBA_BLOCK)
    pad = nb * MOBA_BLOCK - S
    k_pad = jnp.pad(k, ((0, 0), (0, 0), (0, pad), (0, 0)))
    v_pad = jnp.pad(v, ((0, 0), (0, 0), (0, pad), (0, 0)))
    k_blocks = k_pad.reshape(B, H, nb, MOBA_BLOCK, Dh)
    v_blocks = v_pad.reshape(B, H, nb, MOBA_BLOCK, Dh)
    k_mean = jnp.mean(k_blocks, axis=3)
    n_sel = min(MOBA_TOPK, max(nb - 1, 1))
    scale = HEAD_DIM ** -0.5
    n_chunks = S // Q_CHUNK
    b_ix = jnp.arange(B)[:, None, None, None]
    h_ix = jnp.arange(H)[None, :, None, None]
    block_ids = jnp.arange(nb)

    def one_chunk(ci):
        q0 = ci * Q_CHUNK
        qc = lax.dynamic_slice_in_dim(q, q0, Q_CHUNK, axis=2)
        own = q0 // MOBA_BLOCK
        q_pos = q0 + jnp.arange(Q_CHUNK)
        gate = jnp.einsum('bhqd,bhnd->bhqn', qc, k_mean).astype(jnp.float32)
        gate = jnp.where((block_ids < own)[None, None, None, :], gate, -jnp.inf)
        g_val, idx = lax.top_k(gate, n_sel)
        valid = jnp.isfinite(g_val)
        k_g = k_blocks[b_ix, h_ix, idx]
        v_g = v_blocks[b_ix, h_ix, idx]
        s_sel = jnp.einsum('bhqd,bhqksd->bhqks', qc, k_g).astype(jnp.float32) * scale
        s_sel = jnp.where(valid[..., None], s_sel, -jnp.inf)
        k_own = lax.dynamic_slice_in_dim(k_pad, own * MOBA_BLOCK, MOBA_BLOCK, axis=2)
        v_own = lax.dynamic_slice_in_dim(v_pad, own * MOBA_BLOCK, MOBA_BLOCK, axis=2)
        k_pos = own * MOBA_BLOCK + jnp.arange(MOBA_BLOCK)
        s_own = jnp.einsum('bhqd,bhsd->bhqs', qc, k_own).astype(jnp.float32) * scale
        s_own = jnp.where((k_pos[None, :] <= q_pos[:, None])[None, None], s_own, -jnp.inf)
        s_all = jnp.concatenate([s_sel.reshape(B, H, Q_CHUNK, n_sel * MOBA_BLOCK), s_own], axis=-1)
        p = jax.nn.softmax(s_all, axis=-1)
        p_sel = p[..., :n_sel * MOBA_BLOCK].reshape(B, H, Q_CHUNK, n_sel, MOBA_BLOCK).astype(v.dtype)
        p_own = p[..., n_sel * MOBA_BLOCK:].astype(v.dtype)
        return (jnp.einsum('bhqks,bhqksd->bhqd', p_sel, v_g)
                + jnp.einsum('bhqs,bhsd->bhqd', p_own, v_own))

    out = lax.map(one_chunk, jnp.arange(n_chunks))
    return out.transpose(1, 2, 0, 3, 4).reshape(B, H, S, Dh)

def pool_branch(p, w_pool, pool_scale):
    B, S, _ = p.shape
    pf = p.astype(jnp.float32).reshape(B, S, N_POOL_GROUPS, POOL_GROUP_IN)
    pos = jnp.arange(S)
    outs = []
    for gi, w in enumerate(POOL_WINDOWS):
        xg = pf[:, :, gi]
        cs = jnp.cumsum(xg, axis=1)
        lag = jnp.pad(cs, ((0, 0), (w, 0), (0, 0)))[:, :S]
        cnt = jnp.minimum(pos + 1, w).astype(jnp.float32)[None, :, None]
        outs.append((cs - lag) / cnt - xg)
    pooled = jnp.stack(outs, axis=2).astype(p.dtype)
    y = jnp.einsum('bsgc,gco->bsgo', pooled, w_pool).reshape(B, S, D_MODEL)
    return y * pool_scale

def hier_moe(h, w_router_g, b_router_g, w_router_e, b_router_e, w1, w3, w2):
    B, S, D = h.shape
    T = B * S
    t = h.reshape(T, D)
    g_logits = (t @ w_router_g).astype(jnp.float32) + b_router_g
    g_prob = jax.nn.softmax(g_logits, axis=-1)
    g_top, g_idx = lax.top_k(g_prob, 1)
    e_logits = ((t @ w_router_e).astype(jnp.float32) + b_router_e).reshape(T, N_EXPERT_GROUPS, EXPERTS_PER_GROUP)
    e_in = jnp.take_along_axis(e_logits, g_idx[:, :, None], axis=1)[:, 0]
    e_top, e_idx = lax.top_k(e_in, TOP_K_INNER)
    e_w = jax.nn.softmax(e_top, axis=-1) * g_top
    expert_id = g_idx * EXPERTS_PER_GROUP + e_idx
    combine = jnp.einsum('tk,tke->te', e_w, jax.nn.one_hot(expert_id, N_EXPERTS, dtype=jnp.float32))
    combine = combine.reshape(T, N_EXPERT_GROUPS, EXPERTS_PER_GROUP).astype(h.dtype)
    out = jnp.zeros((T, D), dtype=h.dtype)
    for g in range(N_EXPERT_GROUPS):
        a = jnp.einsum('td,edf->tef', t, w1[g])
        b = jnp.einsum('td,edf->tef', t, w3[g])
        hid = jax.nn.silu(a) * b * combine[:, g, :, None]
        out = out + jnp.einsum('tef,efd->td', hid, w2[g])
    return out.reshape(B, S, D)

def setup_inputs(seed: int = 0) -> dict:
    key = jax.random.key(seed)
    ks = jax.random.split(key, 24)
    f32 = jnp.float32
    L, D = DEPTH, D_MODEL

    def nrm(k, shape, s):
        return jax.random.normal(k, shape, f32) * s

    return {
        "x": nrm(ks[0], (BATCH, SEQ, D), 1.0),
        "c": nrm(ks[1], (BATCH, D), 1.0),
        "w_ada": nrm(ks[2], (L, D, N_ADA * D), 0.5 * D ** -0.5),
        "b_ada": nrm(ks[3], (L, N_ADA * D), 0.01),
        "norm1": 1.0 + nrm(ks[4], (L, D), 0.05),
        "w_in": nrm(ks[5], (L, D, IN_PROJ_WIDTH), D ** -0.5),
        "q_norm": 1.0 + nrm(ks[6], (L, HEAD_DIM), 0.05),
        "k_norm": 1.0 + nrm(ks[7], (L, HEAD_DIM), 0.05),
        "w_attn_up": nrm(ks[8], (L, ATTN_WIDTH, D), ATTN_WIDTH ** -0.5),
        "w_pool": nrm(ks[9], (L, N_POOL_GROUPS, POOL_GROUP_IN, POOL_GROUP_OUT), POOL_GROUP_IN ** -0.5),
        "pool_scale": 1.0 + nrm(ks[10], (L, D), 0.1),
        "w_out": nrm(ks[11], (L, D, D), D ** -0.5),
        "norm2": 1.0 + nrm(ks[12], (L, D), 0.05),
        "w_router_g": nrm(ks[13], (L, D, N_EXPERT_GROUPS), D ** -0.5),
        "b_router_g": nrm(ks[14], (L, N_EXPERT_GROUPS), 0.01),
        "w_router_e": nrm(ks[15], (L, D, N_EXPERTS), D ** -0.5),
        "b_router_e": nrm(ks[16], (L, N_EXPERTS), 0.01),
        "w1": nrm(ks[17], (L, N_EXPERT_GROUPS, EXPERTS_PER_GROUP, D, EXPERT_HIDDEN), D ** -0.5),
        "w3": nrm(ks[18], (L, N_EXPERT_GROUPS, EXPERTS_PER_GROUP, D, EXPERT_HIDDEN), D ** -0.5),
        "w2": nrm(ks[19], (L, N_EXPERT_GROUPS, EXPERTS_PER_GROUP, EXPERT_HIDDEN, D), EXPERT_HIDDEN ** -0.5),
    }

def reference(x, c, w_ada, b_ada, norm1, w_in, q_norm, k_norm, w_attn_up, w_pool, pool_scale,
              w_out, norm2, w_router_g, b_router_g, w_router_e, b_router_e, w1, w3, w2):
    B, S, D = x.shape
    c_act = jax.nn.silu(c)
    splits = [ATTN_WIDTH, 2 * ATTN_WIDTH, 3 * ATTN_WIDTH, 3 * ATTN_WIDTH + POOL_WIDTH,
              3 * ATTN_WIDTH + POOL_WIDTH + D_MODEL]
    for l in range(DEPTH):
        mod = c_act @ w_ada[l] + b_ada[l]
        sh1, sc1, g1, sh2, sc2, g2 = jnp.split(mod, N_ADA, axis=-1)
        h = modulate(rmsnorm(x, norm1[l]), sh1, sc1)
        z = h @ w_in[l]
        q, k, v, p_in, ga, gp = jnp.split(z, splits, axis=-1)
        q = rmsnorm(q.reshape(B, S, N_HEADS, HEAD_DIM), q_norm[l]).transpose(0, 2, 1, 3)
        k = rmsnorm(k.reshape(B, S, N_HEADS, HEAD_DIM), k_norm[l]).transpose(0, 2, 1, 3)
        v = v.reshape(B, S, N_HEADS, HEAD_DIM).transpose(0, 2, 1, 3)
        attn = moba_attention(q, k, v).transpose(0, 2, 1, 3).reshape(B, S, ATTN_WIDTH)
        branch_a = attn @ w_attn_up[l]
        branch_p = pool_branch(p_in, w_pool[l], pool_scale[l])
        merged = jax.nn.sigmoid(ga) * branch_a + jax.nn.sigmoid(gp) * branch_p
        x = x + g1[:, None, :] * (merged @ w_out[l])
        h = modulate(rmsnorm(x, norm2[l]), sh2, sc2)
        x = x + g2[:, None, :] * hier_moe(h, w_router_g[l], b_router_g[l], w_router_e[l], b_router_e[l],
                                          w1[l], w3[l], w2[l])
    return x


_drawn_inputs = setup_inputs


def setup_inputs(seed=0):
    import zlib

    import numpy as np

    out = dict(_drawn_inputs(seed))
    spreads = {}
    factors = {'b_ada': 4.5,
     'norm1': 5.324,
     'q_norm': 8.0,
     'k_norm': 8.0,
     'pool_scale': 3.319,
     'norm2': 3.939,
     'b_router_g': 8.0,
     'b_router_e': 8.0}
    for name, (base, spread) in spreads.items():
        noise = np.random.default_rng([zlib.crc32(name.encode()), seed]).standard_normal(out[name].shape)
        drawn = base * np.exp(spread * noise) if base else spread * noise
        out[name] = __import__('jax').numpy.asarray(drawn.astype(out[name].dtype))
    for name, factor in factors.items():
        out[name] = (out[name] * factor).astype(out[name].dtype)
    return out
```

```python
from contextlib import ExitStack

import concourse.bass as bass
from concourse import mybir

F32 = mybir.dt.float32
BF16 = mybir.dt.bfloat16
I32 = mybir.dt.int32
ALU = mybir.AluOpType
ACT = mybir.ActivationFunctionType
AX = mybir.AxisListType

P = 128
T, D = 512, 1024
TT, KT = T // P, D // P
HEADS, HD = 8, 64
AW = HEADS * HD
HP = AW // P
PW = D // 2
WINDOWS = (2, 4, 8, 16)
NG, EPG = 4, 8
E = NG * EPG
F = 256
FT = F // P
SLOTS = 64
PAIRS = E // 2
MAXB = 2 * T // SLOTS
EPS = 1e-6
NEG = -1e30
CH = 512
RING = 4


def hybrid_trunk(nc, x, c, w_ada, b_ada, norm1, w_in, q_norm, k_norm, w_attn_up, w_pool, pool_scale, w_out,
                 norm2, w_router_g, b_router_g, w_router_e, b_router_e, w1, w3, w2, out):
    x_v = x.rearrange("b (t p) d -> (b t) p d", p=P)
    out_v = out.rearrange("b (t p) d -> (b t) p d", p=P)
    ada_v = w_ada.rearrange("l (p k) n -> (l p) k n", k=KT)
    bada_v = b_ada.rearrange("l (j p k) -> (l p) j k", k=KT, p=P)
    win_v = w_in.rearrange("l (p k) n -> (l p) k n", k=KT)
    wup_v = w_attn_up.rearrange("l (k p) n -> (l p) k n", p=P)
    wout_v = w_out.rearrange("l (k p) n -> (l p) k n", p=P)
    w1_v = w1.rearrange("l g e (p k) f -> (l g e) p (k f)", k=KT)
    w3_v = w3.rearrange("l g e (p k) f -> (l g e) p (k f)", k=KT)
    w2_v = w2.rearrange("l g e (p k) n -> (l g e) p (k n)", k=FT)

    xn2_d = nc.dram_tensor("xn2_scratch", (T, D), F32).ap()
    y_d = nc.dram_tensor("y_scratch", ((E + MAXB) * SLOTS, D), F32).ap()

    ctx = ExitStack()
    with ctx:
        def sb(name, shape, dt=F32):
            return ctx.enter_context(nc.sbuf_tensor(name, shape, dt))

        def sem(name):
            return ctx.enter_context(nc.semaphore(name))

        bank = ctx.enter_context(nc.psum_tensor("bank", [P, 8, CH], F32))

        xs = sb("xs", [P, TT, D])
        hT = sb("hT", [P, KT, T])
        mergedT = sb("mergedT", [P, KT, T])
        outer = sb("outer", [P, 2, 4096])
        g1b = sb("g1b", [P, D])
        g2b = sb("g2b", [P, D])
        arena = sb("arena", [P, 4 * 6144])
        acc = sb("acc", [P, 2, D])
        probs = sb("probs", [P, 2, 2, CH])
        ident = sb("ident", [P, P])
        ones = sb("ones", [P, P])
        identb = sb("identb", [P, P], BF16)
        maskb = sb("maskb", [P, P], BF16)
        lowb = sb("lowb", [P, P], BF16)
        onesb = sb("onesb", [P, P], BF16)
        fold = sb("fold", [P, SLOTS])
        wr = sb("wr", [P, KT, NG + E])
        br = sb("br", [1, NG + E])
        cols = sb("cols", [P, 12, KT])
        ab1 = sb("ab1", [P, 2, KT])
        ab2 = sb("ab2", [P, 2, KT])
        xrel = sb("xrel", [P, 2 * TT])
        cth = cols[:, 10, :]
        recip = sb("recip", [P, 16])
        qkg = sb("qkg", [P, 2])
        st = sb("st", [P, 64])
        ss = sb("ss", [P, 2, 2, 8])
        nhalf = sb("nhalf", [P, 8])
        tokp = sb("tokp", [P, 1 + TT], BF16)
        idx = sb("idx", [P, PAIRS], I32)
        pos = sb("pos", [P, TT, 2], I32)
        xtab = sb("xtab", [P, MAXB + 1], I32)
        cw = sb("cw", [P, 2, TT])
        xbase = sb("xbase", [P, 1])
        idxx = sb("idxx", [P, 1], I32)

        def carve(base, start, *shape):
            n = 1
            for s in shape:
                n *= s
            v = base[:, start:start + n]
            names = "abcd"[:len(shape)]
            if len(shape) == 1:
                return v
            return v.rearrange(f"p ({' '.join(names)}) -> p {' '.join(names)}", **dict(zip(names[1:], shape[1:])))

        AR = arena[:, :]
        OU = outer[:, :, :].rearrange("p a b -> p (a b)")
        slot = [carve(AR, 0, 4096), OU[:, 0:4096], OU[:, 4096:8192], carve(AR, 4096, 4096)]
        qT = carve(AR, 8192, HP, T)
        kT = carve(AR, 10240, HP, T)
        vt = carve(AR, 12288, TT, AW)
        pT = carve(AR, 14336, 4, T)
        attnT = carve(AR, 16384, HP, T)
        sg = carve(AR, 18432, KT, T)
        qn = carve(AR, 22528, 2, AW)
        PT = carve(AR, 22528, 2, 2, TT, P)
        pw = sg[:, 2:4, :].rearrange("p a (b n) -> p (a b) n", b=2)
        ptmp = [sg[:, 4, :], sg[:, 5, :]]
        sqbuf = probs[:, 0, 0, :]
        xn = mergedT[:, :, :].rearrange("p a b -> p (a b)").rearrange("p (t d) -> p t d", t=TT)
        xn2 = hT[:, :, :].rearrange("p a b -> p (a b)").rearrange("p (t d) -> p t d", t=TT)
        h2T = probs[:, :, :, :].rearrange("p a b c -> p (a b c)").rearrange("p (u k t) -> p u k t", u=2, k=KT)
        MG = mergedT[:, :, :].rearrange("p a b -> p (a b)")
        place = MG.bitcast(BF16).rearrange("p (t e s) -> p t e s", t=TT, e=E)
        xg = carve(OU, 0, 2, D)
        xgT = carve(OU, 2048, 2, KT, P)
        absb = carve(OU, 4096, 2, CH)
        ysb = carve(OU, 5120, 2, CH)
        th = carve(OU, 6144, 2, FT, SLOTS)
        sl = carve(OU, 6400, 2, FT, SLOTS)
        hid = carve(OU, 6656, 2, FT, SLOTS)
        iota_s = carve(OU, 6912, SLOTS)
        iota_e = carve(OU, 6976, E)
        iota_g = carve(OU, 7008, NG)
        e64 = carve(OU, 7012, E)
        iota_b = carve(OU, 7044, MAXB)
        w13 = [carve(AR, 6144 * s, 2, KT, F) for s in range(RING)]
        w2s = [carve(AR, 6144 * s + 4096, FT, D) for s in range(RING)]
        yg = carve(AR, 0, TT, 2, D)
        RT = acc[:, :, :].rearrange("p a b -> p (a b)")
        used = [0]

        def work(*shape):
            n = 1
            for k in shape:
                n *= k
            used[0] += n
            assert used[0] <= 2 * D
            return carve(RT, used[0] - n, *shape)

        lg = work(TT, NG + E)
        geq, goh, gdif, gexp, gpen = (work(TT, NG) for _ in range(5))
        gbest, gscore, gsum, best1, best2, score1, edif = (work(TT) for _ in range(7))
        em, eq1, oh1, oh2, maskf, rk, rm = (work(TT, E) for _ in range(7))
        maskm = work(TT * E // 2).bitcast(BF16).rearrange("p (t e) -> p t e", t=TT)
        cnt = work(E)
        nx = [work(E) for _ in range(3)]
        xcmp = work(E, MAXB)
        xsum = work(MAXB)
        posf = work(2, TT)

        CHUNKS = [("ada", 1, 0), ("ada", 1, 1), ("ada", 0, 0), ("ada", 0, 1), ("in", 0), ("in", 1), ("in", 2),
                  ("ada", 2, 0), ("in", 3), ("ada", 2, 1), ("in", 6), ("ada", 3, 0), ("in", 7), ("ada", 3, 1),
                  ("in", 4), ("ada", 4, 0), ("ada", 4, 1), ("in", 5), ("ada", 5, 0), ("ada", 5, 1), ("up",),
                  ("out", 0), ("out", 1)]
        at = {k: n for n, k in enumerate(CHUNKS)}
        ADA = [k for k in CHUNKS if k[0] == "ada"]
        IN = [k for k in CHUNKS if k[0] == "in"]
        UNITS = 4 * len(IN)
        U_V, U_P, U_GP, U_GA = 8, 12, 16, 24
        STEPS = HP * TT

        slot_loaded = [sem(f"slot_loaded{i}") for i in range(4)]
        x_loaded = [sem(f"x_loaded{i}") for i in range(TT)]
        small_loaded = sem("small_loaded")
        late_loaded = sem("late_loaded")
        cact_ready = sem("cact_ready")
        silu_ready = sem("silu_ready")
        g_bias_loaded = sem("g_bias_loaded")
        consts_ready = sem("consts_ready")
        pool_link = sem("pool_link")
        chain = sem("chain")
        x_sq = sem("x_sq")
        x_var = sem("x_var")
        x_rstd = sem("x_rstd")
        xn_ready = sem("xn_ready")
        xT_ready = sem("xT_ready")
        hT_dve = sem("hT_dve")
        hT_act = sem("hT_act")
        ada_used = sem("ada_used")
        col_ready = sem("col_ready")
        ab1_ready = sem("ab1_ready")
        unit_done = sem("unit_done")
        unit_drained_dve = sem("unit_drained_dve")
        unit_drained_act = sem("unit_drained_act")
        qk_sq = sem("qk_sq")
        qk_var = sem("qk_var")
        qk_rstd = sem("qk_rstd")
        qkT_ready = sem("qkT_ready")
        qkT_drained = sem("qkT_drained")
        pooled = sem("pooled")
        scores_ready = sem("scores_ready")
        negmax_ready = sem("negmax_ready")
        probs_raw = sem("probs_raw")
        probs_ready = sem("probs_ready")
        PT_ready = sem("PT_ready")
        PT_drained = sem("PT_drained")
        attn_ready = sem("attn_ready")
        attn_drained = sem("attn_drained")
        side_done = sem("side_done")
        side_drained = sem("side_drained")
        up_done = sem("up_done")
        yo_done = sem("yo_done")
        yo_drained = sem("yo_drained")
        x1_sq = sem("x1_sq")
        x1_var = sem("x1_var")
        x1_rstd = sem("x1_rstd")
        xn2_ready = sem("xn2_ready")
        xn2_stored = sem("xn2_stored")
        h2T_psum = sem("h2T_psum")
        h2T_dve = sem("h2T_dve")
        h2T_act = sem("h2T_act")
        logits_ready = sem("logits_ready")
        exp_in = sem("exp_in")
        exp_out = sem("exp_out")
        mask_ready = sem("mask_ready")
        rank_ready = sem("rank_ready")
        place_ready = sem("place_ready")
        idx_psum = sem("idx_psum")
        idx_ready = sem("idx_ready")
        pos_ready = sem("pos_ready")
        iotas_ready = sem("iotas_ready")
        w13_loaded = [sem(f"w13_loaded{i}") for i in range(RING)]
        w2_loaded = [sem(f"w2_loaded{i}") for i in range(RING)]
        xg_loaded = [sem(f"xg_loaded{i}") for i in range(2)]
        xt_ready = sem("xt_ready")
        xgT_ready = sem("xgT_ready")
        ab_done = sem("ab_done")
        ab_drained = sem("ab_drained")
        st_done = sem("st_done")
        th_ready = sem("th_ready")
        hid_ready = sem("hid_ready")
        y_done = sem("y_done")
        y_drained = sem("y_drained")
        y_stored = [sem(f"y_stored{i}") for i in range(2)]
        yg_loaded = [sem(f"yg_loaded{i}") for i in range(TT)]
        yg_scaled = sem("yg_scaled")
        xtab_ready = sem("xtab_ready")
        x_loaded_w = sem("x_loaded_w")
        x_turns = sem("x_turns")
        x_rel = sem("x_rel")
        x_base = sem("x_base")
        x_place = sem("x_place")
        x_idx_psum = sem("x_idx_psum")
        x_idx = sem("x_idx")
        x_rows = sem("x_rows")
        x_rowsT = sem("x_rowsT")
        x_in = sem("x_in")
        x_ab = sem("x_ab")
        x_ab_drained = sem("x_ab_drained")
        x_st = sem("x_st")
        x_th = sem("x_th")
        x_silu = sem("x_silu")
        x_hid = sem("x_hid")
        x_y = sem("x_y")
        x_y_drained = sem("x_y_drained")
        x_stored = sem("x_stored")
        overflow_done = sem("overflow_done")
        y_filled = sem("y_filled")
        out_ready = sem("out_ready")
        out_stored = sem("out_stored")

        C_, N1, N2, PS, BA = 0, 1, 2, 3, 4
        SMALL, LATE = 8, 6

        def overflow_blocks(eng, body):
            eng.wait_ge(xtab_ready, 1)
            n = eng.value_load(xtab[0:1, MAXB:MAXB + 1], min_val=0, max_val=MAXB)
            with eng.If(n > 0):
                with eng.Fori(0, n) as b:
                    body(b)

        xplace = MG.bitcast(BF16)[:, 0:2 * TT * SLOTS].rearrange("p (n s) -> p n s", s=SLOTS)

        block = ctx.enter_context(nc.Block())

        SIDE = ([("g1", 0), ("g1", 1)] + [("B", m) for m in range(KT)] + [("cols",), ("g2", 0), ("g2", 1)]
                + [("A", m) for m in range(KT)])
        side_no = {k: n for n, k in enumerate(SIDE)}
        FIRST_A = side_no[("A", 0)]

        def side_bank(n):
            return 7 if n < FIRST_A or (n - FIRST_A) % 2 == 0 else 6

        def drained(eng, u):
            if u < U_V:
                eng.wait_ge(unit_drained_dve, u + 1)
            else:
                eng.wait_ge(unit_drained_act, u - U_V + 1)

        @block.sync
        def _(sp):
            for n, k in enumerate(CHUNKS):
                if n >= 4:
                    old = CHUNKS[n - 4]
                    if old[0] == "in":
                        sp.wait_ge(unit_done, 4 * (IN.index(old) + 1))
                    else:
                        sp.wait_ge(ada_used, ADA.index(old) + 1)
                if k[0] == "ada":
                    src = ada_v[:, 4 * k[2]:4 * k[2] + 4, D * k[1]:D * (k[1] + 1)]
                    dst = slot[n % 4].rearrange("p (k n) -> p k n", k=4)
                elif k[0] == "in":
                    src = win_v[:, :, CH * k[1]:CH * (k[1] + 1)]
                    dst = slot[n % 4].rearrange("p (k n) -> p k n", k=KT)
                elif k[0] == "up":
                    src = wup_v
                    dst = slot[n % 4].rearrange("p (k n) -> p k n", k=HP)
                else:
                    src = wout_v[:, :, CH * k[1]:CH * (k[1] + 1)]
                    dst = slot[n % 4].rearrange("p (k n) -> p k n", k=KT)
                sp.dma_start(dst, src).then_inc(slot_loaded[n % 4], 16)
            sp.wait_ge(side_drained, len(SIDE))

            def load(e, s, first):
                if not first:
                    sp.wait_ge(y_done, e - (RING - 1))
                sp.dma_start(w13[s][:, 0].rearrange("p k f -> p (k f)"), w1_v[e]).then_inc(w13_loaded[s], 16)
                sp.dma_start(w13[s][:, 1].rearrange("p k f -> p (k f)"), w3_v[e]).then_inc(w13_loaded[s], 16)
                sp.dma_start(w2s[s].rearrange("p k n -> p (k n)"), w2_v[e]).then_inc(w2_loaded[s], 16)

            for e in range(RING):
                load(e, e, True)
            with sp.Fori(1, E // RING) as i:
                for s in range(RING):
                    load(i * RING + s, s, False)

            def overflow(b):
                e = sp.value_load(xtab[0:1, bass.ds(b, 1)], min_val=0, max_val=E - 1)
                for src, dst in ((w1_v, w13[0][:, 0].rearrange("p k f -> p (k f)")),
                                 (w3_v, w13[0][:, 1].rearrange("p k f -> p (k f)")),
                                 (w2_v, w2s[0].rearrange("p k n -> p (k n)"))):
                    sp.dma_start(dst, src[bass.ds(e, 1)].rearrange("o p n -> (o p) n")).then_inc(x_loaded_w, 16)
                sp.wait_ge(x_y, b + 1)
                sp.sem_inc(x_turns, 1)

            sp.wait_ge(y_done, E)
            overflow_blocks(sp, overflow)
            for t in range(TT):
                sp.wait_ge(out_ready, t + 1)
                sp.dma_start(out_v[t], xs[:, t, :]).then_inc(out_stored, 16)
            sp.wait_ge(out_stored, 16 * TT)

        @block.tensor
        def _(pe):
            mm = nc.tensor.matmul

            def chunk_here(k):
                pe.wait_ge(slot_loaded[at[k] % 4], 16 * (at[k] // 4 + 1))

            def x_transposes(ks, t):
                for k in ks:
                    last = nc.tensor.transpose(bank[:, k, P * t:P * (t + 1)],
                                               xn[:, t, k:D:KT], ident[:, :])
                last.then_inc(xT_ready, 1)

            def unit_half(u, h):
                ch = IN[u // 4]
                w = slot[at[ch] % 4].rearrange("p (k n) -> p k n", k=KT)
                if h == 0:
                    if u % 4 == 0:
                        chunk_here(ch)
                    if u >= 2:
                        drained(pe, u - 2)
                m = P * (u % 4)
                for k in range(4 * h, 4 * h + 4):
                    if u < U_P:
                        last = mm(bank[:, u % 2, :], hT[:, k, m:m + P], w[:, k, :], start=k == 0, stop=k == 7)
                    else:
                        last = mm(bank[:, u % 2, :], w[:, k, m:m + P], hT[:, k, :], start=k == 0, stop=k == 7)
                if h == 1:
                    last.then_inc(unit_done, 1)

            def qk_transposes(u):
                pe.wait_ge(unit_drained_dve, u + 1)
                if u >= 2:
                    pe.wait_ge(qkT_drained, u - 1)
                for j in range(HP):
                    last = nc.tensor.transpose(bank[:, 4 + u % 2, P * j:P * (j + 1)],
                                               qn[:, u % 2, P * j:P * (j + 1)], ident[:, :])
                last.then_inc(qkT_ready, 1)

            def scores(a):
                j, qt = a // TT, a % TT
                if a == 0:
                    pe.wait_ge(qkT_drained, 8)
                else:
                    pe.wait_ge(probs_raw, 2 * a)
                n = P * (qt + 1)
                for h in range(2):
                    r = slice(HD * h, HD * (h + 1))
                    mm(bank[:, 2 + h, 0:n], qT[r, j, P * qt:P * (qt + 1)], kT[r, j, 0:n], start=True, stop=True)
                for h in range(2):
                    last = mm(bank[:, 2 + h, P * qt:n], identb[:, :], maskb[:, :], start=False, stop=True,
                              skip_group_check=True)
                last.then_inc(scores_ready, 1)

            def prob_transposes(a):
                qt = a % TT
                pe.wait_ge(probs_ready, a + 1)
                if a >= 1:
                    pe.wait_ge(PT_drained, a)
                for h in range(2):
                    for kt in range(qt + 1):
                        last = nc.tensor.transpose(bank[:, 4 + h, P * kt:P * (kt + 1)],
                                                   probs[:, a % 2, h, P * kt:P * (kt + 1)], ident[:, :])
                last.then_inc(PT_ready, 1)

            def pv(a):
                j, qt = a // TT, a % TT
                pe.wait_ge(PT_drained, a + 1)
                if a == 0:
                    pe.wait_ge(unit_drained_act, 4)
                if a >= 1:
                    pe.wait_ge(attn_drained, a)
                q = slice(P * (a % 4), P * (a % 4) + P)
                for kt in range(qt + 1):
                    for h in range(2):
                        last = mm(bank[HD * h:HD * (h + 1), 6, q], vt[:, kt, P * j + HD * h:P * j + HD * (h + 1)],
                                  PT[:, a % 2, h, kt, :], start=kt == 0, stop=kt == qt)
                last.then_inc(attn_ready, 1)

            def side(*k):
                n = side_no[k]
                b = side_bank(n)
                if n > FIRST_A + 1:
                    pe.wait_ge(side_drained, n - 1)
                elif n == FIRST_A + 1:
                    pe.wait_ge(attn_drained, STEPS)
                elif n > 0:
                    pe.wait_ge(side_drained, n)
                if k[0] in ("g1", "g2"):
                    pe.wait_ge(ada_used, 6 if k[0] == "g1" else 12)
                    last = mm(bank[:, b, :], ones[:, :], acc[:, k[0] == "g2", CH * k[1]:CH * (k[1] + 1)],
                              start=True, stop=True)
                elif k[0] == "B":
                    m = k[1]
                    pe.wait_ge(pooled, m // 2 + 1)
                    if m == 0:
                        pe.wait_ge(late_loaded, 16 * LATE)
                    last = mm(bank[:, b, :], pw[:, m // 2, P * (m % 2):P * (m % 2) + P], pT[:, m // 2, :],
                              start=True, stop=True)
                elif k[0] == "cols":
                    pe.wait_ge(ada_used, 10)
                    for v in range(2):
                        for kk in range(KT):
                            last = mm(bank[:, b, 8 * v + kk:8 * v + kk + 1], acc[:, v, kk:D:KT], ones[:, 0:1],
                                      start=True, stop=True)
                else:
                    m = k[1]
                    if m == 0:
                        pe.wait_ge(side_drained, n)
                        chunk_here(("up",))
                        pe.wait_ge(attn_drained, STEPS)
                    wu = slot[at[("up",)] % 4].rearrange("p (k n) -> p k n", k=HP)
                    for kk in range(HP):
                        last = mm(bank[:, b, :], wu[:, kk, P * m:P * (m + 1)], attnT[:, kk, :],
                                  start=kk == 0, stop=kk == HP - 1)
                last.then_inc(side_done, 1)

            pe.wait_ge(consts_ready, 1)
            for t in range(TT):
                pe.wait_ge(xn_ready, t + 1)
                x_transposes(range(7), t)
            pe.wait_ge(ada_used, 4)
            for v in range(2):
                for k in range(KT):
                    last = mm(bank[:, 7, 8 * v + k:8 * v + k + 1], acc[:, v, k:D:KT], ones[:, 0:1],
                              start=True, stop=True)
            last.then_inc(col_ready, 1)
            pe.wait_ge(ab1_ready, 1)
            for t in range(TT):
                x_transposes([7], t)
            pe.wait_ge(hT_dve, 4)
            pe.wait_ge(hT_act, 4)

            for u in range(UNITS):
                a = u - U_P
                if 0 <= a < STEPS:
                    scores(a)
                unit_half(u, 0)
                if 1 <= u <= 8:
                    qk_transposes(u - 1)
                if 0 <= a - 1 < STEPS:
                    prob_transposes(a - 1)
                unit_half(u, 1)
                if 0 <= a - 2 < STEPS:
                    pv(a - 2)
                if u in (U_P, U_P + 1):
                    side("g1", u - U_P)
                if U_GP + 1 <= u <= U_GA:
                    side("B", u - 1 - U_GP)
                if u == 27:
                    side("cols")
            side("g2", 0)
            side("g2", 1)
            for m in range(KT):
                side("A", m)

            def project(t, h):
                n = 2 * t + h
                if n >= 2:
                    pe.wait_ge(yo_drained, n - 1)
                if t == 0:
                    chunk_here(("out", h))
                w = slot[at[("out", h)] % 4].rearrange("p (k n) -> p k n", k=KT)
                for k in range(KT):
                    last = mm(bank[:, n % 2, :], mergedT[:, k, P * t:P * (t + 1)], w[:, k, :],
                              start=k == 0, stop=k == KT - 1)
                last.then_inc(yo_done, 1)

            def h2_transposes(t):
                pe.wait_ge(xn2_ready, t + 1)
                if t >= 2:
                    pe.wait_ge(h2T_dve, t - 1)
                    pe.wait_ge(h2T_act, t - 1)
                for k in range(KT):
                    last = nc.tensor.transpose(bank[:, 2 + 2 * (t % 2) + k % 2, P * (k // 2):P * (k // 2 + 1)],
                                               xn2[:, t, k:D:KT], ident[:, :])
                last.then_inc(h2T_psum, 1)

            def router(t):
                pe.wait_ge(h2T_dve, t + 1)
                pe.wait_ge(h2T_act, t + 1)
                o = bank[:, 6, 36 * t:36 * (t + 1)]
                for k in range(KT):
                    mm(o, h2T[:, t % 2, k, :], wr[:, k, :], start=k == 0, stop=False)
                mm(o, ones[0:1, :], br[:, :], start=False, stop=True).then_inc(logits_ready, 1)

            pe.wait_ge(side_drained, len(SIDE))
            for t in range(TT + 2):
                if t < TT:
                    project(t, 0)
                if 0 <= t - 1 < TT:
                    h2_transposes(t - 1)
                if t < TT:
                    project(t, 1)
                if 0 <= t - 2 < TT:
                    router(t - 2)

            pe.wait_ge(mask_ready, 1)
            maskv = maskm
            for t in range(TT):
                for s in range(t):
                    mm(bank[:, 7, 32 * t:32 * (t + 1)], onesb[:, :], maskv[:, s, :], start=s == 0, stop=False)
                mm(bank[:, 7, 32 * t:32 * (t + 1)], lowb[:, :], maskv[:, t, :], start=t == 0, stop=True)
            for s in range(TT):
                last = mm(bank[:, 7, 128:160], onesb[:, :], maskv[:, s, :], start=s == 0, stop=s == TT - 1)
            last.then_inc(rank_ready, 1)
            for g in range(4):
                pe.wait_ge(place_ready, g + 1)
                for q in range(4 * g, 4 * g + 4):
                    for t in range(TT):
                        lhs = place[:, t, 2 * q:2 * q + 2, :].rearrange("p e s -> p (e s)")
                        last = mm(bank[:, 2 + g, q % 4:q % 4 + 1], lhs, tokp[:, 0:1], start=t == 0, stop=False)
                        if t:
                            last = mm(bank[:, 2 + g, q % 4:q % 4 + 1], lhs, tokp[:, 1 + t:2 + t], start=False,
                                      stop=t == TT - 1)
                last.then_inc(idx_psum, 1)

            def gather_transposes(q, b, first):
                pe.wait_ge(xg_loaded[b], (q - b) * 8 + 16)
                if not first:
                    pe.wait_ge(xgT_ready, q)
                for k in range(KT):
                    last = nc.tensor.transpose(bank[:, k // 4, P * (k % 4):P * (k % 4 + 1)],
                                               xg[:, b, k:D:KT], ident[:, :])
                last.then_inc(xt_ready, 1)

            def gate_up(e, q, j, first):
                s = j
                pe.wait_ge(w13_loaded[s], (e - s) * 8 + 32)
                if j % 2 == 0:
                    pe.wait_ge(xgT_ready, q + 1)
                if not first:
                    pe.wait_ge(ab_drained, e - 1)
                for k in range(KT):
                    r = slice(SLOTS * (k % 2), SLOTS * (k % 2 + 1))
                    last = mm(bank[r, 2 + j % 2, :].rearrange("p (w f) -> p w f", w=2),
                              xgT[:, (j // 2) % 2, k, SLOTS * (j % 2):SLOTS * (j % 2 + 1)],
                              w13[s][:, :, k, :], start=k < 2, stop=k >= KT - 2)
                last.then_inc(ab_done, 1)

            def fold_halves(e, j, first):
                pe.wait_ge(ab_drained, e + 1)
                if not first:
                    pe.wait_ge(hid_ready, e - 1)
                for w in range(2):
                    for ft in range(FT):
                        last = mm(bank[:, 4 + j % 2, SLOTS * (2 * w + ft):SLOTS * (2 * w + ft + 1)],
                                  absb[:, j % 2, F * w + ft:F * (w + 1):FT], fold[:, :], start=True, stop=True)
                last.then_inc(st_done, 1)

            def down(e, j, first):
                s = j
                pe.wait_ge(hid_ready, e + 1)
                pe.wait_ge(w2_loaded[s], (e - s) * 4 + 16)
                if not first:
                    pe.wait_ge(y_drained, e - 1)
                for ft in range(FT):
                    for h in range(2):
                        last = mm(bank[SLOTS * h:SLOTS * (h + 1), 6 + j % 2, :], hid[:, j % 2, ft, :],
                                  w2s[s][:, ft, CH * h:CH * (h + 1)], start=ft == 0, stop=ft == FT - 1)
                last.then_inc(y_done, 1)

            def experts(i, peeled):
                for j in range(RING):
                    e = i * RING + j
                    q = i * 2 + j // 2
                    start = peeled and i == 0
                    if not (start and j == 0):
                        fold_halves(e - 1, (j - 1) % RING, start and j - 1 < 2)
                    gate_up(e, q, j, start and j < 2)
                    if not (start and j == 0):
                        down(e - 1, (j - 1) % RING, start and j - 1 < 2)
                    if j % 2 and not (peeled and i == E // RING - 1 and j == RING - 1):
                        gather_transposes(q + 1, (j // 2 + 1) % 2, False)

            pe.wait_ge(idx_ready, 4)
            gather_transposes(0, 0, True)
            experts(0, True)
            with pe.Fori(1, E // RING - 1) as i:
                experts(i, False)
            experts(E // RING - 1, True)
            fold_halves(E - 1, RING - 1, False)
            down(E - 1, RING - 1, False)

            def overflow(b):
                pe.wait_ge(x_place, b + 1)
                for n in range(2 * TT):
                    mm(bank[0:SLOTS, 0, 0:1], xplace[:, n, :], tokp[:, 0:1], start=n == 0, stop=False)
                    last = mm(bank[0:SLOTS, 0, 0:1], xplace[:, n, :], tokp[:, 1 + n % TT:2 + n % TT],
                              start=False, stop=n == 2 * TT - 1)
                last.then_inc(x_idx_psum, 1)
                pe.wait_ge(x_rows, 16 * b + 16)
                for k in range(KT):
                    last = nc.tensor.transpose(bank[:, k // 4, P * (k % 4):P * (k % 4 + 1)],
                                               xg[:, 0, k:D:KT], ident[:, :])
                last.then_inc(x_rowsT, 1)
                pe.wait_ge(x_in, b + 1)
                pe.wait_ge(x_loaded_w, 48 * b + 48)
                for k in range(KT):
                    r = slice(SLOTS * (k % 2), SLOTS * (k % 2 + 1))
                    last = mm(bank[r, 2, :].rearrange("p (w f) -> p w f", w=2), xgT[:, 0, k, 0:SLOTS],
                              w13[0][:, :, k, :], start=k < 2, stop=k >= KT - 2)
                last.then_inc(x_ab, 1)
                pe.wait_ge(x_ab_drained, b + 1)
                for w in range(2):
                    for ft in range(FT):
                        last = mm(bank[:, 4, SLOTS * (2 * w + ft):SLOTS * (2 * w + ft + 1)],
                                  absb[:, 0, F * w + ft:F * (w + 1):FT], fold[:, :], start=True, stop=True)
                last.then_inc(x_st, 1)
                pe.wait_ge(x_hid, b + 1)
                for ft in range(FT):
                    for h in range(2):
                        last = mm(bank[SLOTS * h:SLOTS * (h + 1), 6, :], hid[:, 0, ft, :],
                                  w2s[0][:, ft, CH * h:CH * (h + 1)], start=ft == 0, stop=ft == FT - 1)
                last.then_inc(x_y, 1)

            pe.wait_ge(y_drained, E)
            overflow_blocks(pe, overflow)

        @block.scalar
        def _(act):
            sc = nc.scalar
            act.dma_start(cols[:, C_, :], c.rearrange("b (p k) -> (b p) k", k=KT)).then_inc(small_loaded, 16)
            act.dma_start(cols[:, N1, :], norm1.rearrange("b (p k) -> (b p) k", k=KT)).then_inc(small_loaded, 16)
            act.dma_start(cols[:, N2, :], norm2.rearrange("b (p k) -> (b p) k", k=KT)).then_inc(small_loaded, 16)
            act.dma_start(cols[:, BA:BA + 6, :], bada_v).then_inc(small_loaded, 16)
            for h in range(2):
                r = slice(HD * h, HD * (h + 1))
                act.dma_start(qkg[r, 0:1], q_norm.rearrange("a (p b) -> (a p) b", b=1)).then_inc(small_loaded, 16)
                act.dma_start(qkg[r, 1:2], k_norm.rearrange("a (p b) -> (a p) b", b=1)).then_inc(small_loaded, 16)
            for t in range(TT):
                act.dma_start(xs[:, t, :], x_v[t]).then_inc(x_loaded[t], 16)
            act.wait_ge(small_loaded, 16 * SMALL)
            sc.activation(cth, cols[:, C_, :], ACT.Tanh, scale=0.5).then_inc(cact_ready, 1)
            act.dma_start(g1b[:, :], b_ada[0, 2 * D:3 * D].partition_broadcast(P)).then_inc(g_bias_loaded, 16)
            act.dma_start(g2b[:, :], b_ada[0, 5 * D:6 * D].partition_broadcast(P)).then_inc(g_bias_loaded, 16)
            for t in range(TT):
                act.wait_ge(x_loaded[t], 16)
                sc.activation(xn[:, t, :], xs[:, t, :], ACT.Square, accum_out=st[:, t:t + 1]).then_inc(x_sq, 1)
            for k in range(1, KT, 2):
                act.wait_ge(ab1_ready, 1)
                act.wait_ge(xT_ready, 4 if k < 7 else 8)
                sc.activation(hT[:, k, :], bank[:, k, :], ACT.Identity, bias=ab1[:, 1, k:k + 1],
                              scale=ab1[:, 0, k:k + 1]).then_inc(hT_act, 1)

            def attend_exp(a):
                n = P * (a % TT + 1)
                act.wait_ge(negmax_ready, a + 1)
                if a >= 2:
                    act.wait_ge(PT_ready, a - 1)
                for h in range(2):
                    sc.activation(probs[:, a % 2, h, 0:n], bank[:, 2 + h, 0:n], ACT.Exp,
                                  bias=st[:, 18 + h + 4 * (a % 2):19 + h + 4 * (a % 2)],
                                  accum_out=st[:, 28 + h + 4 * (a % 2):29 + h + 4 * (a % 2)]).then_inc(probs_raw, 1)

            def attend_pt(a):
                n = P * (a % TT + 1)
                act.wait_ge(PT_ready, a + 1)
                if a >= 2:
                    act.wait_ge(attn_ready, a - 1)
                sc.copy(PT[:, a % 2].rearrange("p h k q -> p h (k q)")[:, :, 0:n],
                        bank[:, 4:6, 0:n]).then_inc(PT_drained, 1)

            def attend_out(a):
                act.wait_ge(attn_ready, a + 1)
                sc.copy(attnT[:, a // TT, P * (a % TT):P * (a % TT + 1)],
                        bank[:, 6, P * (a % 4):P * (a % 4 + 1)]).then_inc(attn_drained, 1)

            for u in range(UNITS):
                a = u - U_P
                if 0 <= a < STEPS:
                    attend_exp(a)
                if 0 <= a - 1 < STEPS:
                    attend_pt(a - 1)
                if u == 4:
                    for b in range(MAXB * SLOTS // P):
                        act.dma_start(y_d[bass.ds(E * SLOTS + P * b, P), :],
                                      xs[:, b % TT, :]).then_inc(y_filled, 16)
                act.wait_ge(unit_done, u + 1)
                if u < U_V:
                    if u >= 1:
                        act.wait_ge(qk_var, u)
                    sc.activation(sqbuf, bank[:, u % 2, :], ACT.Square).then_inc(qk_sq, 1)
                elif u < U_P:
                    sc.copy(vt[:, u - U_V, :], bank[:, u % 2, :]).then_inc(unit_drained_act, 1)
                elif u < U_GP:
                    sc.copy(pT[:, u - U_P, :], bank[:, u % 2, :]).then_inc(unit_drained_act, 1)
                else:
                    m = (u - U_GP) % KT
                    to = m if u >= U_GA else m % 2
                    if U_GP + 2 <= u <= U_GA:
                        act.wait_ge(side_drained, side_no[("B", min(m - 2 if u < U_GA else 7, 7))] + 1)
                    sc.activation(sg[:, to, :], bank[:, u % 2, :], ACT.Tanh, scale=0.5).then_inc(unit_drained_act, 1)
                if 0 <= a - 2 < STEPS:
                    attend_out(a - 2)

            def square(t):
                act.wait_ge(yo_drained, 2 * t + 2)
                if t == 0:
                    act.wait_ge(unit_done, UNITS)
                sc.activation(xn2[:, t, :], xs[:, t, :], ACT.Square,
                              accum_out=st[:, 8 + t:9 + t]).then_inc(x1_sq, 1)

            def modulate(t):
                act.wait_ge(h2T_psum, t + 1)
                if t == 0:
                    act.wait_ge(PT_ready, STEPS)
                if t >= 2:
                    act.wait_ge(logits_ready, t - 1)
                for k in range(1, KT, 2):
                    last = sc.activation(h2T[:, t % 2, k, :],
                                         bank[:, 3 + 2 * (t % 2), P * (k // 2):P * (k // 2 + 1)], ACT.Identity,
                                         bias=ab2[:, 1, k:k + 1], scale=ab2[:, 0, k:k + 1])
                last.then_inc(h2T_act, 1)

            for t in range(TT + 1):
                if t < TT:
                    square(t)
                if t >= 1:
                    act.wait_ge(xn2_ready, t)
                    act.dma_start(xn2_d[P * (t - 1):P * t, :], xn2[:, t - 1, :]).then_inc(xn2_stored, 16)
                    modulate(t - 1)
            act.wait_ge(exp_in, 1)
            sc.activation(gexp, gdif, ACT.Exp).then_inc(exp_out, 1)
            act.wait_ge(exp_in, 2)
            sc.activation(edif, edif, ACT.Exp).then_inc(exp_out, 1)

            def expert(e, j, first, start):
                act.wait_ge(ab_done, e + 1)
                if not first:
                    act.wait_ge(st_done, e - 1)
                sc.copy(absb[:, j % 2, :], bank[:, 2 + j % 2, :]).then_inc(ab_drained, 1)
                act.wait_ge(st_done, e + 1)
                if not first:
                    act.wait_ge(hid_ready, e - 1)
                sc.activation(th[:, j % 2].rearrange("p f s -> p (f s)"), bank[:, 4 + j % 2, 0:FT * SLOTS],
                              ACT.Tanh, scale=0.5).then_inc(th_ready, 1)
                if not start:
                    store(e - 1, (j - 1) % 2)

            def store(e, b):
                act.wait_ge(y_drained, e + 1)
                for h in range(2):
                    act.dma_start(y_d[bass.ds(e * SLOTS, SLOTS), CH * h:CH * (h + 1)],
                                  ysb[SLOTS * h:SLOTS * (h + 1), b, :]).then_inc(y_stored[b], 16)

            for e in range(RING):
                expert(e, e, e < 2, e == 0)
            with act.Fori(1, E // RING) as i:
                for j in range(RING):
                    expert(i * RING + j, j, False, False)
            store(E - 1, 1)

            def overflow(b):
                act.wait_ge(x_ab, b + 1)
                sc.copy(absb[:, 0, :], bank[:, 2, :]).then_inc(x_ab_drained, 1)
                act.wait_ge(x_st, b + 1)
                sc.activation(th[:, 0].rearrange("p f s -> p (f s)"), bank[:, 4, 0:FT * SLOTS],
                              ACT.Tanh, scale=0.5).then_inc(x_th, 1)
                act.wait_ge(x_y_drained, b + 1)
                for h in range(2):
                    act.dma_start(y_d[bass.ds((b + E) * SLOTS, SLOTS), CH * h:CH * (h + 1)],
                                  ysb[SLOTS * h:SLOTS * (h + 1), 0, :]).then_inc(x_stored, 16)
                act.wait_ge(x_stored, 32 * b + 32)

            act.wait_ge(y_stored[0], 16 * E)
            act.wait_ge(y_filled, 16 * MAXB * SLOTS // P)
            overflow_blocks(act, overflow)
            act.sem_inc(overflow_done, 1)

        @block.vector
        def _(dve):
            v = nc.vector
            count = [0]

            def link(ins):
                count[0] += 1
                ins.then_inc(chain, 1)
                dve.wait_ge(chain, count[0])

            def ada(k):
                n, part, half = at[k], k[1], k[2]
                b = {1: 0, 0: 1, 2: 0, 3: 1, 4: 0, 5: 1}[part]
                w = slot[n % 4].rearrange("p (k n) -> p k n", k=4)
                dve.wait_ge(slot_loaded[n % 4], 16 * (n // 4 + 1))
                if half == 0 and part == 3:
                    dve.wait_ge(col_ready, 1)
                if half == 0 and part == 2:
                    dve.wait_ge(col_ready, 1)
                if half == 0 and part == 4:
                    dve.wait_ge(side_done, 2)
                if half == 0 and part == 5:
                    dve.wait_ge(side_done, side_no[("cols",)] + 1)
                for kk in range(4):
                    cc = cols[:, C_, 4 * half + kk:4 * half + kk + 1]
                    if half == 0 and kk == 0:
                        ins = v.tensor_scalar(acc[:, b, :], w[:, kk, :], cc, None, ALU.mult)
                    else:
                        ins = v.scalar_tensor_tensor(out=acc[:, b, :], in0=w[:, kk, :], scalar=cc,
                                                     in1=acc[:, b, :], op0=ALU.mult, op1=ALU.add)
                    if kk < 3:
                        link(ins)
                ins.then_inc(ada_used, 1)
                dve.wait_ge(ada_used, ADA.index(k) + 1)

            dve.wait_ge(small_loaded, 16 * SMALL)
            dve.wait_ge(cact_ready, 1)
            link(v.scalar_tensor_tensor(out=cols[:, C_, :], in0=cth, scalar=1.0, in1=cols[:, C_, :],
                                        op0=ALU.add, op1=ALU.mult))
            link(v.tensor_scalar(cols[:, C_, :], cols[:, C_, :], 0.5, None, ALU.mult))
            link(v.tensor_scalar(qkg[:, 0:1], qkg[:, 0:1], HD ** -0.5, None, ALU.mult))
            ada(ADA[0])
            dve.wait_ge(x_sq, TT)
            v.tensor_scalar(st[:, 4:8], st[:, 0:4], 1.0 / D, EPS, ALU.mult, ALU.add).then_inc(x_var, 1)
            ada(ADA[1])
            dve.wait_ge(x_rstd, 1)
            for t in range(TT):
                v.tensor_scalar(xn[:, t, :], xs[:, t, :], st[:, 12 + t:13 + t], None, ALU.mult).then_inc(xn_ready, 1)
            ada(ADA[2])
            ada(ADA[3])

            def norm_cols(src, nrow, dst, jb_scale, jb_shift, done):
                link(v.tensor_tensor(dst[:, 1, :], src[:, 8:16], cols[:, BA + jb_shift, :], ALU.add))
                link(v.tensor_tensor(dst[:, 0, :], src[:, 0:8], cols[:, BA + jb_scale, :], ALU.add))
                v.scalar_tensor_tensor(out=dst[:, 0, :], in0=dst[:, 0, :], scalar=1.0, in1=cols[:, nrow, :],
                                       op0=ALU.add, op1=ALU.mult).then_inc(done, 1)

            dve.wait_ge(col_ready, 1)
            norm_cols(bank[:, 7, :], N1, ab1, 1, 0, ab1_ready)
            dve.wait_ge(ab1_ready, 1)
            for k in range(0, KT, 2):
                dve.wait_ge(xT_ready, 4)
                v.tensor_scalar(hT[:, k, :], bank[:, k, :], ab1[:, 0, k:k + 1], ab1[:, 1, k:k + 1],
                                ALU.mult, ALU.add).then_inc(hT_dve, 1)

            def qk_norm(u):
                b = u % 2
                dve.wait_ge(qk_sq, u + 1)
                v.tensor_reduce(ss[:, b, 0, :], sqbuf.rearrange("p (h d) -> p h d", h=HEADS), AX.X,
                                ALU.add).then_inc(chain, 1)
                count[0] += 1
                dve.wait_ge(chain, count[0])
                v.tensor_scalar(ss[:, b, 0, :], ss[:, b, 0, :], 1.0 / HD, EPS, ALU.mult, ALU.add).then_inc(qk_var, 1)

            def qk_scale(u):
                b = u % 2
                dve.wait_ge(qk_rstd, u + 1)
                if u >= 2:
                    dve.wait_ge(qkT_ready, u - 1)
                v.tensor_tensor(qn[:, b, :].rearrange("p (h d) -> p h d", h=HEADS),
                                bank[:, u % 2, :].rearrange("p (h d) -> p h d", h=HEADS),
                                ss[:, b, 1, :].unsqueeze(2).broadcast_to([P, HEADS, HD]),
                                ALU.mult).then_inc(unit_drained_dve, 1)

            def qk_gain(u):
                dve.wait_ge(qkT_ready, u + 1)
                dst = (qT if u < 4 else kT)[:, :, P * (u % 4):P * (u % 4 + 1)]
                g = qkg[:, 0:1] if u < 4 else qkg[:, 1:2]
                v.tensor_scalar(dst, bank[:, 4 + u % 2, :].rearrange("p (j q) -> p j q", j=HP), g, None,
                                ALU.mult).then_inc(qkT_drained, 1)

            def attend_max(a):
                n = P * (a % TT + 1)
                o = 4 * (a % 2)
                dve.wait_ge(scores_ready, a + 1)
                link(v.tensor_reduce(st[:, 16 + o:18 + o], bank[:, 2:4, 0:n], AX.X, ALU.max))
                v.tensor_scalar(st[:, 18 + o:20 + o], st[:, 16 + o:18 + o], -1.0, None,
                                ALU.mult).then_inc(negmax_ready, 1)

            def attend_norm(a):
                n = P * (a % TT + 1)
                o = 4 * (a % 2)
                dve.wait_ge(probs_raw, 2 * a + 2)
                link(v.reciprocal(st[:, 30 + o:32 + o], st[:, 28 + o:30 + o]))
                for h in range(2):
                    last = v.tensor_scalar(probs[:, a % 2, h, 0:n], probs[:, a % 2, h, 0:n],
                                           st[:, 30 + o + h:31 + o + h], None, ALU.mult)
                last.then_inc(probs_ready, 1)

            def side(*k):
                n = side_no[k]
                b = side_bank(n)
                dve.wait_ge(side_done, n + 1)
                if k[0] in ("g1", "g2"):
                    g = (g1b if k[0] == "g1" else g2b)[:, CH * k[1]:CH * (k[1] + 1)]
                    dve.wait_ge(g_bias_loaded, 32)
                    v.tensor_tensor(g, bank[:, b, :], g, ALU.add).then_inc(side_drained, 1)
                elif k[0] == "cols":
                    norm_cols(bank[:, b, :], N2, ab2, 4, 3, side_drained)
                elif k[0] == "B":
                    m = k[1]
                    if m == 0:
                        dve.wait_ge(xT_ready, 8)
                        dve.wait_ge(late_loaded, 16 * LATE)
                        link(v.tensor_scalar(cols[:, PS, :], cols[:, PS, :], 0.5, None, ALU.mult))
                    dve.wait_ge(unit_drained_act, U_GP - U_V + m + 1)
                    link(v.tensor_scalar(mergedT[:, m, :], bank[:, b, :], cols[:, PS, m:m + 1], None, ALU.mult))
                    v.scalar_tensor_tensor(out=mergedT[:, m, :], in0=sg[:, m % 2, :], scalar=1.0,
                                           in1=mergedT[:, m, :], op0=ALU.add, op1=ALU.mult).then_inc(side_drained, 1)
                else:
                    m = k[1]
                    dve.wait_ge(unit_drained_act, U_GA - U_V + m + 1)
                    link(v.scalar_tensor_tensor(out=sg[:, m, :], in0=sg[:, m, :], scalar=1.0, in1=bank[:, b, :],
                                                op0=ALU.add, op1=ALU.mult))
                    v.scalar_tensor_tensor(out=mergedT[:, m, :], in0=sg[:, m, :], scalar=0.5, in1=mergedT[:, m, :],
                                           op0=ALU.mult, op1=ALU.add).then_inc(side_drained, 1)

            ADA_AT = {9: 4, 11: 5, 13: 6, 17: 7, 22: 8, 25: 9}
            for u in range(UNITS):
                a = u - U_P
                if 0 <= a < STEPS:
                    attend_max(a)
                if 1 <= u <= 8:
                    qk_gain(u - 1)
                if u < U_V:
                    qk_norm(u)
                    qk_scale(u)
                if u in (U_P + 1, U_P + 2):
                    side("g1", u - U_P - 1)
                if U_GP + 2 <= u <= U_GA + 1:
                    side("B", u - 2 - U_GP)
                if 0 <= a < STEPS:
                    attend_norm(a)
                if u in ADA_AT:
                    ada(ADA[ADA_AT[u]])
                if u == 28:
                    side("cols")
                    ada(ADA[10])
            ada(ADA[11])
            side("g2", 0)
            side("g2", 1)
            for m in range(KT):
                side("A", m)

            def residual(t, h):
                n = 2 * t + h
                dve.wait_ge(yo_done, n + 1)
                w = slice(CH * h, CH * (h + 1))
                tmp = acc[:, 0, w]
                if n == 0:
                    dve.wait_ge(y_filled, 16 * MAXB * SLOTS // P)
                link(v.tensor_tensor(tmp, bank[:, n % 2, :], g1b[:, w], ALU.mult))
                v.tensor_tensor(xs[:, t, w], tmp, xs[:, t, w], ALU.add).then_inc(yo_drained, 1)

            def modulate(t):
                dve.wait_ge(h2T_psum, t + 1)
                if t >= 2:
                    dve.wait_ge(logits_ready, t - 1)
                for k in range(0, KT, 2):
                    last = v.tensor_scalar(h2T[:, t % 2, k, :], bank[:, 2 + 2 * (t % 2), P * (k // 2):P * (k // 2 + 1)],
                                           ab2[:, 0, k:k + 1], ab2[:, 1, k:k + 1], ALU.mult, ALU.add)
                last.then_inc(h2T_dve, 1)

            for t in range(TT + 1):
                if t < TT:
                    residual(t, 0)
                    residual(t, 1)
                    dve.wait_ge(x1_sq, t + 1)
                    v.tensor_scalar(st[:, 40 + t:41 + t], st[:, 8 + t:9 + t], 1.0 / D, EPS, ALU.mult,
                                    ALU.add).then_inc(x1_var, 1)
                    dve.wait_ge(x1_rstd, t + 1)
                    v.tensor_scalar(xn2[:, t, :], xs[:, t, :], st[:, 44 + t:45 + t], None,
                                    ALU.mult).then_inc(xn2_ready, 1)
                if t >= 1:
                    modulate(t - 1)

            dve.wait_ge(logits_ready, TT)
            dve.wait_ge(iotas_ready, 1)
            bc = lambda ap, shape, d: ap.unsqueeze(d).broadcast_to(shape)
            S4, S32 = [P, TT, NG], [P, TT, E]
            link(v.tensor_copy(lg, bank[:, 6, 0:TT * 36].rearrange("p (t n) -> p t n", t=TT)))
            gl, el = lg[:, :, 0:NG], lg[:, :, NG:NG + E]

            def first_max(vals, best, n, it, shape, eq, score, oh):
                link(v.tensor_reduce(best, vals, AX.X, ALU.max))
                link(v.tensor_tensor(eq, vals, bc(best, shape, 2), ALU.is_equal))
                link(v.tensor_tensor(eq, eq, it.unsqueeze(1).broadcast_to(shape), ALU.mult))
                link(v.tensor_reduce(score, eq, AX.X, ALU.max))
                link(v.tensor_tensor(oh, eq, bc(score, shape, 2), ALU.is_equal))

            first_max(gl, gbest, NG, iota_g, S4, geq, gscore, goh)
            v.tensor_tensor(gdif, gl, bc(gbest, S4, 2), ALU.subtract).then_inc(exp_in, 1)
            link(v.tensor_scalar(gpen, goh, -1.0, -NEG, ALU.add, ALU.mult))
            for t in range(TT):
                last = v.tensor_tensor(em[:, t, :].rearrange("p (g e) -> p g e", g=NG),
                                       el[:, t, :].rearrange("p (g e) -> p g e", g=NG),
                                       bc(gpen[:, t, :], [P, NG, EPG], 2), ALU.add)
            link(last)
            first_max(em, best1, E, iota_e, S32, eq1, score1, oh1)
            link(v.scalar_tensor_tensor(out=em.rearrange("p t e -> p (t e)"), in0=oh1.rearrange("p t e -> p (t e)"),
                                        scalar=10 * NEG, in1=em.rearrange("p t e -> p (t e)"),
                                        op0=ALU.mult, op1=ALU.add))
            first_max(em, best2, E, iota_e, S32, eq1, score1, oh2)
            v.tensor_tensor(maskm, oh1, oh2, ALU.add).then_inc(mask_ready, 1)
            v.tensor_tensor(edif, best2, best1, ALU.subtract).then_inc(exp_in, 1)
            link(v.tensor_tensor(maskf, oh1, oh2, ALU.add))
            dve.wait_ge(exp_out, 1)
            link(v.tensor_reduce(gsum, gexp, AX.X, ALU.add))
            link(v.reciprocal(gsum, gsum))
            dve.wait_ge(exp_out, 2)
            link(v.tensor_scalar(best1, edif, 1.0, None, ALU.add))
            link(v.reciprocal(best1, best1))
            link(v.tensor_tensor(cw[:, 0, :], best1, gsum, ALU.mult))
            link(v.tensor_tensor(cw[:, 1, :], cw[:, 0, :], edif, ALU.mult))
            dve.wait_ge(rank_ready, 1)
            link(v.tensor_copy(cnt, bank[:, 7, 128:160]))
            link(v.tensor_copy(rk.rearrange("p t e -> p (t e)"), bank[:, 7, 0:TT * E]))
            link(v.scalar_tensor_tensor(out=rm.rearrange("p t e -> p (t e)"), in0=rk.rearrange("p t e -> p (t e)"),
                                        scalar=1.0, in1=maskf.rearrange("p t e -> p (t e)"),
                                        op0=ALU.add, op1=ALU.mult))
            dve.wait_ge(yo_done, 2 * TT)
            for g in range(4):
                for t in range(TT):
                    es = slice(8 * g, 8 * g + 8)
                    last = v.tensor_tensor(place[:, t, es, :], bc(rm[:, t, es], [P, 8, SLOTS], 2),
                                           iota_s.unsqueeze(1).broadcast_to([P, 8, SLOTS]), ALU.is_equal)
                last.then_inc(place_ready, 1)
                if g >= 1:
                    dve.wait_ge(idx_psum, g)
                    v.tensor_copy(idx[:, 4 * g - 4:4 * g], bank[:, 1 + g, 0:4]).then_inc(idx_ready, 1)
            dve.wait_ge(idx_psum, 4)
            v.tensor_copy(idx[:, 12:16], bank[:, 5, 0:4]).then_inc(idx_ready, 1)
            def modulate_gathered(q, b, first):
                dve.wait_ge(xt_ready, q + 1)
                if not first:
                    dve.wait_ge(ab_done, (q - 1) * 2)
                for k in range(KT):
                    last = v.tensor_scalar(xgT[:, b, k, :], bank[:, k // 4, P * (k % 4):P * (k % 4 + 1)],
                                           ab2[:, 0, k:k + 1], ab2[:, 1, k:k + 1], ALU.mult, ALU.add)
                last.then_inc(xgT_ready, 1)

            def hidden(e, j, first, linked):
                dve.wait_ge(th_ready, e + 1)
                if not first:
                    dve.wait_ge(y_done, e - 1)
                b = j % 2
                v.scalar_tensor_tensor(out=sl[:, b].rearrange("p f s -> p (f s)"),
                                       in0=th[:, b].rearrange("p f s -> p (f s)"), scalar=1.0,
                                       in1=bank[:, 4 + b, 0:FT * SLOTS], op0=ALU.add,
                                       op1=ALU.mult).then_inc(silu_ready, 1)
                dve.wait_ge(silu_ready, e + 1)
                v.scalar_tensor_tensor(out=hid[:, b].rearrange("p f s -> p (f s)"),
                                       in0=sl[:, b].rearrange("p f s -> p (f s)"), scalar=0.5,
                                       in1=bank[:, 4 + b, FT * SLOTS:2 * FT * SLOTS], op0=ALU.mult,
                                       op1=ALU.mult).then_inc(hid_ready, 1)

            def drain_y(e, b, first):
                dve.wait_ge(y_done, e + 1)
                if not first:
                    dve.wait_ge(y_stored[b], (e - b) * 16)
                v.tensor_copy(ysb[:, b, :], bank[:, 6 + b, :]).then_inc(y_drained, 1)

            def experts(i, peeled):
                for j in range(RING):
                    e = i * RING + j
                    start = peeled and i == 0
                    if not (start and j == 0):
                        drain_y(e - 1, (j - 1) % 2, start and j - 1 < 2)
                    if j % 2 and not (peeled and i == E // RING - 1 and j == RING - 1):
                        modulate_gathered(i * 2 + j // 2 + 1, (j // 2 + 1) % 2, start and j // 2 == 0)
                    hidden(e, j, start and j < 2, None)

            modulate_gathered(0, 0, True)
            experts(0, True)
            link(v.tensor_scalar(nx[0], cnt, float(SLOTS), None, ALU.is_gt))
            for m in range(2, T // SLOTS):
                link(v.scalar_tensor_tensor(out=nx[0], in0=cnt, scalar=float(SLOTS * m), in1=nx[0],
                                            op0=ALU.is_gt, op1=ALU.add))
            link(v.tensor_copy(nx[1], nx[0]))
            cur, s = 1, 1
            while s < E:
                nxt = 3 - cur
                v.tensor_copy(nx[nxt][:, 0:s], nx[cur][:, 0:s])
                link(v.tensor_tensor(nx[nxt][:, s:E], nx[cur][:, s:E], nx[cur][:, 0:E - s], ALU.add))
                cur, s = nxt, 2 * s
            incl = nx[cur]
            link(v.tensor_tensor(xcmp, bc(incl, [P, E, MAXB], 2), iota_b.unsqueeze(1).broadcast_to([P, E, MAXB]),
                                 ALU.is_le))
            link(v.tensor_reduce(xsum, xcmp.rearrange("p e b -> p b e"), AX.X, ALU.add))
            link(v.tensor_scalar(xsum, xsum, float(E - 1), None, ALU.min))
            v.tensor_copy(xtab[:, 0:MAXB], xsum)
            link(v.tensor_copy(xtab[:, MAXB:MAXB + 1], incl[:, E - 1:E]))
            v.tensor_scalar(xbase[:, :], cnt[:, 0:1], 0.0, float(E * SLOTS - 1), ALU.mult,
                            ALU.add).then_inc(xtab_ready, 1)
            dve.wait_ge(xtab_ready, 1)
            link(v.tensor_tensor(cnt, incl, nx[0], ALU.subtract))
            link(v.tensor_scalar(cnt, cnt, float(SLOTS), float((E - 1) * SLOTS), ALU.mult, ALU.add))
            link(v.tensor_tensor(cnt, cnt, e64, ALU.subtract))
            link(v.tensor_scalar(em, rk, float(SLOTS), None, ALU.is_ge))
            link(v.tensor_tensor(em, em, cnt.unsqueeze(1).broadcast_to(S32), ALU.mult))
            link(v.tensor_tensor(rk, rk, e64.unsqueeze(1).broadcast_to(S32), ALU.add))
            link(v.tensor_tensor(rk, rk, em, ALU.add))
            for j, oh in enumerate((oh1, oh2)):
                link(v.tensor_tensor(em, rk, oh, ALU.mult))
                link(v.tensor_reduce(posf[:, j, :], em, AX.X, ALU.add))
            v.tensor_copy(pos[:, :, :], posf.rearrange("p j t -> p t j")).then_inc(pos_ready, 1)

            with dve.Fori(1, E // RING - 1) as i:
                experts(i, False)
            experts(E // RING - 1, True)
            drain_y(E - 1, 1, False)

            def overflow(b):
                v.tensor_scalar(xrel[:, :], posf.rearrange("p j t -> p (j t)"), xbase[:, :], None,
                                ALU.subtract).then_inc(x_rel, 1)
                dve.wait_ge(x_rel, b + 1)
                v.tensor_tensor(xplace, bc(xrel[:, :], [P, 2 * TT, SLOTS], 2),
                                iota_s.unsqueeze(1).broadcast_to([P, 2 * TT, SLOTS]), ALU.is_equal).then_inc(x_place, 1)
                v.tensor_scalar(xbase[:, :], xbase[:, :], float(SLOTS), None, ALU.add).then_inc(x_base, 1)
                dve.wait_ge(x_base, b + 1)
                dve.wait_ge(x_idx_psum, b + 1)
                v.tensor_copy(idxx[0:SLOTS, :], bank[0:SLOTS, 0, 0:1]).then_inc(x_idx, 1)
                dve.wait_ge(x_rowsT, b + 1)
                for k in range(KT):
                    last = v.tensor_scalar(xgT[:, 0, k, 0:SLOTS], bank[:, k // 4, P * (k % 4):P * (k % 4) + SLOTS],
                                           ab2[:, 0, k:k + 1], ab2[:, 1, k:k + 1], ALU.mult, ALU.add)
                last.then_inc(x_in, 1)
                dve.wait_ge(x_th, b + 1)
                v.scalar_tensor_tensor(out=sl[:, 0].rearrange("p f s -> p (f s)"),
                                       in0=th[:, 0].rearrange("p f s -> p (f s)"), scalar=1.0,
                                       in1=bank[:, 4, 0:FT * SLOTS], op0=ALU.add, op1=ALU.mult).then_inc(x_silu, 1)
                dve.wait_ge(x_silu, b + 1)
                v.scalar_tensor_tensor(out=hid[:, 0].rearrange("p f s -> p (f s)"),
                                       in0=sl[:, 0].rearrange("p f s -> p (f s)"), scalar=0.5,
                                       in1=bank[:, 4, FT * SLOTS:2 * FT * SLOTS], op0=ALU.mult,
                                       op1=ALU.mult).then_inc(x_hid, 1)
                dve.wait_ge(x_y, b + 1)
                v.tensor_copy(ysb[:, 0, :], bank[:, 6, :]).then_inc(x_y_drained, 1)
                dve.wait_ge(x_stored, 32 * b + 32)

            dve.wait_ge(y_stored[0], 16 * E)
            overflow_blocks(dve, overflow)

            for t in range(TT):
                dve.wait_ge(yg_loaded[t], 32)
                link(v.tensor_scalar(yg[:, t, 0, :], yg[:, t, 0, :], cw[:, 0, t:t + 1], None, ALU.mult))
                link(v.scalar_tensor_tensor(out=yg[:, t, 0, :], in0=yg[:, t, 1, :], scalar=cw[:, 1, t:t + 1],
                                            in1=yg[:, t, 0, :], op0=ALU.mult, op1=ALU.add))
                link(v.tensor_tensor(yg[:, t, 0, :], yg[:, t, 0, :], g2b[:, :], ALU.mult))
                v.tensor_tensor(xs[:, t, :], yg[:, t, 0, :], xs[:, t, :], ALU.add).then_inc(out_ready, 1)

        @block.gpsimd
        def _(pool):
            g = nc.gpsimd
            count = [0]

            def link(ins):
                count[0] += 1
                ins.then_inc(pool_link, 1)
                pool.wait_ge(pool_link, count[0])

            def fill_diagonal(tile, base, n):
                link(g.affine_select(out=tile, in_=tile, compare_op=ALU.not_equal, fill=1.0, base=base,
                                     pattern=[[-1, n]], channel_multiplier=1))

            link(g.memset(ident[:, :], 0.0))
            fill_diagonal(ident[:, :], 0, P)
            link(g.tensor_copy(identb[:, :], ident[:, :]))
            link(g.memset(fold[:, :], 0.0))
            fill_diagonal(fold[:, :], 0, SLOTS)
            fill_diagonal(fold[:, :], -SLOTS, SLOTS)
            g.memset(ones[:, :], 1.0)
            link(g.memset(onesb[:, :], 1.0))
            link(g.memset(maskb[:, :], 0.0))
            g.affine_select(out=maskb[:, :], in_=maskb[:, :], compare_op=ALU.is_ge, fill=NEG, base=0,
                            pattern=[[-1, P]], channel_multiplier=1)
            g.affine_select(out=lowb[:, :], in_=onesb[:, :], compare_op=ALU.is_gt, fill=0.0, base=0,
                            pattern=[[1, P]], channel_multiplier=-1)
            for j in range(16):
                g.memset(recip[:, j:j + 1], 1.0 / (j + 1))
            g.iota(tokp[:, 0:1], pattern=[[0, 1]], base=0, channel_multiplier=1, allow_small_or_imprecise_dtypes=True)
            g.iota(tokp[:, 1:1 + TT], pattern=[[P, TT]], base=0, channel_multiplier=0,
                   allow_small_or_imprecise_dtypes=True)
            link(g.memset(nhalf[:, :], -0.5))
            link(g.memset(st[:, 48:49], 0.0))
            g.memset(idxx[:, :], 0)
            g.memset(st[:, 49:50], 0.0).then_inc(consts_ready, 1)
            pool.dma_start(cols[:, PS, :], pool_scale.rearrange("b (m p) -> (b p) m", p=P),
                           allow_slow_non_contiguous=True).then_inc(late_loaded, 16)
            pool.dma_start(pw, w_pool.rearrange("l g c n -> (l c) g n")).then_inc(late_loaded, 16)
            pool.dma_start(wr[:, :, 0:NG], w_router_g.rearrange("l (p k) n -> (l p) k n", k=KT)).then_inc(late_loaded, 16)
            pool.dma_start(wr[:, :, NG:NG + E], w_router_e.rearrange("l (p k) n -> (l p) k n", k=KT)).then_inc(late_loaded, 16)
            pool.dma_start(br[:, 0:NG], b_router_g).then_inc(late_loaded, 16)
            pool.dma_start(br[:, NG:NG + E], b_router_e).then_inc(late_loaded, 16)
            pool.wait_ge(x_var, 1)
            g.tensor_tensor(st[:, 12:16], st[:, 4:8], nhalf[:, 0:4], ALU.pow).then_inc(x_rstd, 1)
            for u in range(U_V):
                pool.wait_ge(qk_var, u + 1)
                if u >= 2:
                    pool.wait_ge(unit_drained_dve, u - 1)
                g.tensor_tensor(ss[:, u % 2, 1, :], ss[:, u % 2, 0, :], nhalf[:, :], ALU.pow).then_inc(qk_rstd, 1)

            for gi, w in enumerate(WINDOWS):
                pool.wait_ge(unit_drained_act, U_P - U_V + gi + 1)
                src, s, b = pT[:, gi, :], 1, 0
                while s < w:
                    dst = ptmp[b]
                    g.tensor_copy(dst[:, 0:s], src[:, 0:s])
                    link(g.tensor_tensor(dst[:, s:T], src[:, s:T], src[:, 0:T - s], ALU.add))
                    src, s, b = dst, 2 * s, 1 - b
                g.tensor_tensor(src[:, 0:w - 1], src[:, 0:w - 1], recip[:, 0:w - 1], ALU.mult)
                link(g.tensor_scalar(src[:, w - 1:T], src[:, w - 1:T], 1.0 / w, None, ALU.mult))
                g.tensor_tensor(pT[:, gi, :], src, pT[:, gi, :], ALU.subtract).then_inc(pooled, 1)
                pool.wait_ge(pooled, gi + 1)

            for t in range(TT):
                pool.wait_ge(x1_var, t + 1)
                g.tensor_tensor(st[:, 44 + t:45 + t], st[:, 40 + t:41 + t], nhalf[:, 0:1],
                                ALU.pow).then_inc(x1_rstd, 1)
            pool.wait_ge(yo_done, 2 * TT)
            kw = dict(allow_small_or_imprecise_dtypes=True, channel_multiplier=0)
            g.iota(iota_g, pattern=[[-1, NG]], base=NG, **kw)
            g.iota(iota_e, pattern=[[-1, E]], base=E, **kw)
            g.iota(e64, pattern=[[SLOTS, E]], base=0, **kw)
            g.iota(iota_b, pattern=[[1, MAXB]], base=0, **kw)
            g.iota(iota_s, pattern=[[1, SLOTS]], base=1, **kw).then_inc(iotas_ready, 1)

            pool.wait_ge(xn2_stored, 16 * TT)
            for q in range(PAIRS):
                if q % 4 == 0:
                    pool.wait_ge(idx_ready, q // 4 + 1)
                if q >= 2:
                    pool.wait_ge(xt_ready, q - 1)
                pool.indirect_dma_start(out=xg[:, q % 2, :], out_offset=None, in_=xn2_d,
                                        in_offset=bass.IndirectOffsetOnAxis(ap=idx[:, q:q + 1], axis=0)
                                        ).then_inc(xg_loaded[q % 2], 16)
            def overflow(b):
                pool.wait_ge(x_idx, b + 1)
                pool.sem_inc(x_turns, 1)
                pool.indirect_dma_start(out=xg[:, 0, :], out_offset=None, in_=xn2_d,
                                        in_offset=bass.IndirectOffsetOnAxis(ap=idxx[:, 0:1], axis=0)
                                        ).then_inc(x_rows, 16)

            overflow_blocks(pool, overflow)
            pool.wait_ge(pos_ready, 1)
            pool.wait_ge(overflow_done, 1)
            pool.wait_ge(y_filled, 16 * MAXB * SLOTS // P)
            for b in range(2):
                pool.wait_ge(y_stored[b], 16 * E)
            for t in range(TT):
                for j in range(2):
                    pool.indirect_dma_start(out=yg[:, t, j, :], out_offset=None, in_=y_d,
                                            in_offset=bass.IndirectOffsetOnAxis(ap=pos[:, t, j:j + 1], axis=0)
                                            ).then_inc(yg_loaded[t], 16)


_INS = ['x', 'c', 'w_ada', 'b_ada', 'norm1', 'w_in', 'q_norm', 'k_norm', 'w_attn_up', 'w_pool', 'pool_scale',
        'w_out', 'norm2', 'w_router_g', 'b_router_g', 'w_router_e', 'b_router_e', 'w1', 'w3', 'w2']


def kernel(**inputs):
    import numpy as _np
    import concourse.bacc as _bacc
    from concourse import mybir as _mybir
    from concourse.bass_utils import run_bass_kernel_spmd as _run

    nc = _bacc.Bacc("TRN2", target_bir_lowering=False, num_devices=1)
    arrays, args = {}, []
    for name in _INS:
        a = _np.ascontiguousarray(inputs[name])
        arrays[f"in_{name}_dram"] = a
        args.append(nc.dram_tensor(f"in_{name}_dram", a.shape, _mybir.dt.from_np(a.dtype), kind="ExternalInput").ap())
    args.append(nc.dram_tensor("out_0_dram", (1, T, D), F32, kind="ExternalOutput").ap())
    hybrid_trunk(nc, *args)
    r = _run(nc, [arrays], core_ids=[0])
    return r.results[0]["out_0_dram"]
```

```python
from contextlib import ExitStack

import concourse.bass as bass
from concourse import mybir

F32 = mybir.dt.float32
BF16 = mybir.dt.bfloat16
I32 = mybir.dt.int32
ALU = mybir.AluOpType
ACT = mybir.ActivationFunctionType
AX = mybir.AxisListType

P = 128
T, D = 512, 1024
TT, KT = T // P, D // P
HEADS, HD = 8, 64
AW = HEADS * HD
HP = AW // P
PW = D // 2
WINDOWS = (2, 4, 8, 16)
NG, EPG = 4, 8
E = NG * EPG
F = 256
FT = F // P
SLOTS = 64
PAIRS = E // 2
MAXB = 2 * T // SLOTS
EPS = 1e-6
NEG = -1e30
CH = 512
RING = 6
HEAD = E % RING
TURNS = E // RING
OUT_OF_BOUNDS = 4096


def hybrid_trunk(nc, x, c, w_ada, b_ada, norm1, w_in, q_norm, k_norm, w_attn_up, w_pool, pool_scale, w_out,
                 norm2, w_router_g, b_router_g, w_router_e, b_router_e, w1, w3, w2, out):
    x_v = x.rearrange("b (t p) d -> (b t) p d", p=P)
    out_v = out.rearrange("b (t p) d -> (b t) p d", p=P)
    ada_v = w_ada.rearrange("l (p k) n -> (l p) k n", k=KT)
    bada_v = b_ada.rearrange("l (j p k) -> (l p) j k", k=KT, p=P)
    win_v = w_in.rearrange("l (p k) n -> (l p) k n", k=KT)
    wup_v = w_attn_up.rearrange("l (k p) n -> (l p) k n", p=P)
    wout_v = w_out.rearrange("l (k p) n -> (l p) k n", p=P)
    w1_v = w1.rearrange("l g e (p k) f -> (l g e) p (k f)", k=KT)
    w3_v = w3.rearrange("l g e (p k) f -> (l g e) p (k f)", k=KT)
    w2_v = w2.rearrange("l g e (p k) n -> (l g e) p (k n)", k=FT)

    xn2_d = nc.dram_tensor("xn2_scratch", (T, D), F32).ap()
    y_d = nc.dram_tensor("y_scratch", (2 * T, D), F32).ap()

    ctx = ExitStack()
    with ctx:
        def sb(name, shape, dt=F32):
            return ctx.enter_context(nc.sbuf_tensor(name, shape, dt))

        def sem(name):
            return ctx.enter_context(nc.semaphore(name))

        bank = ctx.enter_context(nc.psum_tensor("bank", [P, 8, CH], F32))

        xs = sb("xs", [P, TT, D])
        hT = sb("hT", [P, KT, T])
        late = sb("late", [P, 2 * 6144])
        g1b = sb("g1b", [P, D])
        g2b = sb("g2b", [P, D])
        arena = sb("arena", [P, 4 * 6144])
        ROUTE = 3 * TT * E + 4 * E + 2 * TT
        route = sb("route", [P, ROUTE])
        acc = sb("acc", [P, 2, D])
        probs = sb("probs", [P, 2, 2, CH])
        ident = sb("ident", [P, P])
        ones = sb("ones", [P, P])
        identb = sb("identb", [P, P], BF16)
        maskb = sb("maskb", [P, P], BF16)
        lowb = sb("lowb", [P, P], BF16)
        onesb = sb("onesb", [P, P], BF16)
        fold = sb("fold", [P, SLOTS])
        wr = sb("wr", [P, KT, NG + E])
        br = sb("br", [1, NG + E])
        cols = sb("cols", [P, 12, KT])
        ab1 = sb("ab1", [P, 2, KT])
        ab2 = sb("ab2", [P, 2, KT])
        xrel = sb("xrel", [P, 2 * TT])
        xv = sb("xv", [P, 8])
        cth = cols[:, 10, :]
        recip = sb("recip", [P, 16])
        qkg = sb("qkg", [P, 2])
        st = sb("st", [P, 64])
        ss = sb("ss", [P, 2, 2, 8])
        nhalf = sb("nhalf", [P, 8])
        tokc = sb("tokc", [P, TT, 2], BF16)
        gidx = sb("gidx", [P, PAIRS], I32)
        sidx = sb("sidx", [P, PAIRS], I32)
        slotv = sb("slotv", [P, PAIRS, 4])
        iotas = sb("iotas", [P, 128])
        xtab = sb("xtab", [P, MAXB + 1], I32)
        cw = sb("cw", [P, 2, TT])
        xbase = sb("xbase", [P, 1])
        gidxx = sb("gidxx", [P, 1], I32)
        sidxx = sb("sidxx", [P, 1], I32)

        def carve(base, start, *shape):
            n = 1
            for s in shape:
                n *= s
            v = base[:, start:start + n]
            names = "abcd"[:len(shape)]
            if len(shape) == 1:
                return v
            return v.rearrange(f"p ({' '.join(names)}) -> p {' '.join(names)}", **dict(zip(names[1:], shape[1:])))

        AR = arena[:, :]
        OU = late[:, 0:8192]
        MG = late[:, 8192:12288]
        mergedT = MG.rearrange("p (k t) -> p k t", k=KT)
        slot = [carve(AR, 0, 4096), OU[:, 0:4096], OU[:, 4096:8192], carve(AR, 4096, 4096)]
        qT = carve(AR, 8192, HP, T)
        kT = carve(AR, 10240, HP, T)
        vt = carve(AR, 12288, TT, AW)
        pT = carve(AR, 14336, 4, T)
        attnT = carve(AR, 16384, HP, T)
        sg = carve(AR, 18432, KT, T)
        qn = carve(AR, 22528, 2, AW)
        PT = carve(AR, 22528, 2, 2, TT, P)
        pw = sg[:, 2:4, :].rearrange("p a (b n) -> p (a b) n", b=2)
        ptmp = [sg[:, 4, :], sg[:, 5, :]]
        rows = acc[:, 0, 0:CH]
        sqbuf = probs[:, 0, 0, :]
        xn = MG.rearrange("p (t d) -> p t d", t=TT)
        xn2 = hT[:, :, :].rearrange("p a b -> p (a b)").rearrange("p (t d) -> p t d", t=TT)
        h2T = probs[:, :, :, :].rearrange("p a b c -> p (a b c)").rearrange("p (u k t) -> p u k t", u=2, k=KT)
        IDX_GROUPS = [range(0, 2), range(2, PAIRS)]
        idx_bank = lambda g: bank[:, (2, 7)[g], :]
        HT = hT[:, :, :].rearrange("p a b -> p (a b)")
        PR = probs[:, :, :, :].rearrange("p a b c -> p (a b c)")
        xg = carve(HT, 0, 3, D)
        xgT = carve(HT, 3072, KT, P)
        place = []
        for qs, starts in zip(IDX_GROUPS, ([HT[:, 3072 + 128 * t:] for t in range(TT)],
                                           [PR[:, 1024:], HT[:, 2048:], late[:, 10240:], late[:, 11264:]])):
            e_ = 2 * len(qs)
            place.append([b[:, 0:e_ * SLOTS // 2].bitcast(BF16).rearrange("p (e s) -> p e s", e=e_) for b in starts])
        absb = carve(PR, 0, 2, CH)
        th = carve(g1b[:, :], 0, 2, FT, SLOTS)
        sl = carve(g1b[:, :], 256, 2, FT, SLOTS)
        hid = carve(g1b[:, :], 512, 2, FT, SLOTS)
        iota_s = iotas[:, 0:SLOTS]
        iota_e = iotas[:, 64:64 + E]
        iota_g = iotas[:, 96:96 + NG]
        iota_b = iotas[:, 100:100 + MAXB]
        ring = [AR[:, 6144 * s:6144 * (s + 1)] for s in range(4)] + [late[:, 0:6144], late[:, 6144:12288]]
        w13 = [carve(r, 0, 2, KT, F) for r in ring]
        w2s = [carve(r, 4096, FT, D) for r in ring]
        yg = carve(AR, 0, TT, 2, D)
        RT = acc[:, :, :].rearrange("p a b -> p (a b)")

        def worker(base, size):
            used = [0]

            def take(*shape):
                n = 1
                for k in shape:
                    n *= k
                used[0] += n
                assert used[0] <= size
                return carve(base, used[0] - n, *shape)
            return take

        work = worker(RT, 2 * D)
        lg = work(TT, NG + E)
        geq, goh, gdif, gexp, gpen = (work(TT, NG) for _ in range(5))
        gbest, gscore, gsum, best1, best2, score1, edif = (work(TT) for _ in range(7))
        em, eq1, maskf, rm = (work(TT, E) for _ in range(4))
        maskm, oh2b = (work(TT * E // 2).bitcast(BF16).rearrange("p (t e) -> p t e", t=TT) for _ in range(2))
        tok1, tokg = (work(PAIRS) for _ in range(2))
        work = worker(route[:, :], ROUTE)
        oh1, oh2, rk = (work(TT, E) for _ in range(3))
        cnt = work(E)
        nx = [work(E) for _ in range(3)]
        xsum = st[:, 0:2 * MAXB].rearrange("p (h b) -> p h b", h=2)
        posf = work(2, TT)
        xcmp = carve(g1b[:, :], 768, E // 2, MAXB)
        xem = wr[:, :, :].rearrange("p k n -> p (k n)")[:, 0:TT * E].rearrange("p (t e) -> p t e", t=TT)
        ysb = [carve(PR, 1024, D), carve(RT, 0, D), carve(RT, D, D)]

        CHUNKS = [("ada", 1, 0), ("ada", 1, 1), ("ada", 0, 0), ("ada", 0, 1), ("in", 0), ("in", 1), ("in", 2),
                  ("ada", 2, 0), ("in", 3), ("ada", 2, 1), ("in", 6), ("ada", 3, 0), ("in", 7), ("ada", 3, 1),
                  ("in", 4), ("ada", 4, 0), ("ada", 4, 1), ("in", 5), ("ada", 5, 0), ("ada", 5, 1), ("up",),
                  ("out", 0), ("out", 1)]
        at = {k: n for n, k in enumerate(CHUNKS)}
        ADA_NOW = CHUNKS[:4]
        ADA = [k for k in CHUNKS[4:] if k[0] == "ada"]
        IN = [k for k in CHUNKS if k[0] == "in"]
        UNITS = 4 * len(IN)
        U_V, U_P, U_GP, U_GA = 8, 12, 16, 24
        STEPS = HP * TT

        slot_loaded = [sem(f"slot_loaded{i}") for i in range(4)]
        x_loaded = [sem(f"x_loaded{i}") for i in range(TT)]
        c_loaded = sem("c_loaded")
        c_silu = sem("c_silu")
        small_loaded = sem("small_loaded")
        late_loaded = sem("late_loaded")
        cact_ready = sem("cact_ready")
        silu_ready = sem("silu_ready")
        sidx_ready = sem("sidx_ready")
        g_bias_loaded = sem("g_bias_loaded")
        consts_ready = sem("consts_ready")
        pool_link = sem("pool_link")
        chain = sem("chain")
        x_sq = sem("x_sq")
        x_var = sem("x_var")
        x_rstd = sem("x_rstd")
        xn_ready = sem("xn_ready")
        xT_ready = sem("xT_ready")
        hT_dve = sem("hT_dve")
        hT_act = sem("hT_act")
        ada_used = sem("ada_used")
        ada_rows_done = sem("ada_rows_done")
        ada_rows_out = sem("ada_rows_out")
        ada_cols_done = sem("ada_cols_done")
        ab1_ready = sem("ab1_ready")
        unit_done = sem("unit_done")
        unit_drained_dve = sem("unit_drained_dve")
        unit_drained_act = sem("unit_drained_act")
        qk_sq = sem("qk_sq")
        qk_var = sem("qk_var")
        qk_rstd = sem("qk_rstd")
        qkT_ready = sem("qkT_ready")
        qkT_drained = sem("qkT_drained")
        pooled = sem("pooled")
        scores_ready = sem("scores_ready")
        negmax_ready = sem("negmax_ready")
        probs_raw = sem("probs_raw")
        probs_ready = sem("probs_ready")
        PT_ready = sem("PT_ready")
        PT_drained = sem("PT_drained")
        attn_ready = sem("attn_ready")
        attn_drained = sem("attn_drained")
        side_done = sem("side_done")
        side_drained = sem("side_drained")
        up_done = sem("up_done")
        yo_done = sem("yo_done")
        yo_drained = sem("yo_drained")
        x1_sq = sem("x1_sq")
        x1_var = sem("x1_var")
        x1_rstd = sem("x1_rstd")
        xn2_ready = sem("xn2_ready")
        xn2_stored = [sem(f"xn2_stored{i}") for i in range(TT)]
        h2T_psum = sem("h2T_psum")
        h2T_dve = sem("h2T_dve")
        h2T_act = sem("h2T_act")
        logits_ready = sem("logits_ready")
        exp_in = sem("exp_in")
        exp_out = sem("exp_out")
        mask_ready = sem("mask_ready")
        rank_ready = sem("rank_ready")
        place_ready = sem("place_ready")
        idx_psum = sem("idx_psum")
        idx_ready = sem("idx_ready")
        iotas_ready = sem("iotas_ready")
        w13_loaded = [sem(f"w13_loaded{i}") for i in range(RING)]
        w2_loaded = [sem(f"w2_loaded{i}") for i in range(RING)]
        xg_loaded = [sem(f"xg_loaded{i}") for i in range(3)]
        xt_ready = sem("xt_ready")
        xgT_ready = sem("xgT_ready")
        xgT_act = sem("xgT_act")
        ab_done = sem("ab_done")
        ab_drained = sem("ab_drained")
        st_done = sem("st_done")
        th_ready = sem("th_ready")
        hid_ready = sem("hid_ready")
        y_done = sem("y_done")
        y_drained = sem("y_drained")
        y_stored = [sem(f"y_stored{i}") for i in range(3)]
        yg_loaded = [sem(f"yg_loaded{i}") for i in range(TT)]
        xtab_ready = sem("xtab_ready")
        x_loaded_w = sem("x_loaded_w")
        x_turns = sem("x_turns")
        x_rel = sem("x_rel")
        x_steps = sem("x_steps")
        x_base = sem("x_base")
        x_place = sem("x_place")
        x_idx_psum = sem("x_idx_psum")
        x_idx = sem("x_idx")
        x_rows = sem("x_rows")
        x_rowsT = sem("x_rowsT")
        x_in = sem("x_in")
        x_ab = sem("x_ab")
        x_ab_drained = sem("x_ab_drained")
        x_st = sem("x_st")
        x_th = sem("x_th")
        x_silu = sem("x_silu")
        x_hid = sem("x_hid")
        x_y = sem("x_y")
        x_y_drained = sem("x_y_drained")
        x_stored = sem("x_stored")
        overflow_done = sem("overflow_done")
        out_ready = sem("out_ready")
        out_stored = sem("out_stored")

        C_, N1, N2, PS, BA = 0, 1, 2, 3, 4
        SMALL, LATE = 7, 6

        def overflow_blocks(eng, body):
            eng.wait_ge(xtab_ready, 1)
            n = eng.value_load(xtab[0:1, MAXB:MAXB + 1], min_val=0, max_val=MAXB)
            with eng.If(n > 0):
                with eng.Fori(0, n) as b:
                    body(b)

        def all_experts(eng, step, before_last=None):
            for n in range(HEAD + RING):
                step(n, 0)
            with eng.Fori(1, TURNS - 1) as turn:
                for j in range(RING):
                    step(HEAD + j, turn)
            if before_last:
                before_last()
            for n in range(E - RING, E):
                step(n, 0)

        def reached(n, turn, m):
            return n >= m if isinstance(turn, int) else True

        xplace = MG.bitcast(BF16)[:, 0:2 * TT * SLOTS].rearrange("p (n s) -> p n s", s=SLOTS)

        block = ctx.enter_context(nc.Block())

        SIDE = ([("g1", 0), ("g1", 1)] + [("B", m) for m in range(KT)] + [("cols",), ("g2", 0), ("g2", 1)]
                + [("A", m) for m in range(KT)])
        side_no = {k: n for n, k in enumerate(SIDE)}
        FIRST_A = side_no[("A", 0)]

        def side_bank(n):
            return 7 if n < FIRST_A or (n - FIRST_A) % 2 == 0 else 6

        def drained(eng, u):
            if u < U_V:
                eng.wait_ge(unit_drained_dve, u + 1)
            else:
                eng.wait_ge(unit_drained_act, u - U_V + 1)

        @block.sync
        def _(sp):
            sp.dma_start(cols[:, C_, :], c.rearrange("b (p k) -> (b p) k", k=KT)).then_inc(c_loaded, 16)
            for n, k in enumerate(CHUNKS):
                if n == 1:
                    for t in range(TT):
                        sp.dma_start(xs[:, t, :], x_v[t]).then_inc(x_loaded[t], 16)
                if n >= 4:
                    old = CHUNKS[n - 4]
                    if old[0] == "in":
                        sp.wait_ge(unit_done, 4 * (IN.index(old) + 1))
                    elif old in ADA_NOW:
                        sp.wait_ge(ada_rows_done, ADA_NOW.index(old) + 1)
                    else:
                        sp.wait_ge(ada_used, ADA.index(old) + 1)
                if k[0] == "ada":
                    src = ada_v[:, 4 * k[2]:4 * k[2] + 4, D * k[1]:D * (k[1] + 1)]
                    dst = slot[n % 4].rearrange("p (k n) -> p k n", k=4)
                elif k[0] == "in":
                    src = win_v[:, :, CH * k[1]:CH * (k[1] + 1)]
                    dst = slot[n % 4].rearrange("p (k n) -> p k n", k=KT)
                elif k[0] == "up":
                    src = wup_v
                    dst = slot[n % 4].rearrange("p (k n) -> p k n", k=HP)
                else:
                    src = wout_v[:, :, CH * k[1]:CH * (k[1] + 1)]
                    dst = slot[n % 4].rearrange("p (k n) -> p k n", k=KT)
                sp.dma_start(dst, src).then_inc(slot_loaded[n % 4], 16)
            sp.wait_ge(side_drained, len(SIDE))

            def load13(e, s):
                sp.dma_start(w13[s][:, 0].rearrange("p k f -> p (k f)"), w1_v[e]).then_inc(w13_loaded[s], 16)
                sp.dma_start(w13[s][:, 1].rearrange("p k f -> p (k f)"), w3_v[e]).then_inc(w13_loaded[s], 16)

            def load2(e, s):
                sp.dma_start(w2s[s].rearrange("p k n -> p (k n)"), w2_v[e]).then_inc(w2_loaded[s], 16)

            def load_pair(n, turn):
                e = n + turn * RING
                for j in range(2):
                    sp.wait_ge(ab_done, e + (j + 1 - RING))
                    load13(e + j, (n + j) % RING)
                sp.wait_ge(y_done, turn * (RING // 2) + (n // 2 + 1 - RING // 2))
                for j in range(2):
                    load2(e + j, (n + j) % RING)

            for e in range(RING):
                if e == 4:
                    sp.wait_ge(yo_done, 2 * TT)
                load13(e, e)
                if e == 5:
                    sp.wait_ge(idx_psum, 2)
                load2(e, e)
            for n in range(RING, RING + HEAD, 2):
                load_pair(n, 0)
            with sp.Fori(1, TURNS) as turn:
                for j in range(0, RING, 2):
                    load_pair(HEAD + j, turn)

            def overflow(b):
                e = sp.value_load(xtab[0:1, bass.ds(b, 1)], min_val=0, max_val=E - 1)
                for src, dst in ((w1_v, w13[0][:, 0].rearrange("p k f -> p (k f)")),
                                 (w3_v, w13[0][:, 1].rearrange("p k f -> p (k f)")),
                                 (w2_v, w2s[0].rearrange("p k n -> p (k n)"))):
                    sp.dma_start(dst, src[bass.ds(e, 1)].rearrange("o p n -> (o p) n")).then_inc(x_loaded_w, 16)
                sp.wait_ge(x_y, b + 1)
                sp.sem_inc(x_turns, 1)

            sp.wait_ge(y_done, PAIRS)
            overflow_blocks(sp, overflow)
            for i in range(3):
                sp.wait_ge(y_stored[i], 16 * len(range(i, PAIRS, 3)))
            sp.wait_ge(overflow_done, 1)
            for t in range(TT):
                sp.dma_start(yg[:, t].rearrange("p j d -> p (j d)"),
                             y_d[2 * P * t:2 * P * (t + 1), :].rearrange("(p j) d -> p (j d)", j=2)
                             ).then_inc(yg_loaded[t], 16)
            for t in range(TT):
                sp.wait_ge(out_ready, t + 1)
                sp.dma_start(out_v[t], xs[:, t, :]).then_inc(out_stored, 16)
            sp.wait_ge(out_stored, 16 * TT)

        @block.tensor
        def _(pe):
            mm = nc.tensor.matmul

            def chunk_here(k):
                pe.wait_ge(slot_loaded[at[k] % 4], 16 * (at[k] // 4 + 1))

            def x_transposes(ks, t):
                for k in ks:
                    last = nc.tensor.transpose(bank[:, k, P * t:P * (t + 1)],
                                               xn[:, t, k:D:KT], ident[:, :])
                last.then_inc(xT_ready, 1)

            def unit_half(u, h):
                ch = IN[u // 4]
                w = slot[at[ch] % 4].rearrange("p (k n) -> p k n", k=KT)
                if h == 0:
                    if u % 4 == 0:
                        chunk_here(ch)
                    if u >= 2:
                        drained(pe, u - 2)
                m = P * (u % 4)
                for k in range(4 * h, 4 * h + 4):
                    if u == 0:
                        pe.wait_ge(hT_act if k % 2 else hT_dve, k // 2 + 1)
                    if u < U_P:
                        last = mm(bank[:, u % 2, :], hT[:, k, m:m + P], w[:, k, :], start=k == 0, stop=k == 7)
                    else:
                        last = mm(bank[:, u % 2, :], w[:, k, m:m + P], hT[:, k, :], start=k == 0, stop=k == 7)
                if h == 1:
                    last.then_inc(unit_done, 1)

            def qk_transposes(u):
                pe.wait_ge(unit_drained_dve, u + 1)
                if u >= 2:
                    pe.wait_ge(qkT_drained, u - 1)
                for j in range(HP):
                    last = nc.tensor.transpose(bank[:, 4 + u % 2, P * j:P * (j + 1)],
                                               qn[:, u % 2, P * j:P * (j + 1)], ident[:, :])
                last.then_inc(qkT_ready, 1)

            def scores(a):
                j, qt = a // TT, a % TT
                if a == 0:
                    pe.wait_ge(qkT_drained, 8)
                else:
                    pe.wait_ge(probs_raw, 2 * a)
                n = P * (qt + 1)
                for h in range(2):
                    r = slice(HD * h, HD * (h + 1))
                    mm(bank[:, 2 + h, 0:n], qT[r, j, P * qt:P * (qt + 1)], kT[r, j, 0:n], start=True, stop=True)
                for h in range(2):
                    last = mm(bank[:, 2 + h, P * qt:n], identb[:, :], maskb[:, :], start=False, stop=True,
                              skip_group_check=True)
                last.then_inc(scores_ready, 1)

            def prob_transposes(a):
                qt = a % TT
                pe.wait_ge(probs_ready, a + 1)
                if a >= 1:
                    pe.wait_ge(PT_drained, a)
                for h in range(2):
                    for kt in range(qt + 1):
                        last = nc.tensor.transpose(bank[:, 4 + h, P * kt:P * (kt + 1)],
                                                   probs[:, a % 2, h, P * kt:P * (kt + 1)], ident[:, :])
                last.then_inc(PT_ready, 1)

            def pv(a):
                j, qt = a // TT, a % TT
                pe.wait_ge(PT_drained, a + 1)
                if a == 0:
                    pe.wait_ge(unit_drained_act, 4)
                if a >= 1:
                    pe.wait_ge(attn_drained, a)
                q = slice(P * (a % 4), P * (a % 4) + P)
                for kt in range(qt + 1):
                    for h in range(2):
                        last = mm(bank[HD * h:HD * (h + 1), 6, q], vt[:, kt, P * j + HD * h:P * j + HD * (h + 1)],
                                  PT[:, a % 2, h, kt, :], start=kt == 0, stop=kt == qt)
                last.then_inc(attn_ready, 1)

            def side(*k):
                n = side_no[k]
                b = side_bank(n)
                if n > FIRST_A + 1:
                    pe.wait_ge(side_drained, n - 1)
                elif n == FIRST_A + 1:
                    pe.wait_ge(attn_drained, STEPS)
                elif n > 0:
                    pe.wait_ge(side_drained, n)
                if k[0] in ("g1", "g2"):
                    pe.wait_ge(ada_used, 2 if k[0] == "g1" else 8)
                    last = mm(bank[:, b, :], ones[:, :], acc[:, k[0] == "g2", CH * k[1]:CH * (k[1] + 1)],
                              start=True, stop=True)
                elif k[0] == "B":
                    m = k[1]
                    pe.wait_ge(pooled, m // 2 + 1)
                    if m == 0:
                        pe.wait_ge(late_loaded, 16 * LATE)
                    last = mm(bank[:, b, :], pw[:, m // 2, P * (m % 2):P * (m % 2) + P], pT[:, m // 2, :],
                              start=True, stop=True)
                elif k[0] == "cols":
                    pe.wait_ge(ada_used, 6)
                    for v in range(2):
                        for kk in range(KT):
                            last = mm(bank[:, b, 8 * v + kk:8 * v + kk + 1], acc[:, v, kk:D:KT], ones[:, 0:1],
                                      start=True, stop=True)
                else:
                    m = k[1]
                    if m == 0:
                        pe.wait_ge(side_drained, n)
                        chunk_here(("up",))
                        pe.wait_ge(attn_drained, STEPS)
                    wu = slot[at[("up",)] % 4].rearrange("p (k n) -> p k n", k=HP)
                    for kk in range(HP):
                        last = mm(bank[:, b, :], wu[:, kk, P * m:P * (m + 1)], attnT[:, kk, :],
                                  start=kk == 0, stop=kk == HP - 1)
                last.then_inc(side_done, 1)

            def ada_rows(v, part_half):
                n = 2 * v + part_half
                pe.wait_ge(slot_loaded[n], 16)
                w = slot[n].rearrange("p (k n) -> p k n", k=4)
                for kk in range(4):
                    k = 4 * part_half + kk
                    for h in range(2):
                        r = 32 * (2 * v + h)
                        last = mm(bank[r:r + 1, 7, :], cols[:, C_, k:k + 1], w[:, kk, CH * h:CH * (h + 1)],
                                  start=k == 0, stop=k == KT - 1, tile_position=(0, r))
                last.then_inc(ada_rows_done, 1)

            def ada_columns(v):
                pe.wait_ge(ada_rows_out, 2 * v + 2)
                for h in range(2):
                    r = 32 * (2 * v + h)
                    for m in range(KT):
                        last = mm(bank[SLOTS * h:SLOTS * (h + 1), 6, 8 * v + m:8 * v + m + 1],
                                  rows[r:r + 1, m:CH:KT], ones[r:r + 1, 0:1], start=True, stop=True,
                                  tile_position=(r, SLOTS * h))
                if v == 1:
                    last.then_inc(ada_cols_done, 1)

            pe.wait_ge(c_silu, 1)
            ada_rows(0, 0)
            ada_rows(0, 1)
            pe.wait_ge(consts_ready, 1)
            for t in range(TT):
                pe.wait_ge(xn_ready, t + 1)
                x_transposes(range(6), t)
            ada_rows(1, 0)
            ada_columns(0)
            ada_rows(1, 1)
            ada_columns(1)
            pe.wait_ge(ab1_ready, 1)
            for t in range(TT):
                x_transposes([6, 7], t)

            for u in range(UNITS):
                a = u - U_P
                if 0 <= a < STEPS:
                    scores(a)
                unit_half(u, 0)
                if 1 <= u <= 8:
                    qk_transposes(u - 1)
                if 0 <= a - 1 < STEPS:
                    prob_transposes(a - 1)
                unit_half(u, 1)
                if 0 <= a - 2 < STEPS:
                    pv(a - 2)
                if u in (U_P, U_P + 1):
                    side("g1", u - U_P)
                if U_GP + 1 <= u <= U_GA:
                    side("B", u - 1 - U_GP)
                if u == 27:
                    side("cols")
            side("g2", 0)
            side("g2", 1)
            for m in range(KT):
                side("A", m)

            def project(t, h):
                n = 2 * t + h
                if n >= 2:
                    pe.wait_ge(yo_drained, n - 1)
                if t == 0:
                    chunk_here(("out", h))
                w = slot[at[("out", h)] % 4].rearrange("p (k n) -> p k n", k=KT)
                for k in range(KT):
                    last = mm(bank[:, n % 2, :], mergedT[:, k, P * t:P * (t + 1)], w[:, k, :],
                              start=k == 0, stop=k == KT - 1)
                last.then_inc(yo_done, 1)

            def h2_transposes(t):
                pe.wait_ge(xn2_ready, t + 1)
                if t >= 2:
                    pe.wait_ge(h2T_dve, t - 1)
                    pe.wait_ge(h2T_act, t - 1)
                for k in range(KT):
                    last = nc.tensor.transpose(bank[:, 2 + 2 * (t % 2) + k % 2, P * (k // 2):P * (k // 2 + 1)],
                                               xn2[:, t, k:D:KT], ident[:, :])
                last.then_inc(h2T_psum, 1)

            def router(t):
                pe.wait_ge(h2T_dve, t + 1)
                pe.wait_ge(h2T_act, t + 1)
                o = bank[:, 6, 36 * t:36 * (t + 1)]
                for k in range(KT):
                    mm(o, h2T[:, t % 2, k, :], wr[:, k, :], start=k == 0, stop=False)
                mm(o, ones[0:1, :], br[:, :], start=False, stop=True).then_inc(logits_ready, 1)

            pe.wait_ge(side_drained, len(SIDE))
            for t in range(TT + 1):
                if t < TT:
                    project(t, 0)
                if t >= 1:
                    h2_transposes(t - 1)
                if t < TT:
                    project(t, 1)
                if t >= 1:
                    router(t - 1)

            pe.wait_ge(mask_ready, 1)
            maskv = maskm
            for t in range(TT):
                for s in range(t):
                    mm(bank[:, 7, 32 * t:32 * (t + 1)], onesb[:, :], maskv[:, s, :], start=s == 0, stop=False)
                mm(bank[:, 7, 32 * t:32 * (t + 1)], lowb[:, :], maskv[:, t, :], start=t == 0, stop=True)
            for s in range(TT):
                last = mm(bank[:, 7, 128:160], onesb[:, :], maskv[:, s, :], start=s == 0, stop=s == TT - 1)
            last.then_inc(rank_ready, 1)

            def slot_sums(g):
                pe.wait_ge(place_ready, g + 1)
                for q in IDX_GROUPS[g]:
                    for c, rhs in ((0, tokc[:, :, :]), (2, oh2b[:, :, 2 * q:2 * q + 2])):
                        for t in range(TT):
                            e = 2 * (q - IDX_GROUPS[g][0])
                            lhs = place[g][t][:, e:e + 2, :].rearrange("p e s -> p (e s)")
                            last = mm(idx_bank(g)[:, 4 * q + c:4 * q + c + 2], lhs, rhs[:, t, :],
                                      start=t == 0, stop=t == TT - 1)
                last.then_inc(idx_psum, 1)

            slot_sums(0)

            def gather_transposes(n, turn):
                q = n + turn * (RING // 2)
                pe.wait_ge(xg_loaded[n % 3], turn * 16 + 16 * (n // 3 + 1))
                if reached(n, turn, 1):
                    pe.wait_ge(xgT_ready, q)
                    pe.wait_ge(xgT_act, q)
                for k in range(KT):
                    last = nc.tensor.transpose(bank[:, k // 4, P * (k % 4):P * (k % 4 + 1)],
                                               xg[:, n % 3, k:D:KT], ident[:, :])
                last.then_inc(xt_ready, 1)

            def gate_up(n, turn):
                e, s = n + turn * RING, n % RING
                pe.wait_ge(w13_loaded[s], turn * 32 + 32 * (n // RING + 1))
                if n % 2 == 0:
                    pe.wait_ge(xgT_ready, n // 2 + 1 + turn * (RING // 2))
                    pe.wait_ge(xgT_act, n // 2 + 1 + turn * (RING // 2))
                if reached(n, turn, 2):
                    pe.wait_ge(ab_drained, e - 1)
                for k in range(KT):
                    r = slice(SLOTS * (k % 2), SLOTS * (k % 2 + 1))
                    last = mm(bank[r, 2 + n % 2, :].rearrange("p (w f) -> p w f", w=2),
                              xgT[:, k, SLOTS * (n % 2):SLOTS * (n % 2 + 1)],
                              w13[s][:, :, k, :], start=k < 2, stop=k >= KT - 2)
                last.then_inc(ab_done, 1)

            def fold_halves(n, turn):
                e = n + turn * RING
                pe.wait_ge(ab_drained, e + 1)
                if reached(n, turn, 2):
                    pe.wait_ge(hid_ready, e - 1)
                for w in range(2):
                    for ft in range(FT):
                        last = mm(bank[:, 4 + n % 2, SLOTS * (2 * w + ft):SLOTS * (2 * w + ft + 1)],
                                  absb[:, n % 2, F * w + ft:F * (w + 1):FT], fold[:, :], start=True, stop=True)
                last.then_inc(st_done, 1)

            def down(n, turn):
                q = n // 2 + turn * (RING // 2)
                slots = (n % RING, (n + 1) % RING)
                pe.wait_ge(hid_ready, n + 2 + turn * RING)
                for s in slots:
                    pe.wait_ge(w2_loaded[s], turn * 16 + 16 * (n // RING + 1))
                if reached(n, turn, 2):
                    pe.wait_ge(y_drained, q)
                for ft in range(FT):
                    for h in range(2):
                        for x, s in enumerate(slots):
                            last = mm(bank[SLOTS * x:SLOTS * (x + 1), 6 + h, :], hid[:, x, ft, :],
                                      w2s[s][:, ft, CH * h:CH * (h + 1)], start=ft == 0, stop=ft == FT - 1)
                last.then_inc(y_done, 1)

            def step(n, turn):
                if reached(n, turn, 1):
                    fold_halves(n - 1, turn)
                gate_up(n, turn)
                if n % 2 == 0 and reached(n, turn, 2):
                    down(n - 2, turn)
                if n == 0:
                    slot_sums(1)
                if n % 2 and n < E - 1:
                    gather_transposes((n + 1) // 2, turn)

            pe.wait_ge(idx_ready, 1)
            gather_transposes(0, 0)
            all_experts(pe, step)
            fold_halves(E - 1, 0)
            down(E - 2, 0)

            def overflow(b):
                pe.wait_ge(x_place, b + 1)
                for n in range(2 * TT):
                    mm(bank[0:SLOTS, 0, 0:2], xplace[:, n, :], tokc[:, n % TT, :],
                       start=n == 0, stop=n == 2 * TT - 1)
                for n in range(TT, 2 * TT):
                    last = mm(bank[0:SLOTS, 0, 2:3], xplace[:, n, :], onesb[:, 0:1],
                              start=n == TT, stop=n == 2 * TT - 1)
                last.then_inc(x_idx_psum, 1)
                pe.wait_ge(x_rows, 16 * b + 16)
                for k in range(KT):
                    last = nc.tensor.transpose(bank[:, k // 4, P * (k % 4):P * (k % 4 + 1)],
                                               xg[:, 0, k:D:KT], ident[:, :])
                last.then_inc(x_rowsT, 1)
                pe.wait_ge(x_in, b + 1)
                pe.wait_ge(x_loaded_w, 48 * b + 48)
                for k in range(KT):
                    r = slice(SLOTS * (k % 2), SLOTS * (k % 2 + 1))
                    last = mm(bank[r, 2, :].rearrange("p (w f) -> p w f", w=2), xgT[:, k, 0:SLOTS],
                              w13[0][:, :, k, :], start=k < 2, stop=k >= KT - 2)
                last.then_inc(x_ab, 1)
                pe.wait_ge(x_ab_drained, b + 1)
                for w in range(2):
                    for ft in range(FT):
                        last = mm(bank[:, 4, SLOTS * (2 * w + ft):SLOTS * (2 * w + ft + 1)],
                                  absb[:, 0, F * w + ft:F * (w + 1):FT], fold[:, :], start=True, stop=True)
                last.then_inc(x_st, 1)
                pe.wait_ge(x_hid, b + 1)
                for ft in range(FT):
                    for h in range(2):
                        last = mm(bank[0:SLOTS, 6 + h, :], hid[:, 0, ft, :],
                                  w2s[0][:, ft, CH * h:CH * (h + 1)], start=ft == 0, stop=ft == FT - 1)
                last.then_inc(x_y, 1)

            pe.wait_ge(y_drained, PAIRS)
            overflow_blocks(pe, overflow)

        @block.scalar
        def _(act):
            sc = nc.scalar
            act.dma_start(cols[:, N1, :], norm1.rearrange("b (p k) -> (b p) k", k=KT)).then_inc(small_loaded, 16)
            act.dma_start(cols[:, N2, :], norm2.rearrange("b (p k) -> (b p) k", k=KT)).then_inc(small_loaded, 16)
            act.dma_start(cols[:, BA:BA + 6, :], bada_v).then_inc(small_loaded, 16)
            for h in range(2):
                r = slice(HD * h, HD * (h + 1))
                act.dma_start(qkg[r, 0:1], q_norm.rearrange("a (p b) -> (a p) b", b=1)).then_inc(small_loaded, 16)
                act.dma_start(qkg[r, 1:2], k_norm.rearrange("a (p b) -> (a p) b", b=1)).then_inc(small_loaded, 16)
            act.wait_ge(c_loaded, 16)
            sc.activation(cth, cols[:, C_, :], ACT.Tanh, scale=0.5).then_inc(cact_ready, 1)
            for t in range(TT):
                act.wait_ge(x_loaded[t], 16)
                sc.activation(xn[:, t, :], xs[:, t, :], ACT.Square, accum_out=st[:, t:t + 1]).then_inc(x_sq, 1)
            for k in range(1, KT, 2):
                act.wait_ge(ab1_ready, 1)
                act.wait_ge(xT_ready, 4 if k < 6 else 8)
                sc.activation(hT[:, k, :], bank[:, k, :], ACT.Identity, bias=ab1[:, 1, k:k + 1],
                              scale=ab1[:, 0, k:k + 1]).then_inc(hT_act, 1)

            def attend_exp(a):
                n = P * (a % TT + 1)
                act.wait_ge(negmax_ready, a + 1)
                if a >= 2:
                    act.wait_ge(PT_ready, a - 1)
                for h in range(2):
                    sc.activation(probs[:, a % 2, h, 0:n], bank[:, 2 + h, 0:n], ACT.Exp,
                                  bias=st[:, 18 + h + 4 * (a % 2):19 + h + 4 * (a % 2)],
                                  accum_out=st[:, 28 + h + 4 * (a % 2):29 + h + 4 * (a % 2)]).then_inc(probs_raw, 1)

            def attend_pt(a):
                n = P * (a % TT + 1)
                act.wait_ge(PT_ready, a + 1)
                if a >= 2:
                    act.wait_ge(attn_ready, a - 1)
                sc.copy(PT[:, a % 2].rearrange("p h k q -> p h (k q)")[:, :, 0:n],
                        bank[:, 4:6, 0:n]).then_inc(PT_drained, 1)

            def attend_out(a):
                act.wait_ge(attn_ready, a + 1)
                sc.copy(attnT[:, a // TT, P * (a % TT):P * (a % TT + 1)],
                        bank[:, 6, P * (a % 4):P * (a % 4 + 1)]).then_inc(attn_drained, 1)

            for u in range(UNITS):
                a = u - U_P
                if 0 <= a < STEPS:
                    attend_exp(a)
                if 0 <= a - 1 < STEPS:
                    attend_pt(a - 1)
                act.wait_ge(unit_done, u + 1)
                if u == 3:
                    act.dma_start(g1b[:, :], b_ada[0, 2 * D:3 * D].partition_broadcast(P)).then_inc(g_bias_loaded, 16)
                    act.dma_start(g2b[:, :], b_ada[0, 5 * D:6 * D].partition_broadcast(P)).then_inc(g_bias_loaded, 16)
                if u < U_V:
                    if u >= 1:
                        act.wait_ge(qk_var, u)
                    sc.activation(sqbuf, bank[:, u % 2, :], ACT.Square).then_inc(qk_sq, 1)
                elif u < U_P:
                    sc.copy(vt[:, u - U_V, :], bank[:, u % 2, :]).then_inc(unit_drained_act, 1)
                elif u < U_GP:
                    sc.copy(pT[:, u - U_P, :], bank[:, u % 2, :]).then_inc(unit_drained_act, 1)
                else:
                    m = (u - U_GP) % KT
                    to = m if u >= U_GA else m % 2
                    if U_GP + 2 <= u <= U_GA:
                        act.wait_ge(side_drained, side_no[("B", min(m - 2 if u < U_GA else 7, 7))] + 1)
                    sc.activation(sg[:, to, :], bank[:, u % 2, :], ACT.Tanh, scale=0.5).then_inc(unit_drained_act, 1)
                if 0 <= a - 2 < STEPS:
                    attend_out(a - 2)

            def square(t):
                act.wait_ge(yo_drained, 2 * t + 2)
                if t == 0:
                    act.wait_ge(unit_done, UNITS)
                sc.activation(xn2[:, t, :], xs[:, t, :], ACT.Square,
                              accum_out=st[:, 8 + t:9 + t]).then_inc(x1_sq, 1)

            def modulate(t):
                act.wait_ge(h2T_psum, t + 1)
                if t == 0:
                    act.wait_ge(PT_ready, STEPS)
                if t >= 2:
                    act.wait_ge(logits_ready, t - 1)
                for k in range(1, KT, 2):
                    last = sc.activation(h2T[:, t % 2, k, :],
                                         bank[:, 3 + 2 * (t % 2), P * (k // 2):P * (k // 2 + 1)], ACT.Identity,
                                         bias=ab2[:, 1, k:k + 1], scale=ab2[:, 0, k:k + 1])
                last.then_inc(h2T_act, 1)

            for t in range(TT + 1):
                if t >= 1:
                    act.wait_ge(xn2_ready, t)
                    act.dma_start(xn2_d[P * (t - 1):P * t, :], xn2[:, t - 1, :]).then_inc(xn2_stored[t - 1], 16)
                    modulate(t - 1)
                if t < TT:
                    square(t)
            act.wait_ge(exp_in, 1)
            sc.activation(gexp, gdif, ACT.Exp).then_inc(exp_out, 1)
            act.wait_ge(exp_in, 2)
            sc.activation(edif, edif, ACT.Exp).then_inc(exp_out, 1)

            def modulate_gathered(n, turn):
                q = n + turn * (RING // 2)
                act.wait_ge(xt_ready, q + 1)
                if reached(n, turn, 1):
                    act.wait_ge(ab_done, q * 2)
                for k in range(KT // 2, KT):
                    last = sc.activation(xgT[:, k, :], bank[:, 1, P * (k % 4):P * (k % 4 + 1)], ACT.Identity,
                                         bias=ab2[:, 1, k:k + 1], scale=ab2[:, 0, k:k + 1])
                last.then_inc(xgT_act, 1)

            def step(n, turn):
                e, b = n + turn * RING, n % 2
                act.wait_ge(ab_done, e + 1)
                if reached(n, turn, 2):
                    act.wait_ge(st_done, e - 1)
                sc.copy(absb[:, b, :], bank[:, 2 + b, :]).then_inc(ab_drained, 1)
                if n % 2 and n < E - 1:
                    modulate_gathered((n + 1) // 2, turn)
                act.wait_ge(st_done, e + 1)
                if reached(n, turn, 2):
                    act.wait_ge(hid_ready, e - 1)
                sc.activation(th[:, b].rearrange("p f s -> p (f s)"), bank[:, 4 + b, 0:FT * SLOTS],
                              ACT.Tanh, scale=0.5).then_inc(th_ready, 1)

            act.wait_ge(yo_drained, 2 * TT)
            modulate_gathered(0, 0)
            all_experts(act, step)

            def overflow(b):
                act.wait_ge(x_ab, b + 1)
                sc.copy(absb[:, 0, :], bank[:, 2, :]).then_inc(x_ab_drained, 1)
                act.wait_ge(x_st, b + 1)
                sc.activation(th[:, 0].rearrange("p f s -> p (f s)"), bank[:, 4, 0:FT * SLOTS],
                              ACT.Tanh, scale=0.5).then_inc(x_th, 1)

            overflow_blocks(act, overflow)

        @block.vector
        def _(dve):
            v = nc.vector
            count = [0]

            def link(ins):
                count[0] += 1
                ins.then_inc(chain, 1)
                dve.wait_ge(chain, count[0])

            def ada(k):
                n, part, half = at[k], k[1], k[2]
                b = {2: 0, 3: 1, 4: 0, 5: 1}[part]
                w = slot[n % 4].rearrange("p (k n) -> p k n", k=4)
                dve.wait_ge(slot_loaded[n % 4], 16 * (n // 4 + 1))
                if half == 0 and part == 4:
                    dve.wait_ge(side_done, 2)
                if half == 0 and part == 5:
                    dve.wait_ge(side_done, side_no[("cols",)] + 1)
                for kk in range(4):
                    cc = cols[:, C_, 4 * half + kk:4 * half + kk + 1]
                    if half == 0 and kk == 0:
                        ins = v.tensor_scalar(acc[:, b, :], w[:, kk, :], cc, None, ALU.mult)
                    else:
                        ins = v.scalar_tensor_tensor(out=acc[:, b, :], in0=w[:, kk, :], scalar=cc,
                                                     in1=acc[:, b, :], op0=ALU.mult, op1=ALU.add)
                    if kk < 3:
                        link(ins)
                ins.then_inc(ada_used, 1)
                dve.wait_ge(ada_used, ADA.index(k) + 1)

            dve.wait_ge(cact_ready, 1)
            link(v.scalar_tensor_tensor(out=cols[:, C_, :], in0=cth, scalar=1.0, in1=cols[:, C_, :],
                                        op0=ALU.add, op1=ALU.mult))
            ins = v.tensor_scalar(cols[:, C_, :], cols[:, C_, :], 0.5, None, ALU.mult)
            ins.then_inc(c_silu, 1)
            dve.wait_ge(c_silu, 1)
            dve.wait_ge(x_sq, TT)
            v.tensor_scalar(st[:, 4:8], st[:, 0:4], 1.0 / D, EPS, ALU.mult, ALU.add).then_inc(x_var, 1)
            dve.wait_ge(x_rstd, 1)
            for t in range(TT):
                v.tensor_scalar(xn[:, t, :], xs[:, t, :], st[:, 12 + t:13 + t], None, ALU.mult).then_inc(xn_ready, 1)
            dve.wait_ge(small_loaded, 16 * SMALL)
            link(v.tensor_scalar(qkg[:, 0:1], qkg[:, 0:1], HD ** -0.5, None, ALU.mult))

            def norm_cols(src, nrow, dst, jb_scale, jb_shift, done):
                link(v.tensor_tensor(dst[:, 1, :], src[:, 8:16], cols[:, BA + jb_shift, :], ALU.add))
                link(v.tensor_tensor(dst[:, 0, :], src[:, 0:8], cols[:, BA + jb_scale, :], ALU.add))
                v.scalar_tensor_tensor(out=dst[:, 0, :], in0=dst[:, 0, :], scalar=1.0, in1=cols[:, nrow, :],
                                       op0=ALU.add, op1=ALU.mult).then_inc(done, 1)

            for v_ in range(2):
                dve.wait_ge(ada_rows_done, 2 * v_ + 2)
                for r in (64 * v_, 64 * v_ + 32):
                    v.tensor_copy(rows[r:r + 1, :], bank[r:r + 1, 7, :]).then_inc(ada_rows_out, 1)
            dve.wait_ge(ada_cols_done, 1)
            norm_cols(bank[:, 6, :], N1, ab1, 1, 0, ab1_ready)
            dve.wait_ge(ab1_ready, 1)
            for k in range(0, KT, 2):
                dve.wait_ge(xT_ready, 4 if k < 6 else 8)
                v.tensor_scalar(hT[:, k, :], bank[:, k, :], ab1[:, 0, k:k + 1], ab1[:, 1, k:k + 1],
                                ALU.mult, ALU.add).then_inc(hT_dve, 1)

            def qk_norm(u):
                b = u % 2
                dve.wait_ge(qk_sq, u + 1)
                v.tensor_reduce(ss[:, b, 0, :], sqbuf.rearrange("p (h d) -> p h d", h=HEADS), AX.X,
                                ALU.add).then_inc(chain, 1)
                count[0] += 1
                dve.wait_ge(chain, count[0])
                v.tensor_scalar(ss[:, b, 0, :], ss[:, b, 0, :], 1.0 / HD, EPS, ALU.mult, ALU.add).then_inc(qk_var, 1)

            def qk_scale(u):
                b = u % 2
                dve.wait_ge(qk_rstd, u + 1)
                if u >= 2:
                    dve.wait_ge(qkT_ready, u - 1)
                v.tensor_tensor(qn[:, b, :].rearrange("p (h d) -> p h d", h=HEADS),
                                bank[:, u % 2, :].rearrange("p (h d) -> p h d", h=HEADS),
                                ss[:, b, 1, :].unsqueeze(2).broadcast_to([P, HEADS, HD]),
                                ALU.mult).then_inc(unit_drained_dve, 1)

            def qk_gain(u):
                dve.wait_ge(qkT_ready, u + 1)
                dst = (qT if u < 4 else kT)[:, :, P * (u % 4):P * (u % 4 + 1)]
                g = qkg[:, 0:1] if u < 4 else qkg[:, 1:2]
                v.tensor_scalar(dst, bank[:, 4 + u % 2, :].rearrange("p (j q) -> p j q", j=HP), g, None,
                                ALU.mult).then_inc(qkT_drained, 1)

            def attend_max(a):
                n = P * (a % TT + 1)
                o = 4 * (a % 2)
                dve.wait_ge(scores_ready, a + 1)
                link(v.tensor_reduce(st[:, 16 + o:18 + o], bank[:, 2:4, 0:n], AX.X, ALU.max))
                v.tensor_scalar(st[:, 18 + o:20 + o], st[:, 16 + o:18 + o], -1.0, None,
                                ALU.mult).then_inc(negmax_ready, 1)

            def attend_norm(a):
                n = P * (a % TT + 1)
                o = 4 * (a % 2)
                dve.wait_ge(probs_raw, 2 * a + 2)
                link(v.reciprocal(st[:, 30 + o:32 + o], st[:, 28 + o:30 + o]))
                for h in range(2):
                    last = v.tensor_scalar(probs[:, a % 2, h, 0:n], probs[:, a % 2, h, 0:n],
                                           st[:, 30 + o + h:31 + o + h], None, ALU.mult)
                last.then_inc(probs_ready, 1)

            def side(*k):
                n = side_no[k]
                b = side_bank(n)
                dve.wait_ge(side_done, n + 1)
                if k[0] in ("g1", "g2"):
                    g = (g1b if k[0] == "g1" else g2b)[:, CH * k[1]:CH * (k[1] + 1)]
                    dve.wait_ge(g_bias_loaded, 32)
                    v.tensor_tensor(g, bank[:, b, :], g, ALU.add).then_inc(side_drained, 1)
                elif k[0] == "cols":
                    norm_cols(bank[:, b, :], N2, ab2, 4, 3, side_drained)
                elif k[0] == "B":
                    m = k[1]
                    if m == 0:
                        dve.wait_ge(xT_ready, 8)
                        dve.wait_ge(late_loaded, 16 * LATE)
                        link(v.tensor_scalar(cols[:, PS, :], cols[:, PS, :], 0.5, None, ALU.mult))
                    dve.wait_ge(unit_drained_act, U_GP - U_V + m + 1)
                    link(v.tensor_scalar(mergedT[:, m, :], bank[:, b, :], cols[:, PS, m:m + 1], None, ALU.mult))
                    v.scalar_tensor_tensor(out=mergedT[:, m, :], in0=sg[:, m % 2, :], scalar=1.0,
                                           in1=mergedT[:, m, :], op0=ALU.add, op1=ALU.mult).then_inc(side_drained, 1)
                else:
                    m = k[1]
                    dve.wait_ge(unit_drained_act, U_GA - U_V + m + 1)
                    link(v.scalar_tensor_tensor(out=sg[:, m, :], in0=sg[:, m, :], scalar=1.0, in1=bank[:, b, :],
                                                op0=ALU.add, op1=ALU.mult))
                    v.scalar_tensor_tensor(out=mergedT[:, m, :], in0=sg[:, m, :], scalar=0.5, in1=mergedT[:, m, :],
                                           op0=ALU.mult, op1=ALU.add).then_inc(side_drained, 1)

            ADA_AT = {9: 0, 11: 1, 13: 2, 17: 3, 22: 4, 25: 5}
            for u in range(UNITS):
                a = u - U_P
                if 0 <= a < STEPS:
                    attend_max(a)
                if 1 <= u <= 8:
                    qk_gain(u - 1)
                if u < U_V:
                    qk_norm(u)
                    qk_scale(u)
                if u in (U_P + 1, U_P + 2):
                    side("g1", u - U_P - 1)
                if U_GP + 2 <= u <= U_GA + 1:
                    side("B", u - 2 - U_GP)
                if 0 <= a < STEPS:
                    attend_norm(a)
                if u in ADA_AT:
                    ada(ADA[ADA_AT[u]])
                if u == 28:
                    side("cols")
                    ada(ADA[6])
            ada(ADA[7])
            side("g2", 0)
            side("g2", 1)
            for m in range(KT):
                side("A", m)

            def residual(t, h):
                n = 2 * t + h
                dve.wait_ge(yo_done, n + 1)
                w = slice(CH * h, CH * (h + 1))
                tmp = acc[:, 0, w]
                link(v.tensor_tensor(tmp, bank[:, n % 2, :], g1b[:, w], ALU.mult))
                v.tensor_tensor(xs[:, t, w], tmp, xs[:, t, w], ALU.add).then_inc(yo_drained, 1)

            def modulate(t):
                dve.wait_ge(h2T_psum, t + 1)
                if t >= 2:
                    dve.wait_ge(logits_ready, t - 1)
                for k in range(0, KT, 2):
                    last = v.tensor_scalar(h2T[:, t % 2, k, :], bank[:, 2 + 2 * (t % 2), P * (k // 2):P * (k // 2 + 1)],
                                           ab2[:, 0, k:k + 1], ab2[:, 1, k:k + 1], ALU.mult, ALU.add)
                last.then_inc(h2T_dve, 1)

            for t in range(TT + 1):
                if t < TT:
                    residual(t, 0)
                if t >= 1:
                    modulate(t - 1)
                if t < TT:
                    residual(t, 1)
                    dve.wait_ge(x1_sq, t + 1)
                    v.tensor_scalar(st[:, 40 + t:41 + t], st[:, 8 + t:9 + t], 1.0 / D, EPS, ALU.mult,
                                    ALU.add).then_inc(x1_var, 1)
                    dve.wait_ge(x1_rstd, t + 1)
                    v.tensor_scalar(xn2[:, t, :], xs[:, t, :], st[:, 44 + t:45 + t], None,
                                    ALU.mult).then_inc(xn2_ready, 1)

            dve.wait_ge(logits_ready, TT)
            dve.wait_ge(iotas_ready, 1)
            bc = lambda ap, shape, d: ap.unsqueeze(d).broadcast_to(shape)
            S4, S32 = [P, TT, NG], [P, TT, E]
            link(v.tensor_copy(lg, bank[:, 6, 0:TT * 36].rearrange("p (t n) -> p t n", t=TT)))
            gl, el = lg[:, :, 0:NG], lg[:, :, NG:NG + E]

            def first_max(vals, best, n, it, shape, eq, score, oh):
                link(v.tensor_reduce(best, vals, AX.X, ALU.max))
                link(v.tensor_tensor(eq, vals, bc(best, shape, 2), ALU.is_equal))
                link(v.tensor_tensor(eq, eq, it.unsqueeze(1).broadcast_to(shape), ALU.mult))
                link(v.tensor_reduce(score, eq, AX.X, ALU.max))
                link(v.tensor_tensor(oh, eq, bc(score, shape, 2), ALU.is_equal))

            first_max(gl, gbest, NG, iota_g, S4, geq, gscore, goh)
            v.tensor_tensor(gdif, gl, bc(gbest, S4, 2), ALU.subtract).then_inc(exp_in, 1)
            link(v.tensor_scalar(gpen, goh, -1.0, -NEG, ALU.add, ALU.mult))
            for t in range(TT):
                last = v.tensor_tensor(em[:, t, :].rearrange("p (g e) -> p g e", g=NG),
                                       el[:, t, :].rearrange("p (g e) -> p g e", g=NG),
                                       bc(gpen[:, t, :], [P, NG, EPG], 2), ALU.add)
            link(last)
            first_max(em, best1, E, iota_e, S32, eq1, score1, oh1)
            link(v.scalar_tensor_tensor(out=em.rearrange("p t e -> p (t e)"), in0=oh1.rearrange("p t e -> p (t e)"),
                                        scalar=10 * NEG, in1=em.rearrange("p t e -> p (t e)"),
                                        op0=ALU.mult, op1=ALU.add))
            first_max(em, best2, E, iota_e, S32, eq1, score1, oh2)
            v.tensor_tensor(maskm, oh1, oh2, ALU.add).then_inc(mask_ready, 1)
            v.tensor_tensor(edif, best2, best1, ALU.subtract).then_inc(exp_in, 1)
            v.tensor_copy(oh2b, oh2)
            link(v.tensor_tensor(maskf, oh1, oh2, ALU.add))
            dve.wait_ge(rank_ready, 1)
            link(v.tensor_copy(cnt, bank[:, 7, 128:160]))
            link(v.tensor_copy(rk.rearrange("p t e -> p (t e)"), bank[:, 7, 0:TT * E]))
            link(v.scalar_tensor_tensor(out=rm.rearrange("p t e -> p (t e)"), in0=rk.rearrange("p t e -> p (t e)"),
                                        scalar=1.0, in1=maskf.rearrange("p t e -> p (t e)"),
                                        op0=ALU.add, op1=ALU.mult))
            for t in range(TT):
                dve.wait_ge(xn2_stored[t], 16)

            def one_hot(g, ts):
                qs = IDX_GROUPS[g]
                es, n = slice(2 * qs[0], 2 * qs[-1] + 2), 2 * len(qs)
                for t in ts:
                    last = v.tensor_tensor(place[g][t], bc(rm[:, t, es], [P, n, SLOTS], 2),
                                           iota_s.unsqueeze(1).broadcast_to([P, n, SLOTS]), ALU.is_equal)
                if t == TT - 1:
                    last.then_inc(place_ready, 1)

            def indices(g):
                a, b = IDX_GROUPS[g][0], IDX_GROUPS[g][-1] + 1
                dve.wait_ge(idx_psum, g + 1)
                link(v.tensor_copy(slotv[:, a:b, :], idx_bank(g)[:, 4 * a:4 * b].rearrange("p (q c) -> p q c", c=4)))
                dst, tmp = tokg[:, a:b], tok1[:, a:b]
                link(v.tensor_tensor(tmp, slotv[:, a:b, 0], slotv[:, a:b, 1], ALU.add))
                link(v.tensor_scalar(dst, tmp, 0.0, float(OUT_OF_BOUNDS), ALU.is_equal, ALU.mult))
                link(v.scalar_tensor_tensor(out=dst, in0=dst, scalar=-1.0, in1=tmp, op0=ALU.add, op1=ALU.add))
                v.tensor_copy(gidx[:, a:b], tokg[:, a:b]).then_inc(idx_ready, 1)
                for x in range(2):
                    r = slice(SLOTS * x, SLOTS * (x + 1))
                    last = v.scalar_tensor_tensor(out=sidx[r, a:b], in0=tokg[r, a:b], scalar=2.0,
                                                  in1=slotv[r, a:b, 2 + x], op0=ALU.mult, op1=ALU.add)
                last.then_inc(sidx_ready, 1)

            one_hot(0, range(TT))
            indices(0)
            one_hot(1, range(0, 2))

            def modulate_gathered(n, turn):
                q = n + turn * (RING // 2)
                dve.wait_ge(xt_ready, q + 1)
                if reached(n, turn, 1):
                    dve.wait_ge(ab_done, q * 2)
                for k in range(KT // 2):
                    last = v.tensor_scalar(xgT[:, k, :], bank[:, k // 4, P * (k % 4):P * (k % 4 + 1)],
                                           ab2[:, 0, k:k + 1], ab2[:, 1, k:k + 1], ALU.mult, ALU.add)
                last.then_inc(xgT_ready, 1)

            def hidden(n, turn):
                e, b = n + turn * RING, n % 2
                dve.wait_ge(th_ready, e + 1)
                if reached(n, turn, 2):
                    dve.wait_ge(y_done, n // 2 + turn * (RING // 2))
                v.scalar_tensor_tensor(out=sl[:, b].rearrange("p f s -> p (f s)"),
                                       in0=th[:, b].rearrange("p f s -> p (f s)"), scalar=1.0,
                                       in1=bank[:, 4 + b, 0:FT * SLOTS], op0=ALU.add,
                                       op1=ALU.mult).then_inc(silu_ready, 1)
                dve.wait_ge(silu_ready, e + 1)
                v.scalar_tensor_tensor(out=hid[:, b].rearrange("p f s -> p (f s)"),
                                       in0=sl[:, b].rearrange("p f s -> p (f s)"), scalar=0.5,
                                       in1=bank[:, 4 + b, FT * SLOTS:2 * FT * SLOTS], op0=ALU.mult,
                                       op1=ALU.mult).then_inc(hid_ready, 1)

            def drain_y(n, turn):
                q = n + turn * (RING // 2)
                dve.wait_ge(y_done, q + 1)
                if reached(n, turn, 3):
                    dve.wait_ge(y_stored[n % 3], turn * 16 + 16 * (n // 3))
                for h in range(2):
                    w = slice(CH * h, CH * (h + 1))
                    last = v.tensor_tensor(ysb[n % 3][:, w], bank[:, 6 + h, :], g2b[:, w], ALU.mult)
                last.then_inc(y_drained, 1)

            def step(n, turn):
                if n % 2 == 0 and reached(n, turn, 2):
                    drain_y(n // 2 - 1, turn)
                if n % 2 and n < E - 1:
                    modulate_gathered((n + 1) // 2, turn)
                hidden(n, turn)

            modulate_gathered(0, 0)
            one_hot(1, range(2, TT))
            indices(1)
            dve.wait_ge(exp_out, 1)
            link(v.tensor_reduce(gsum, gexp, AX.X, ALU.add))
            link(v.reciprocal(gsum, gsum))
            dve.wait_ge(exp_out, 2)
            link(v.tensor_scalar(best1, edif, 1.0, None, ALU.add))
            link(v.reciprocal(best1, best1))
            link(v.tensor_tensor(cw[:, 0, :], best1, gsum, ALU.mult))
            link(v.tensor_tensor(cw[:, 1, :], cw[:, 0, :], edif, ALU.mult))

            def overflow_counts():
                link(v.tensor_scalar(nx[0], cnt, float(SLOTS), None, ALU.is_gt))
                for m in range(2, T // SLOTS):
                    link(v.scalar_tensor_tensor(out=nx[0], in0=cnt, scalar=float(SLOTS * m), in1=nx[0],
                                                op0=ALU.is_gt, op1=ALU.add))
                link(v.tensor_copy(nx[1], nx[0]))
                cur, s = 1, 1
                while s < E:
                    nxt = 3 - cur
                    v.tensor_copy(nx[nxt][:, 0:s], nx[cur][:, 0:s])
                    link(v.tensor_tensor(nx[nxt][:, s:E], nx[cur][:, s:E], nx[cur][:, 0:E - s], ALU.add))
                    cur, s = nxt, 2 * s
                incl = nx[cur]
                for h in range(2):
                    half = incl[:, E // 2 * h:E // 2 * (h + 1)]
                    S = [P, E // 2, MAXB]
                    link(v.tensor_tensor(xcmp, bc(half, S, 2), iota_b.unsqueeze(1).broadcast_to(S), ALU.is_le))
                    link(v.tensor_reduce(xsum[:, h, :], xcmp.rearrange("p e b -> p b e"), AX.X, ALU.add))
                link(v.tensor_tensor(xsum[:, 0, :], xsum[:, 0, :], xsum[:, 1, :], ALU.add))
                link(v.tensor_scalar(xsum[:, 0, :], xsum[:, 0, :], float(E - 1), None, ALU.min))
                v.tensor_copy(xtab[:, 0:MAXB], xsum[:, 0, :])
                link(v.tensor_copy(xtab[:, MAXB:MAXB + 1], incl[:, E - 1:E]))
                v.tensor_scalar(xbase[:, :], cnt[:, 0:1], 0.0, float(E * SLOTS - 1), ALU.mult,
                                ALU.add).then_inc(xtab_ready, 1)
                dve.wait_ge(xtab_ready, 1)
                link(v.tensor_tensor(cnt, incl, nx[0], ALU.subtract))
                link(v.tensor_scalar(cnt, cnt, float(SLOTS), float((E - 1) * SLOTS), ALU.mult, ALU.add))
                link(v.tensor_scalar(nx[cur], iota_e, -float(SLOTS), float(E * SLOTS), ALU.mult, ALU.add))
                e64 = nx[cur]
                link(v.tensor_tensor(cnt, cnt, e64, ALU.subtract))
                link(v.tensor_scalar(xem, rk, float(SLOTS), None, ALU.is_ge))
                link(v.tensor_tensor(xem, xem, cnt.unsqueeze(1).broadcast_to(S32), ALU.mult))
                link(v.tensor_tensor(rk, rk, e64.unsqueeze(1).broadcast_to(S32), ALU.add))
                link(v.tensor_tensor(rk, rk, xem, ALU.add))
                for j, oh in enumerate((oh1, oh2)):
                    link(v.tensor_tensor(xem, rk, oh, ALU.mult))
                    link(v.tensor_reduce(posf[:, j, :], xem, AX.X, ALU.add))

            all_experts(dve, step, overflow_counts)
            drain_y(PAIRS - 1, 0)

            def overflow(b):
                v.tensor_scalar(xrel[:, :], posf.rearrange("p j t -> p (j t)"), xbase[:, :], None,
                                ALU.subtract).then_inc(x_rel, 1)
                dve.wait_ge(x_rel, b + 1)
                v.tensor_tensor(xplace, bc(xrel[:, :], [P, 2 * TT, SLOTS], 2),
                                iota_s.unsqueeze(1).broadcast_to([P, 2 * TT, SLOTS]), ALU.is_equal).then_inc(x_place, 1)
                v.tensor_scalar(xbase[:, :], xbase[:, :], float(SLOTS), None, ALU.add).then_inc(x_base, 1)
                dve.wait_ge(x_base, b + 1)
                dve.wait_ge(x_idx_psum, b + 1)
                r = slice(0, SLOTS)
                v.tensor_copy(xv[r, 0:3], bank[r, 0, 0:3]).then_inc(x_steps, 1)
                dve.wait_ge(x_steps, 6 * b + 1)
                v.tensor_tensor(xv[r, 3:4], xv[r, 0:1], xv[r, 1:2], ALU.add).then_inc(x_steps, 1)
                dve.wait_ge(x_steps, 6 * b + 2)
                v.tensor_scalar(xv[r, 4:5], xv[r, 3:4], 0.0, float(OUT_OF_BOUNDS), ALU.is_equal,
                                ALU.mult).then_inc(x_steps, 1)
                dve.wait_ge(x_steps, 6 * b + 3)
                v.scalar_tensor_tensor(out=xv[r, 5:6], in0=xv[r, 4:5], scalar=-1.0, in1=xv[r, 3:4], op0=ALU.add,
                                       op1=ALU.add).then_inc(x_steps, 1)
                dve.wait_ge(x_steps, 6 * b + 4)
                v.tensor_copy(gidxx[r, :], xv[r, 5:6]).then_inc(x_steps, 1)
                v.scalar_tensor_tensor(out=sidxx[r, :], in0=xv[r, 5:6], scalar=2.0, in1=xv[r, 2:3], op0=ALU.mult,
                                       op1=ALU.add).then_inc(x_steps, 1)
                dve.wait_ge(x_steps, 6 * b + 6)
                v.tensor_copy(xv[r, 6:7], xv[r, 5:6]).then_inc(x_idx, 1)
                dve.wait_ge(x_rowsT, b + 1)
                for k in range(KT):
                    last = v.tensor_scalar(xgT[:, k, 0:SLOTS], bank[:, k // 4, P * (k % 4):P * (k % 4) + SLOTS],
                                           ab2[:, 0, k:k + 1], ab2[:, 1, k:k + 1], ALU.mult, ALU.add)
                last.then_inc(x_in, 1)
                dve.wait_ge(x_th, b + 1)
                v.scalar_tensor_tensor(out=sl[:, 0].rearrange("p f s -> p (f s)"),
                                       in0=th[:, 0].rearrange("p f s -> p (f s)"), scalar=1.0,
                                       in1=bank[:, 4, 0:FT * SLOTS], op0=ALU.add, op1=ALU.mult).then_inc(x_silu, 1)
                dve.wait_ge(x_silu, b + 1)
                v.scalar_tensor_tensor(out=hid[:, 0].rearrange("p f s -> p (f s)"),
                                       in0=sl[:, 0].rearrange("p f s -> p (f s)"), scalar=0.5,
                                       in1=bank[:, 4, FT * SLOTS:2 * FT * SLOTS], op0=ALU.mult,
                                       op1=ALU.mult).then_inc(x_hid, 1)
                dve.wait_ge(x_y, b + 1)
                for h in range(2):
                    w = slice(CH * h, CH * (h + 1))
                    last = v.tensor_tensor(ysb[0][r, w], bank[r, 6 + h, :], g2b[r, w], ALU.mult)
                last.then_inc(x_y_drained, 1)
                dve.wait_ge(x_stored, 16 * b + 16)

            dve.wait_ge(y_stored[0], 16 * len(range(0, PAIRS, 3)))
            overflow_blocks(dve, overflow)

            for t in range(TT):
                dve.wait_ge(yg_loaded[t], 16)
                for j in range(2):
                    last = v.scalar_tensor_tensor(out=xs[:, t, :], in0=yg[:, t, j, :], scalar=cw[:, j, t:t + 1],
                                                  in1=xs[:, t, :], op0=ALU.mult, op1=ALU.add)
                    if j == 0:
                        link(last)
                last.then_inc(out_ready, 1)

        @block.gpsimd
        def _(pool):
            g = nc.gpsimd
            count = [0]

            def link(ins):
                count[0] += 1
                ins.then_inc(pool_link, 1)
                pool.wait_ge(pool_link, count[0])

            def fill_diagonal(tile, base, n):
                link(g.affine_select(out=tile, in_=tile, compare_op=ALU.not_equal, fill=1.0, base=base,
                                     pattern=[[-1, n]], channel_multiplier=1))

            link(g.memset(ident[:, :], 0.0))
            fill_diagonal(ident[:, :], 0, P)
            link(g.tensor_copy(identb[:, :], ident[:, :]))
            link(g.memset(fold[:, :], 0.0))
            fill_diagonal(fold[:, :], 0, SLOTS)
            fill_diagonal(fold[:, :], -SLOTS, SLOTS)
            g.memset(ones[:, :], 1.0)
            link(g.memset(onesb[:, :], 1.0))
            link(g.memset(maskb[:, :], 0.0))
            g.affine_select(out=maskb[:, :], in_=maskb[:, :], compare_op=ALU.is_ge, fill=NEG, base=0,
                            pattern=[[-1, P]], channel_multiplier=1)
            g.affine_select(out=lowb[:, :], in_=onesb[:, :], compare_op=ALU.is_gt, fill=0.0, base=0,
                            pattern=[[1, P]], channel_multiplier=-1)
            for j in range(16):
                g.memset(recip[:, j:j + 1], 1.0 / (j + 1))
            for t in range(TT):
                g.iota(tokc[:, t, 0:1], pattern=[[0, 1]], base=1, channel_multiplier=1,
                       allow_small_or_imprecise_dtypes=True)
                g.iota(tokc[:, t, 1:2], pattern=[[0, 1]], base=P * t, channel_multiplier=0,
                       allow_small_or_imprecise_dtypes=True)
            kw = dict(allow_small_or_imprecise_dtypes=True, channel_multiplier=0)
            g.iota(iota_g, pattern=[[-1, NG]], base=NG, **kw)
            g.iota(iota_e, pattern=[[-1, E]], base=E, **kw)
            g.iota(iota_b, pattern=[[1, MAXB]], base=0, **kw)
            g.iota(iota_s, pattern=[[1, SLOTS]], base=1, **kw).then_inc(iotas_ready, 1)
            link(g.memset(nhalf[:, :], -0.5))
            g.memset(gidxx[:, :], 2 * OUT_OF_BOUNDS)
            g.memset(sidxx[:, :], 2 * OUT_OF_BOUNDS).then_inc(consts_ready, 1)
            pool.wait_ge(x_var, 1)
            g.tensor_tensor(st[:, 12:16], st[:, 4:8], nhalf[:, 0:4], ALU.pow).then_inc(x_rstd, 1)
            pool.wait_ge(slot_loaded[0], 32)
            pool.dma_start(cols[:, PS, :], pool_scale.rearrange("b (m p) -> (b p) m", p=P),
                           allow_slow_non_contiguous=True).then_inc(late_loaded, 16)
            pool.dma_start(pw, w_pool.rearrange("l g c n -> (l c) g n")).then_inc(late_loaded, 16)
            pool.dma_start(wr[:, :, 0:NG], w_router_g.rearrange("l (p k) n -> (l p) k n", k=KT)).then_inc(late_loaded, 16)
            pool.dma_start(wr[:, :, NG:NG + E], w_router_e.rearrange("l (p k) n -> (l p) k n", k=KT)).then_inc(late_loaded, 16)
            pool.dma_start(br[:, 0:NG], b_router_g).then_inc(late_loaded, 16)
            pool.dma_start(br[:, NG:NG + E], b_router_e).then_inc(late_loaded, 16)
            for u in range(U_V):
                pool.wait_ge(qk_var, u + 1)
                if u >= 2:
                    pool.wait_ge(unit_drained_dve, u - 1)
                g.tensor_tensor(ss[:, u % 2, 1, :], ss[:, u % 2, 0, :], nhalf[:, :], ALU.pow).then_inc(qk_rstd, 1)

            for gi, w in enumerate(WINDOWS):
                pool.wait_ge(unit_drained_act, U_P - U_V + gi + 1)
                src, s, b = pT[:, gi, :], 1, 0
                while s < w:
                    dst = ptmp[b]
                    g.tensor_copy(dst[:, 0:s], src[:, 0:s])
                    link(g.tensor_tensor(dst[:, s:T], src[:, s:T], src[:, 0:T - s], ALU.add))
                    src, s, b = dst, 2 * s, 1 - b
                g.tensor_tensor(src[:, 0:w - 1], src[:, 0:w - 1], recip[:, 0:w - 1], ALU.mult)
                link(g.tensor_scalar(src[:, w - 1:T], src[:, w - 1:T], 1.0 / w, None, ALU.mult))
                g.tensor_tensor(pT[:, gi, :], src, pT[:, gi, :], ALU.subtract).then_inc(pooled, 1)
                pool.wait_ge(pooled, gi + 1)

            for t in range(TT):
                pool.wait_ge(x1_var, t + 1)
                g.tensor_tensor(st[:, 44 + t:45 + t], st[:, 40 + t:41 + t], nhalf[:, 0:1],
                                ALU.pow).then_inc(x1_rstd, 1)

            def gather(dst, ix, done):
                pool.indirect_dma_start(out=dst, out_offset=None, in_=xn2_d,
                                        in_offset=bass.IndirectOffsetOnAxis(ap=ix, axis=0),
                                        bounds_check=T - 1, oob_is_err=False).then_inc(done, 16)

            def scatter(src, ix, done):
                pool.indirect_dma_start(out=y_d, out_offset=bass.IndirectOffsetOnAxis(ap=ix, axis=0), in_=src,
                                        in_offset=None, bounds_check=2 * T - 1, oob_is_err=False).then_inc(done, 16)

            for t in range(TT):
                pool.wait_ge(xn2_stored[t], 16)
            for q in range(PAIRS + 5):
                if q >= 5:
                    if q == 5:
                        pool.wait_ge(sidx_ready, len(IDX_GROUPS))
                    pool.wait_ge(y_drained, q - 4)
                    scatter(ysb[(q - 5) % 3], sidx[:, q - 5:q - 4], y_stored[(q - 5) % 3])
                if q < PAIRS:
                    for g_, qs in enumerate(IDX_GROUPS):
                        if q == qs[0]:
                            pool.wait_ge(idx_ready, g_ + 1)
                    if q >= 3:
                        pool.wait_ge(xt_ready, q - 2)
                    gather(xg[:, q % 3, :], gidx[:, q:q + 1], xg_loaded[q % 3])

            def overflow(b):
                pool.wait_ge(x_idx, b + 1)
                pool.sem_inc(x_turns, 1)
                gather(xg[:, 0, :], gidxx[:, :], x_rows)
                pool.wait_ge(x_y_drained, b + 1)
                pool.sem_inc(x_turns, 1)
                scatter(ysb[0], sidxx[:, :], x_stored)
                pool.wait_ge(x_stored, 16 * b + 16)
                pool.sem_inc(x_turns, 1)

            overflow_blocks(pool, overflow)
            pool.sem_inc(overflow_done, 1)


_INS = ['x', 'c', 'w_ada', 'b_ada', 'norm1', 'w_in', 'q_norm', 'k_norm', 'w_attn_up', 'w_pool', 'pool_scale',
        'w_out', 'norm2', 'w_router_g', 'b_router_g', 'w_router_e', 'b_router_e', 'w1', 'w3', 'w2']


def kernel(**inputs):
    import numpy as _np
    import concourse.bacc as _bacc
    from concourse import mybir as _mybir
    from concourse.bass_utils import run_bass_kernel_spmd as _run

    nc = _bacc.Bacc("TRN2", target_bir_lowering=False, num_devices=1)
    arrays, args = {}, []
    for name in _INS:
        a = _np.ascontiguousarray(inputs[name])
        arrays[f"in_{name}_dram"] = a
        args.append(nc.dram_tensor(f"in_{name}_dram", a.shape, _mybir.dt.from_np(a.dtype), kind="ExternalInput").ap())
    args.append(nc.dram_tensor("out_0_dram", (1, T, D), F32, kind="ExternalOutput").ap())
    hybrid_trunk(nc, *args)
    r = _run(nc, [arrays], core_ids=[0])
    return r.results[0]["out_0_dram"]
```

```python
from contextlib import ExitStack

import concourse.bass as bass
from concourse import mybir

F32 = mybir.dt.float32
F32R = mybir.dt.float32r
BF16 = mybir.dt.bfloat16
I32 = mybir.dt.int32
ALU = mybir.AluOpType
ACT = mybir.ActivationFunctionType
AX = mybir.AxisListType

P = 128
T, D = 512, 1024
TT, KT = T // P, D // P
HEADS, HD = 8, 64
AW = HEADS * HD
HP = AW // P
PW = D // 2
WINDOWS = (2, 4, 8, 16)
NG, EPG = 4, 8
E = NG * EPG
F = 256
FT = F // P
SLOTS = 64
PAIRS = E // 2
MAXB = 2 * T // SLOTS
EPS = 1e-6
NEG = -1e30
CH = 512
RING = 6
HEAD = E % RING
TURNS = E // RING
OUT_OF_BOUNDS = 4096


def hybrid_trunk(nc, x, c, w_ada, b_ada, norm1, w_in, q_norm, k_norm, w_attn_up, w_pool, pool_scale, w_out,
                 norm2, w_router_g, b_router_g, w_router_e, b_router_e, w1, w3, w2, out):
    x_v = x.rearrange("b (t p) d -> (b t) p d", p=P)
    out_v = out.rearrange("b (t p) d -> (b t) p d", p=P)
    ada_v = w_ada.rearrange("l (p k) n -> (l p) k n", k=KT)
    bada_v = b_ada.rearrange("l (j p k) -> (l p) j k", k=KT, p=P)
    win_v = w_in.rearrange("l (p k) n -> (l p) k n", k=KT)
    wup_v = w_attn_up.rearrange("l (k p) n -> (l p) k n", p=P)
    wout_v = w_out.rearrange("l (k p) n -> (l p) k n", p=P)
    w1_v = w1.rearrange("l g e (p k) f -> (l g e) p (k f)", k=KT)
    w3_v = w3.rearrange("l g e (p k) f -> (l g e) p (k f)", k=KT)
    w2_v = w2.rearrange("l g e (p k) n -> (l g e) p (k n)", k=FT)

    xn2_d = nc.dram_tensor("xn2_scratch", (T, D), F32).ap()
    y_d = nc.dram_tensor("y_scratch", (2 * T, D), F32).ap()

    ctx = ExitStack()
    with ctx:
        def sb(name, shape, dt=F32):
            return ctx.enter_context(nc.sbuf_tensor(name, shape, dt))

        def sem(name):
            return ctx.enter_context(nc.semaphore(name))

        bank = ctx.enter_context(nc.psum_tensor("bank", [P, 8, CH], F32))

        xs = sb("xs", [P, TT, D])
        hT_at = nc.sbuf_base
        hT = sb("hT", [P, KT, T])
        late_at = nc.sbuf_base
        late = sb("late", [P, 2 * 6144])
        g1b = sb("g1b", [P, D])
        g2b = sb("g2b", [P, D])
        arena_at = nc.sbuf_base
        arena = sb("arena", [P, 4 * 6144])
        ROUTE = 3 * TT * E + 4 * E + 2 * TT
        route = sb("route", [P, ROUTE])
        acc = sb("acc", [P, 2, D])
        probs = sb("probs", [P, 2, 2, CH])
        ident = sb("ident", [P, P])
        ones = sb("ones", [P, P])
        identb = sb("identb", [P, P], BF16)
        maskb = sb("maskb", [P, P], BF16)
        lowb = sb("lowb", [P, P], BF16)
        onesb = sb("onesb", [P, P], BF16)
        fold = sb("fold", [P, SLOTS])
        wr = sb("wr", [P, KT, NG + E])
        br = sb("br", [1, NG + E])
        cols = sb("cols", [P, 12, KT])
        ab1 = sb("ab1", [P, 2, KT])
        ab2 = sb("ab2", [P, 2, KT])
        xrel = sb("xrel", [P, 2 * TT])
        xv = sb("xv", [P, 8])
        cth = cols[:, 10, :]
        recip = sb("recip", [P, 16])
        qkg = sb("qkg", [P, 2])
        st = sb("st", [P, 64])
        ss = sb("ss", [P, 2, 2, 8])
        nhalf = sb("nhalf", [P, 8])
        tokc = sb("tokc", [P, TT, 2], BF16)
        gidx = sb("gidx", [P, PAIRS], I32)
        sidx = sb("sidx", [P, PAIRS], I32)
        slotv = sb("slotv", [P, PAIRS, 4])
        iotas = sb("iotas", [P, 128])
        xtab = sb("xtab", [P, MAXB + 1], I32)
        cw = sb("cw", [P, 2, TT])
        xbase = sb("xbase", [P, 1])
        gidxx = sb("gidxx", [P, 1], I32)
        sidxx = sb("sidxx", [P, 1], I32)

        hL = nc.alloc_sbuf_tensor_at("hT_low", [P, KT, T], F32R, offset=hT_at)
        hH = nc.alloc_sbuf_tensor_at("hT_high", [P, KT, T], F32R, offset=arena_at + 4 * 4096)
        wHL = nc.alloc_sbuf_tensor_at("w_in_parts", [P, 2, 2, KT, P], F32R, offset=late_at + 4 * 4096)
        wH, wL = wHL[:, 0], wHL[:, 1]
        cH = nc.alloc_sbuf_tensor_at("w_in_chunk_high", [P, KT, CH], F32R, offset=late_at + 4 * 8192)
        cL = nc.alloc_sbuf_tensor_at("w_in_chunk_low", [P, KT, CH], F32R, offset=arena_at + 4 * 14336)
        mH = nc.alloc_sbuf_tensor_at("merged_high", [P, KT, T], F32R, offset=arena_at + 4 * 12288)
        mL = nc.alloc_sbuf_tensor_at("merged_low", [P, KT, T], F32R, offset=late_at + 4 * 8192)
        oL = nc.alloc_sbuf_tensor_at("w_out_low", [P, 2, KT, CH], F32R, offset=late_at)
        oH0 = nc.alloc_sbuf_tensor_at("w_out_high_0", [P, KT, CH], F32R, offset=arena_at + 4 * 8192)
        oH1a = nc.alloc_sbuf_tensor_at("w_out_high_1a", [P, KT // 2, CH], F32R, offset=arena_at + 4 * 6144)
        oH1b = nc.alloc_sbuf_tensor_at("w_out_high_1b", [P, KT // 2, CH], F32R, offset=arena_at + 4 * 16384)

        def w_out_high(h, k):
            if h == 0:
                return oH0[:, k, :]
            return oH1a[:, k, :] if k < KT // 2 else oH1b[:, k - KT // 2, :]

        def carve(base, start, *shape):
            n = 1
            for s in shape:
                n *= s
            v = base[:, start:start + n]
            names = "abcd"[:len(shape)]
            if len(shape) == 1:
                return v
            return v.rearrange(f"p ({' '.join(names)}) -> p {' '.join(names)}", **dict(zip(names[1:], shape[1:])))

        AR = arena[:, :]
        OU = late[:, 0:8192]
        MG = late[:, 8192:12288]
        mergedT = MG.rearrange("p (k t) -> p k t", k=KT)
        slot = [carve(AR, 0, 4096), OU[:, 0:4096], OU[:, 4096:8192], carve(AR, 4096, 4096),
                carve(AR, 18432, 4096)]
        qT = carve(AR, 8192, HP, T)
        kT = carve(AR, 10240, HP, T)
        vt = carve(AR, 12288, TT, AW)
        pT = carve(AR, 14336, 4, T)
        attnT = carve(AR, 16384, HP, T)
        sg = carve(AR, 18432, KT, T)
        qn = carve(AR, 22528, 2, AW)
        PT = carve(AR, 22528, 2, 2, TT, P)
        pw = sg[:, 2:4, :].rearrange("p a (b n) -> p (a b) n", b=2)
        ptmp = [sg[:, 4, :], sg[:, 5, :]]
        rows = acc[:, 0, 0:CH]
        sqbuf = probs[:, 0, 0, :]
        xn = MG.rearrange("p (t d) -> p t d", t=TT)
        xn2 = hT[:, :, :].rearrange("p a b -> p (a b)").rearrange("p (t d) -> p t d", t=TT)
        h2T = probs[:, :, :, :].rearrange("p a b c -> p (a b c)").rearrange("p (u k t) -> p u k t", u=2, k=KT)
        IDX_GROUPS = [range(0, 2), range(2, PAIRS)]
        idx_bank = lambda g: bank[:, (2, 7)[g], :]
        HT = hT[:, :, :].rearrange("p a b -> p (a b)")
        PR = probs[:, :, :, :].rearrange("p a b c -> p (a b c)")
        xg = carve(HT, 0, 3, D)
        xgT = carve(HT, 3072, KT, P)
        place = []
        for qs, starts in zip(IDX_GROUPS, ([HT[:, 3072 + 128 * t:] for t in range(TT)],
                                           [PR[:, 1024:], HT[:, 2048:], late[:, 10240:], late[:, 11264:]])):
            e_ = 2 * len(qs)
            place.append([b[:, 0:e_ * SLOTS // 2].bitcast(BF16).rearrange("p (e s) -> p e s", e=e_) for b in starts])
        absb = carve(PR, 0, 2, CH)
        th = carve(g1b[:, :], 0, 2, FT, SLOTS)
        sl = carve(g1b[:, :], 256, 2, FT, SLOTS)
        hid = carve(g1b[:, :], 512, 2, FT, SLOTS)
        iota_s = iotas[:, 0:SLOTS]
        iota_e = iotas[:, 64:64 + E]
        iota_g = iotas[:, 96:96 + NG]
        iota_b = iotas[:, 100:100 + MAXB]
        ring = [AR[:, 6144 * s:6144 * (s + 1)] for s in range(4)] + [late[:, 0:6144], late[:, 6144:12288]]
        w13 = [carve(r, 2048 if s == 1 else 0, 2, KT, F) for s, r in enumerate(ring)]
        w2s = [carve(r, 0 if s == 1 else 4096, FT, D) for s, r in enumerate(ring)]
        yg = carve(AR, 0, TT, 2, D)
        RT = acc[:, :, :].rearrange("p a b -> p (a b)")

        def worker(base, size):
            used = [0]

            def take(*shape):
                n = 1
                for k in shape:
                    n *= k
                used[0] += n
                assert used[0] <= size
                return carve(base, used[0] - n, *shape)
            return take

        work = worker(RT, 2 * D)
        lg = work(TT, NG + E)
        geq, goh, gdif, gexp, gpen = (work(TT, NG) for _ in range(5))
        gbest, gscore, gsum, best1, best2, score1, edif = (work(TT) for _ in range(7))
        em, eq1, maskf, rm = (work(TT, E) for _ in range(4))
        maskm, oh2b = (work(TT * E // 2).bitcast(BF16).rearrange("p (t e) -> p t e", t=TT) for _ in range(2))
        tok1, tokg = (work(PAIRS) for _ in range(2))
        work = worker(route[:, :], ROUTE)
        oh1, oh2, rk = (work(TT, E) for _ in range(3))
        cnt = work(E)
        nx = [work(E) for _ in range(3)]
        xsum = st[:, 0:2 * MAXB].rearrange("p (h b) -> p h b", h=2)
        posf = work(2, TT)
        xcmp = carve(g1b[:, :], 768, E // 2, MAXB)
        xem = wr[:, :, :].rearrange("p k n -> p (k n)")[:, 0:TT * E].rearrange("p (t e) -> p t e", t=TT)
        ysb = [carve(PR, 1024, D), carve(RT, 0, D), carve(RT, D, D)]

        CHUNKS = [("ada", 1, 0), ("ada", 1, 1), ("ada", 0, 0), ("ada", 0, 1), ("in", 0), ("in", 1), ("ada", 2, 0),
                  ("ada", 2, 1), ("ada", 3, 0), ("ada", 3, 1), ("in", 2), ("ada", 4, 0), ("ada", 4, 1),
                  ("ada", 5, 0), ("ada", 5, 1), ("in", 3), ("in", 6), ("in", 7), ("in", 4), ("in", 5), ("up",),
                  ("out", 0), ("out", 1)]
        SLOT = [0, 1, 2, 3, 0, 1, 2, 4, 2, 4, 0, 2, 4, 2, 4, 1, 0, 1, 0, 1, 0, 1, 2]
        at = {k: n for n, k in enumerate(CHUNKS)}
        ADA_NOW = CHUNKS[:4]
        ADA = [k for k in CHUNKS[4:] if k[0] == "ada"]
        IN = [k for k in CHUNKS if k[0] == "in"]
        UNITS = 4 * len(IN)
        U_K, U_V, U_P, U_GP, U_GA = 4, 8, 12, 16, 24

        def slot_of(k):
            return SLOT[at[k]]

        def turn_of(k):
            return SLOT[:at[k] + 1].count(slot_of(k))

        STEPS = HP * TT

        slot_loaded = [sem(f"slot_loaded{i}") for i in range(5)]
        x_loaded = [sem(f"x_loaded{i}") for i in range(TT)]
        c_loaded = sem("c_loaded")
        c_silu = sem("c_silu")
        small_loaded = sem("small_loaded")
        late_loaded = sem("late_loaded")
        cact_ready = sem("cact_ready")
        silu_ready = sem("silu_ready")
        sidx_ready = sem("sidx_ready")
        g_bias_loaded = sem("g_bias_loaded")
        consts_ready = sem("consts_ready")
        pool_link = sem("pool_link")
        chain = sem("chain")
        x_sq = sem("x_sq")
        x_var = sem("x_var")
        x_rstd = sem("x_rstd")
        xn_ready = sem("xn_ready")
        xT_ready = sem("xT_ready")
        hT_dve = sem("hT_dve")
        hT_act = sem("hT_act")
        ada_used = sem("ada_used")
        ada_rows_done = sem("ada_rows_done")
        ada_rows_out = sem("ada_rows_out")
        ada_cols_done = sem("ada_cols_done")
        ab1_ready = sem("ab1_ready")
        cH_used = sem("cH_used")
        cH_ready = sem("cH_ready")
        cL_ready = sem("cL_ready")
        hT_used = sem("hT_used")
        hH_ready = sem("hH_ready")
        hL_ready = sem("hL_ready")
        mH_ready = sem("mH_ready")
        mL_ready = sem("mL_ready")
        oH_ready = sem("oH_ready")
        oL_ready = sem("oL_ready")
        wH_ready = sem("wH_ready")
        wL_ready = sem("wL_ready")
        unit_done = sem("unit_done")
        unit_drained_dve = sem("unit_drained_dve")
        unit_drained_act = sem("unit_drained_act")
        qk_sq = sem("qk_sq")
        qk_var = sem("qk_var")
        qk_rstd = sem("qk_rstd")
        qkT_ready = sem("qkT_ready")
        qkT_drained = sem("qkT_drained")
        pooled = sem("pooled")
        scores_ready = sem("scores_ready")
        negmax_ready = sem("negmax_ready")
        probs_raw = sem("probs_raw")
        probs_ready = sem("probs_ready")
        PT_ready = sem("PT_ready")
        PT_drained = sem("PT_drained")
        attn_ready = sem("attn_ready")
        attn_drained = sem("attn_drained")
        side_done = sem("side_done")
        side_drained = sem("side_drained")
        yo_done = sem("yo_done")
        yo_drained = sem("yo_drained")
        x1_sq = sem("x1_sq")
        x1_var = sem("x1_var")
        x1_rstd = sem("x1_rstd")
        xn2_ready = sem("xn2_ready")
        xn2_stored = [sem(f"xn2_stored{i}") for i in range(TT)]
        h2T_psum = sem("h2T_psum")
        h2T_dve = sem("h2T_dve")
        h2T_act = sem("h2T_act")
        logits_ready = sem("logits_ready")
        exp_in = sem("exp_in")
        exp_out = sem("exp_out")
        mask_ready = sem("mask_ready")
        rank_ready = sem("rank_ready")
        place_ready = sem("place_ready")
        idx_psum = sem("idx_psum")
        idx_ready = sem("idx_ready")
        iotas_ready = sem("iotas_ready")
        w13_loaded = [sem(f"w13_loaded{i}") for i in range(RING)]
        w2_loaded = [sem(f"w2_loaded{i}") for i in range(RING)]
        xg_loaded = [sem(f"xg_loaded{i}") for i in range(3)]
        xt_ready = sem("xt_ready")
        xgT_ready = sem("xgT_ready")
        xgT_act = sem("xgT_act")
        ab_done = sem("ab_done")
        ab_drained = sem("ab_drained")
        st_done = sem("st_done")
        th_ready = sem("th_ready")
        hid_ready = sem("hid_ready")
        y_done = sem("y_done")
        y_drained = sem("y_drained")
        y_stored = [sem(f"y_stored{i}") for i in range(3)]
        yg_loaded = [sem(f"yg_loaded{i}") for i in range(2 * TT)]
        xtab_ready = sem("xtab_ready")
        x_loaded_w = sem("x_loaded_w")
        x_turns = sem("x_turns")
        x_rel = sem("x_rel")
        x_steps = sem("x_steps")
        x_base = sem("x_base")
        x_place = sem("x_place")
        x_idx_psum = sem("x_idx_psum")
        x_idx = sem("x_idx")
        x_rows = sem("x_rows")
        x_rowsT = sem("x_rowsT")
        x_in = sem("x_in")
        x_ab = sem("x_ab")
        x_ab_drained = sem("x_ab_drained")
        x_st = sem("x_st")
        x_th = sem("x_th")
        x_silu = sem("x_silu")
        x_hid = sem("x_hid")
        x_y = sem("x_y")
        x_y_drained = sem("x_y_drained")
        x_stored = sem("x_stored")
        overflow_done = sem("overflow_done")
        out_ready = sem("out_ready")
        out_stored = sem("out_stored")

        C_, N1, N2, PS, BA = 0, 1, 2, 3, 4
        SMALL, LATE = 7, 6

        def overflow_blocks(eng, body):
            eng.wait_ge(xtab_ready, 1)
            n = eng.value_load(xtab[0:1, MAXB:MAXB + 1], min_val=0, max_val=MAXB)
            with eng.If(n > 0):
                with eng.Fori(0, n) as b:
                    body(b)

        def all_experts(eng, step, before_last=None):
            for n in range(HEAD + RING):
                step(n, 0)
            with eng.Fori(1, TURNS - 1) as turn:
                for j in range(RING):
                    step(HEAD + j, turn)
            if before_last:
                before_last()
            for n in range(E - RING, E):
                step(n, 0)

        def reached(n, turn, m):
            return n >= m if isinstance(turn, int) else True

        xplace = MG.bitcast(BF16)[:, 0:2 * TT * SLOTS].rearrange("p (n s) -> p n s", s=SLOTS)

        block = ctx.enter_context(nc.Block())

        SIDE = ([("g1", 0), ("g1", 1), ("cols",), ("g2", 0), ("g2", 1)] + [("B", m) for m in range(KT)]
                + [("A", m) for m in range(KT)])
        side_no = {k: n for n, k in enumerate(SIDE)}
        FIRST_A = side_no[("A", 0)]

        def side_bank(n):
            return 7 if n < FIRST_A or (n - FIRST_A) % 2 == 0 else 6

        def unit_weights(u):
            w = slot[slot_of(IN[u // 4])].rearrange("p (k n) -> p k n", k=KT)
            return w[:, :, P * (u % 4):P * (u % 4 + 1)]

        def drained(eng, u):
            if u < U_V:
                eng.wait_ge(unit_drained_dve, u + 1)
            else:
                eng.wait_ge(unit_drained_act, u - U_V + 1)

        @block.sync
        def _(sp):
            sp.dma_start(cols[:, C_, :], c.rearrange("b (p k) -> (b p) k", k=KT)).then_inc(c_loaded, 16)
            for n, k in enumerate(CHUNKS):
                if n == 1:
                    for t in range(TT):
                        sp.dma_start(xs[:, t, :], x_v[t]).then_inc(x_loaded[t], 16)
                if n >= 4:
                    before = [m for m in range(n) if SLOT[m] == SLOT[n]]
                    old = CHUNKS[before[-1]] if before else None
                    if old is None:
                        pass
                    elif old[0] == "in":
                        units = 4 * (IN.index(old) + 1)
                        if units <= U_K:
                            sp.wait_ge(unit_done, units)
                        elif units <= U_P:
                            sp.wait_ge(cL_ready, KT * IN.index(old))
                        else:
                            sp.wait_ge(wL_ready, units - U_P)
                    elif old in ADA_NOW:
                        sp.wait_ge(ada_rows_done, ADA_NOW.index(old) + 1)
                    else:
                        sp.wait_ge(ada_used, ADA.index(old) + 1)
                if k == ("out", 1):
                    sp.wait_ge(unit_done, UNITS)
                if k[0] == "ada":
                    src = ada_v[:, 4 * k[2]:4 * k[2] + 4, D * k[1]:D * (k[1] + 1)]
                    dst = slot[SLOT[n]].rearrange("p (k n) -> p k n", k=4)
                elif k[0] == "in":
                    src = win_v[:, :, CH * k[1]:CH * (k[1] + 1)]
                    dst = slot[SLOT[n]].rearrange("p (k n) -> p k n", k=KT)
                elif k[0] == "up":
                    src = wup_v
                    dst = slot[SLOT[n]].rearrange("p (k n) -> p k n", k=HP)
                else:
                    src = wout_v[:, :, CH * k[1]:CH * (k[1] + 1)]
                    dst = slot[SLOT[n]].rearrange("p (k n) -> p k n", k=KT)
                sp.dma_start(dst, src).then_inc(slot_loaded[SLOT[n]], 16)
            sp.wait_ge(side_drained, len(SIDE))

            def load13(e, s):
                sp.dma_start(w13[s][:, 0].rearrange("p k f -> p (k f)"), w1_v[e]).then_inc(w13_loaded[s], 16)
                sp.dma_start(w13[s][:, 1].rearrange("p k f -> p (k f)"), w3_v[e]).then_inc(w13_loaded[s], 16)

            def load2(e, s):
                sp.dma_start(w2s[s].rearrange("p k n -> p (k n)"), w2_v[e]).then_inc(w2_loaded[s], 16)

            def load_pair(n, turn):
                e = n + turn * RING
                for j in range(2):
                    sp.wait_ge(ab_done, e + (j + 1 - RING))
                    load13(e + j, (n + j) % RING)
                sp.wait_ge(y_done, turn * (RING // 2) + (n // 2 + 1 - RING // 2))
                for j in range(2):
                    load2(e + j, (n + j) % RING)

            load13(0, 0)
            load2(0, 0)
            load13(3, 3)
            load2(3, 3)
            sp.wait_ge(yo_done, TT)
            load13(1, 1)
            load13(4, 4)
            for t in range(TT):
                if t == TT - 1:
                    sp.wait_ge(yo_done, 2 * TT)
                    load2(1, 1)
                sp.wait_ge(xn2_ready, t + 1)
                sp.dma_start(xn2_d[P * t:P * (t + 1), :], xn2[:, t, :]).then_inc(xn2_stored[t], 16)
            load13(2, 2)
            load2(2, 2)
            load2(4, 4)
            load13(5, 5)
            sp.wait_ge(ab_done, 1)
            load13(RING, 0)
            sp.wait_ge(idx_psum, 2)
            load2(5, 5)
            sp.wait_ge(ab_done, 2)
            load13(RING + 1, 1)
            sp.wait_ge(y_done, 1)
            load2(RING, 0)
            load2(RING + 1, 1)
            with sp.Fori(1, TURNS) as turn:
                for j in range(0, RING, 2):
                    load_pair(HEAD + j, turn)

            def overflow(b):
                e = sp.value_load(xtab[0:1, bass.ds(b, 1)], min_val=0, max_val=E - 1)
                for src, dst in ((w1_v, w13[0][:, 0].rearrange("p k f -> p (k f)")),
                                 (w3_v, w13[0][:, 1].rearrange("p k f -> p (k f)")),
                                 (w2_v, w2s[0].rearrange("p k n -> p (k n)"))):
                    sp.dma_start(dst, src[bass.ds(e, 1)].rearrange("o p n -> (o p) n")).then_inc(x_loaded_w, 16)
                sp.wait_ge(x_y, b + 1)
                sp.sem_inc(x_turns, 1)

            sp.wait_ge(y_done, PAIRS)
            overflow_blocks(sp, overflow)
            for i in range(3):
                sp.wait_ge(y_stored[i], 16 * len(range(i, PAIRS, 3)))
            sp.wait_ge(overflow_done, 1)
            halves = [(t, h, slice(CH * h, CH * (h + 1))) for t in range(TT) for h in range(2)]
            for n, (t, h, w) in enumerate(halves):
                sp.dma_start(yg[:, t, :, w], y_d[2 * P * t:2 * P * (t + 1), w].rearrange("(p j) d -> p j d", j=2)
                             ).then_inc(yg_loaded[n], 16)
            for n, (t, h, w) in enumerate(halves):
                sp.wait_ge(out_ready, n + 1)
                sp.dma_start(out_v[t][:, w], xs[:, t, w]).then_inc(out_stored, 16)
            sp.wait_ge(out_stored, 16 * 2 * TT)

        @block.tensor
        def _(pe):
            mm = nc.tensor.matmul

            def chunk_here(k):
                pe.wait_ge(slot_loaded[slot_of(k)], 16 * turn_of(k))

            def x_transposes(ks, t):
                for k in ks:
                    last = nc.tensor.transpose(bank[:, k, P * t:P * (t + 1)],
                                               xn[:, t, k:D:KT], ident[:, :])
                last.then_inc(xT_ready, 1)

            def unit_half(u, h):
                ch = IN[u // 4]
                w = slot[slot_of(ch)].rearrange("p (k n) -> p k n", k=KT)
                if h == 0:
                    if u >= U_P:
                        pe.wait_ge(wL_ready, u - U_P + 1)
                    elif u == 0:
                        chunk_here(ch)
                    if u >= 2:
                        drained(pe, u - 2)
                m = P * (u % 4)
                for k in range(4 * h, 4 * h + 4):
                    if u == 0:
                        pe.wait_ge(hT_act if k % 2 else hT_dve, k // 2 + 1)
                    if u == U_K:
                        pe.wait_ge(hL_ready, k + 1)
                    if u in (U_K, U_V):
                        pe.wait_ge(cL_ready, KT * (u // 4 - 1) + k + 1)
                    if u < U_K:
                        last = mm(bank[:, u % 2, :], hT[:, k, m:m + P], w[:, k, :], start=k == 0, stop=k == 7)
                        if u == U_K - 1 and k < KT - 1:
                            last.then_inc(hT_used, 1)
                    elif u < U_P:
                        mm(bank[:, u % 2, :], hH[:, k, m:m + P], cH[:, k, :], start=k == 0, stop=False)
                        mm(bank[:, u % 2, :], hH[:, k, m:m + P], cL[:, k, :], start=False, stop=False)
                        last = mm(bank[:, u % 2, :], hL[:, k, m:m + P], cH[:, k, :], start=False, stop=k == 7)
                        if u == U_V - 1 and k < KT - 1:
                            last.then_inc(cH_used, 1)
                    else:
                        b = u % 2
                        mm(bank[:, b, :], wH[:, b, k, :], hH[:, k, :], start=k == 0, stop=False)
                        mm(bank[:, b, :], wH[:, b, k, :], hL[:, k, :], start=False, stop=False)
                        last = mm(bank[:, b, :], wL[:, b, k, :], hH[:, k, :], start=False, stop=k == 7)
                if h == 1:
                    last.then_inc(unit_done, 1)

            def qk_transposes(u):
                pe.wait_ge(unit_drained_dve, u + 1)
                if u >= 2:
                    pe.wait_ge(qkT_drained, u - 1)
                for j in range(HP):
                    last = nc.tensor.transpose(bank[:, 4 + u % 2, P * j:P * (j + 1)],
                                               qn[:, u % 2, P * j:P * (j + 1)], ident[:, :])
                last.then_inc(qkT_ready, 1)

            def scores(a):
                j, qt = a // TT, a % TT
                if a == 0:
                    pe.wait_ge(qkT_drained, 8)
                else:
                    pe.wait_ge(probs_raw, 2 * a)
                n = P * (qt + 1)
                for h in range(2):
                    r = slice(HD * h, HD * (h + 1))
                    mm(bank[:, 2 + h, 0:n], qT[r, j, P * qt:P * (qt + 1)], kT[r, j, 0:n], start=True, stop=True)
                for h in range(2):
                    last = mm(bank[:, 2 + h, P * qt:n], identb[:, :], maskb[:, :], start=False, stop=True,
                              skip_group_check=True)
                last.then_inc(scores_ready, 1)

            def prob_transposes(a):
                qt = a % TT
                pe.wait_ge(probs_ready, a + 1)
                if a >= 1:
                    pe.wait_ge(PT_drained, a)
                for h in range(2):
                    for kt in range(qt + 1):
                        last = nc.tensor.transpose(bank[:, 4 + h, P * kt:P * (kt + 1)],
                                                   probs[:, a % 2, h, P * kt:P * (kt + 1)], ident[:, :])
                last.then_inc(PT_ready, 1)

            def pv(a):
                j, qt = a // TT, a % TT
                pe.wait_ge(PT_drained, a + 1)
                if a == 0:
                    pe.wait_ge(unit_drained_act, 4)
                if a >= 1:
                    pe.wait_ge(attn_drained, a)
                q = slice(P * (a % 4), P * (a % 4) + P)
                for kt in range(qt + 1):
                    for h in range(2):
                        last = mm(bank[HD * h:HD * (h + 1), 6, q], vt[:, kt, P * j + HD * h:P * j + HD * (h + 1)],
                                  PT[:, a % 2, h, kt, :], start=kt == 0, stop=kt == qt)
                last.then_inc(attn_ready, 1)

            def side(*k):
                n = side_no[k]
                b = side_bank(n)
                if n > FIRST_A + 1:
                    pe.wait_ge(side_drained, n - 1)
                elif n == FIRST_A + 1:
                    pe.wait_ge(attn_drained, STEPS)
                elif n > 0:
                    pe.wait_ge(side_drained, n)
                if k[0] in ("g1", "g2"):
                    pe.wait_ge(ada_used, 2 if k[0] == "g1" else 8)
                    last = mm(bank[:, b, :], ones[:, :], acc[:, k[0] == "g2", CH * k[1]:CH * (k[1] + 1)],
                              start=True, stop=True)
                elif k[0] == "B":
                    m = k[1]
                    pe.wait_ge(pooled, m // 2 + 1)
                    if m == 0:
                        pe.wait_ge(late_loaded, 16 * LATE)
                    last = mm(bank[:, b, :], pw[:, m // 2, P * (m % 2):P * (m % 2) + P], pT[:, m // 2, :],
                              start=True, stop=True)
                elif k[0] == "cols":
                    pe.wait_ge(ada_used, 6)
                    for v in range(2):
                        for kk in range(KT):
                            last = mm(bank[:, b, 8 * v + kk:8 * v + kk + 1], acc[:, v, kk:D:KT], ones[:, 0:1],
                                      start=True, stop=True)
                else:
                    m = k[1]
                    if m == 0:
                        pe.wait_ge(side_drained, n)
                        chunk_here(("up",))
                        pe.wait_ge(attn_drained, STEPS)
                    wu = slot[slot_of(("up",))].rearrange("p (k n) -> p k n", k=HP)
                    for kk in range(HP):
                        last = mm(bank[:, b, :], wu[:, kk, P * m:P * (m + 1)], attnT[:, kk, :],
                                  start=kk == 0, stop=kk == HP - 1)
                last.then_inc(side_done, 1)

            def ada_rows(v, part_half):
                n = 2 * v + part_half
                pe.wait_ge(slot_loaded[n], 16)
                w = slot[n].rearrange("p (k n) -> p k n", k=4)
                for kk in range(4):
                    k = 4 * part_half + kk
                    for h in range(2):
                        r = 32 * (2 * v + h)
                        last = mm(bank[r:r + 1, 7, :], cols[:, C_, k:k + 1], w[:, kk, CH * h:CH * (h + 1)],
                                  start=k == 0, stop=k == KT - 1, tile_position=(0, r))
                last.then_inc(ada_rows_done, 1)

            def ada_columns(v):
                pe.wait_ge(ada_rows_out, 2 * v + 2)
                for h in range(2):
                    r = 32 * (2 * v + h)
                    for m in range(KT):
                        last = mm(bank[SLOTS * h:SLOTS * (h + 1), 6, 8 * v + m:8 * v + m + 1],
                                  rows[r:r + 1, m:CH:KT], ones[r:r + 1, 0:1], start=True, stop=True,
                                  tile_position=(r, SLOTS * h))
                if v == 1:
                    last.then_inc(ada_cols_done, 1)

            pe.wait_ge(c_silu, 1)
            ada_rows(0, 0)
            ada_rows(0, 1)
            pe.wait_ge(consts_ready, 1)
            for t in range(TT):
                pe.wait_ge(xn_ready, t + 1)
                x_transposes(range(6), t)
            ada_rows(1, 0)
            ada_columns(0)
            ada_rows(1, 1)
            ada_columns(1)
            pe.wait_ge(ab1_ready, 1)
            for t in range(TT):
                x_transposes([6, 7], t)

            for u in range(UNITS):
                a = u - U_P
                if 0 <= a < STEPS:
                    scores(a)
                unit_half(u, 0)
                if 0 <= a - 1 < STEPS:
                    prob_transposes(a - 1)
                unit_half(u, 1)
                if 1 <= u <= U_V:
                    qk_transposes(u - 1)
                if 0 <= a - 2 < STEPS:
                    pv(a - 2)
                if u in (4, 6):
                    side("g1", u // 2 - 2)
                if u == 9:
                    side("cols")
                if u in (12, 14):
                    side("g2", u // 2 - 6)
                if U_GP + 1 <= u <= U_GA:
                    side("B", u - 1 - U_GP)
            for m in range(KT):
                side("A", m)

            def project(t, h):
                n = t + TT * h
                if n >= 2:
                    pe.wait_ge(yo_drained, n - 1)
                ts = slice(P * t, P * (t + 1))
                for k in range(KT):
                    if t == 0:
                        pe.wait_ge(oL_ready, KT * h + k + 1)
                        if h == 0:
                            pe.wait_ge(mL_ready, k + 1)
                    mm(bank[:, n % 2, :], mH[:, k, ts], w_out_high(h, k), start=k == 0, stop=False)
                    mm(bank[:, n % 2, :], mH[:, k, ts], oL[:, h, k, :], start=False, stop=False)
                    last = mm(bank[:, n % 2, :], mL[:, k, ts], w_out_high(h, k), start=False, stop=k == KT - 1)
                last.then_inc(yo_done, 1)

            def h2_transposes(t):
                pe.wait_ge(xn2_ready, t + 1)
                if t >= 2:
                    pe.wait_ge(h2T_dve, t - 1)
                    pe.wait_ge(h2T_act, t - 1)
                for k in range(KT):
                    last = nc.tensor.transpose(bank[:, 2 + 2 * (t % 2) + k % 2, P * (k // 2):P * (k // 2 + 1)],
                                               xn2[:, t, k:D:KT], ident[:, :])
                last.then_inc(h2T_psum, 1)

            def router(t):
                pe.wait_ge(h2T_dve, t + 1)
                pe.wait_ge(h2T_act, t + 1)
                o = bank[:, 6, 36 * t:36 * (t + 1)]
                for k in range(KT):
                    mm(o, h2T[:, t % 2, k, :], wr[:, k, :], start=k == 0, stop=False)
                mm(o, ones[0:1, :], br[:, :], start=False, stop=True).then_inc(logits_ready, 1)

            pe.wait_ge(side_drained, len(SIDE))
            for t in range(TT):
                project(t, 0)
            for t in range(TT):
                project(t, 1)
                if t >= 1:
                    h2_transposes(t - 1)
                if t >= 2:
                    router(t - 2)
            h2_transposes(TT - 1)
            router(TT - 2)
            router(TT - 1)

            pe.wait_ge(mask_ready, 1)
            for t in range(TT):
                for s in range(t):
                    mm(bank[:, 7, 32 * t:32 * (t + 1)], onesb[:, :], maskm[:, s, :], start=s == 0, stop=False)
                mm(bank[:, 7, 32 * t:32 * (t + 1)], lowb[:, :], maskm[:, t, :], start=t == 0, stop=True)
            for s in range(TT):
                last = mm(bank[:, 7, 128:160], onesb[:, :], maskm[:, s, :], start=s == 0, stop=s == TT - 1)
            last.then_inc(rank_ready, 1)

            def slot_sums(g):
                pe.wait_ge(place_ready, g + 1)
                for q in IDX_GROUPS[g]:
                    for c, rhs in ((0, tokc[:, :, :]), (2, oh2b[:, :, 2 * q:2 * q + 2])):
                        for t in range(TT):
                            e = 2 * (q - IDX_GROUPS[g][0])
                            lhs = place[g][t][:, e:e + 2, :].rearrange("p e s -> p (e s)")
                            last = mm(idx_bank(g)[:, 4 * q + c:4 * q + c + 2], lhs, rhs[:, t, :],
                                      start=t == 0, stop=t == TT - 1)
                last.then_inc(idx_psum, 1)

            slot_sums(0)

            def gather_transposes(n, turn):
                q = n + turn * (RING // 2)
                pe.wait_ge(xg_loaded[n % 3], turn * 16 + 16 * (n // 3 + 1))
                if reached(n, turn, 1):
                    pe.wait_ge(xgT_ready, q)
                    pe.wait_ge(xgT_act, q)
                for k in range(KT):
                    last = nc.tensor.transpose(bank[:, k // 4, P * (k % 4):P * (k % 4 + 1)],
                                               xg[:, n % 3, k:D:KT], ident[:, :])
                last.then_inc(xt_ready, 1)

            def gate_up(n, turn):
                e, s = n + turn * RING, n % RING
                pe.wait_ge(w13_loaded[s], turn * 32 + 32 * (n // RING + 1))
                if n % 2 == 0:
                    pe.wait_ge(xgT_ready, n // 2 + 1 + turn * (RING // 2))
                    pe.wait_ge(xgT_act, n // 2 + 1 + turn * (RING // 2))
                if reached(n, turn, 2):
                    pe.wait_ge(ab_drained, e - 1)
                for k in range(KT):
                    r = slice(SLOTS * (k % 2), SLOTS * (k % 2 + 1))
                    last = mm(bank[r, 2 + n % 2, :].rearrange("p (w f) -> p w f", w=2),
                              xgT[:, k, SLOTS * (n % 2):SLOTS * (n % 2 + 1)],
                              w13[s][:, :, k, :], start=k < 2, stop=k >= KT - 2)
                last.then_inc(ab_done, 1)

            def fold_halves(n, turn):
                e = n + turn * RING
                pe.wait_ge(ab_drained, e + 1)
                if reached(n, turn, 2):
                    pe.wait_ge(hid_ready, e - 1)
                for w in range(2):
                    for ft in range(FT):
                        last = mm(bank[:, 4 + n % 2, SLOTS * (2 * w + ft):SLOTS * (2 * w + ft + 1)],
                                  absb[:, n % 2, F * w + ft:F * (w + 1):FT], fold[:, :], start=True, stop=True)
                last.then_inc(st_done, 1)

            def down(n, turn):
                q = n // 2 + turn * (RING // 2)
                slots = (n % RING, (n + 1) % RING)
                pe.wait_ge(hid_ready, n + 2 + turn * RING)
                for s in slots:
                    pe.wait_ge(w2_loaded[s], turn * 16 + 16 * (n // RING + 1))
                if reached(n, turn, 2):
                    pe.wait_ge(y_drained, q)
                for ft in range(FT):
                    for h in range(2):
                        for x, s in enumerate(slots):
                            last = mm(bank[SLOTS * x:SLOTS * (x + 1), 6 + h, :], hid[:, x, ft, :],
                                      w2s[s][:, ft, CH * h:CH * (h + 1)], start=ft == 0, stop=ft == FT - 1)
                last.then_inc(y_done, 1)

            def step(n, turn):
                if reached(n, turn, 1):
                    fold_halves(n - 1, turn)
                gate_up(n, turn)
                if n % 2 == 0 and reached(n, turn, 2):
                    down(n - 2, turn)
                if n == 0:
                    slot_sums(1)
                if n % 2 and n < E - 1:
                    gather_transposes((n + 1) // 2, turn)

            pe.wait_ge(idx_ready, 1)
            gather_transposes(0, 0)
            all_experts(pe, step)
            fold_halves(E - 1, 0)
            down(E - 2, 0)

            def overflow(b):
                pe.wait_ge(x_place, b + 1)
                for n in range(2 * TT):
                    mm(bank[0:SLOTS, 0, 0:2], xplace[:, n, :], tokc[:, n % TT, :],
                       start=n == 0, stop=n == 2 * TT - 1)
                for n in range(TT, 2 * TT):
                    last = mm(bank[0:SLOTS, 0, 2:3], xplace[:, n, :], onesb[:, 0:1],
                              start=n == TT, stop=n == 2 * TT - 1)
                last.then_inc(x_idx_psum, 1)
                pe.wait_ge(x_rows, 16 * b + 16)
                for k in range(KT):
                    last = nc.tensor.transpose(bank[:, k // 4, P * (k % 4):P * (k % 4 + 1)],
                                               xg[:, 0, k:D:KT], ident[:, :])
                last.then_inc(x_rowsT, 1)
                pe.wait_ge(x_in, b + 1)
                pe.wait_ge(x_loaded_w, 48 * b + 48)
                for k in range(KT):
                    r = slice(SLOTS * (k % 2), SLOTS * (k % 2 + 1))
                    last = mm(bank[r, 2, :].rearrange("p (w f) -> p w f", w=2), xgT[:, k, 0:SLOTS],
                              w13[0][:, :, k, :], start=k < 2, stop=k >= KT - 2)
                last.then_inc(x_ab, 1)
                pe.wait_ge(x_ab_drained, b + 1)
                for w in range(2):
                    for ft in range(FT):
                        last = mm(bank[:, 4, SLOTS * (2 * w + ft):SLOTS * (2 * w + ft + 1)],
                                  absb[:, 0, F * w + ft:F * (w + 1):FT], fold[:, :], start=True, stop=True)
                last.then_inc(x_st, 1)
                pe.wait_ge(x_hid, b + 1)
                for ft in range(FT):
                    for h in range(2):
                        last = mm(bank[0:SLOTS, 6 + h, :], hid[:, 0, ft, :],
                                  w2s[0][:, ft, CH * h:CH * (h + 1)], start=ft == 0, stop=ft == FT - 1)
                last.then_inc(x_y, 1)

            pe.wait_ge(y_drained, PAIRS)
            overflow_blocks(pe, overflow)

        @block.scalar
        def _(act):
            sc = nc.scalar
            act.dma_start(cols[:, N1, :], norm1.rearrange("b (p k) -> (b p) k", k=KT)).then_inc(small_loaded, 16)
            act.dma_start(cols[:, N2, :], norm2.rearrange("b (p k) -> (b p) k", k=KT)).then_inc(small_loaded, 16)
            act.dma_start(cols[:, BA:BA + 6, :], bada_v).then_inc(small_loaded, 16)
            for h in range(2):
                r = slice(HD * h, HD * (h + 1))
                act.dma_start(qkg[r, 0:1], q_norm.rearrange("a (p b) -> (a p) b", b=1)).then_inc(small_loaded, 16)
                act.dma_start(qkg[r, 1:2], k_norm.rearrange("a (p b) -> (a p) b", b=1)).then_inc(small_loaded, 16)
            act.wait_ge(c_loaded, 16)
            sc.activation(cth, cols[:, C_, :], ACT.Tanh, scale=0.5).then_inc(cact_ready, 1)
            for t in range(TT):
                act.wait_ge(x_loaded[t], 16)
                sc.activation(xn[:, t, :], xs[:, t, :], ACT.Square, accum_out=st[:, t:t + 1]).then_inc(x_sq, 1)
            for k in range(1, KT, 2):
                act.wait_ge(ab1_ready, 1)
                act.wait_ge(xT_ready, 4 if k < 6 else 8)
                sc.activation(hT[:, k, :], bank[:, k, :], ACT.Identity, bias=ab1[:, 1, k:k + 1],
                              scale=ab1[:, 0, k:k + 1]).then_inc(hT_act, 1)

            def attend_exp(a):
                n = P * (a % TT + 1)
                act.wait_ge(negmax_ready, a + 1)
                if a >= 2:
                    act.wait_ge(PT_ready, a - 1)
                for h in range(2):
                    sc.activation(probs[:, a % 2, h, 0:n], bank[:, 2 + h, 0:n], ACT.Exp,
                                  bias=st[:, 18 + h + 4 * (a % 2):19 + h + 4 * (a % 2)],
                                  accum_out=st[:, 28 + h + 4 * (a % 2):29 + h + 4 * (a % 2)]).then_inc(probs_raw, 1)

            def attend_pt(a):
                n = P * (a % TT + 1)
                act.wait_ge(PT_ready, a + 1)
                if a >= 2:
                    act.wait_ge(attn_ready, a - 1)
                sc.copy(PT[:, a % 2].rearrange("p h k q -> p h (k q)")[:, :, 0:n],
                        bank[:, 4:6, 0:n]).then_inc(PT_drained, 1)

            def attend_out(a):
                act.wait_ge(attn_ready, a + 1)
                sc.copy(attnT[:, a // TT, P * (a % TT):P * (a % TT + 1)],
                        bank[:, 6, P * (a % 4):P * (a % 4 + 1)]).then_inc(attn_drained, 1)

            def weights_high(u):
                k = IN[u // 4]
                if u < U_P + 2:
                    act.wait_ge(ada_used, 7)
                else:
                    act.wait_ge(unit_done, u - 1)
                act.wait_ge(slot_loaded[slot_of(k)], 16 * turn_of(k))
                sc.copy(wH[:, u % 2], unit_weights(u)).then_inc(wH_ready, 1)

            for u in range(UNITS):
                a = u - U_P
                if U_P <= u + 1 < UNITS:
                    weights_high(u + 1)
                if u in (1, U_V - 1):
                    c_ = 1 if u == 1 else 2
                    act.wait_ge(slot_loaded[slot_of(IN[c_])], 16 * turn_of(IN[c_]))
                    if c_ == 1:
                        act.wait_ge(xT_ready, 8)
                    w = slot[slot_of(IN[c_])].rearrange("p (k n) -> p k n", k=KT)
                    for k in range(KT):
                        if c_ == 2 and k < KT - 1:
                            act.wait_ge(cH_used, k + 1)
                        elif c_ == 2:
                            act.wait_ge(unit_done, U_V)
                        sc.copy(cH[:, k, :], w[:, k, :]).then_inc(cH_ready, 1)
                if u == 2:
                    act.wait_ge(hT_dve, 4)
                    act.wait_ge(ada_rows_done, 4)
                    for k in range(KT):
                        sc.copy(hH[:, k, :], hT[:, k, :]).then_inc(hH_ready, 1)
                if 0 <= a < STEPS:
                    attend_exp(a)
                if 0 <= a - 1 < STEPS:
                    attend_pt(a - 1)
                act.wait_ge(unit_done, u + 1)
                if u == 0:
                    act.dma_start(g1b[:, :], b_ada[0, 2 * D:3 * D].partition_broadcast(P)).then_inc(g_bias_loaded, 16)
                    act.dma_start(g2b[:, :], b_ada[0, 5 * D:6 * D].partition_broadcast(P)).then_inc(g_bias_loaded, 16)
                if u < U_V:
                    if u >= 1:
                        act.wait_ge(qk_var, u)
                    sc.activation(sqbuf, bank[:, u % 2, :], ACT.Square).then_inc(qk_sq, 1)
                elif u < U_P:
                    sc.copy(vt[:, u - U_V, :], bank[:, u % 2, :]).then_inc(unit_drained_act, 1)
                elif u < U_GP:
                    sc.copy(pT[:, u - U_P, :], bank[:, u % 2, :]).then_inc(unit_drained_act, 1)
                else:
                    m = (u - U_GP) % KT
                    to = m if u >= U_GA else m % 2
                    if U_GP + 2 <= u <= U_GA:
                        act.wait_ge(side_drained, side_no[("B", min(m - 2 if u < U_GA else 7, 7))] + 1)
                    sc.activation(sg[:, to, :], bank[:, u % 2, :], ACT.Tanh, scale=0.5).then_inc(unit_drained_act, 1)
                if 0 <= a - 2 < STEPS:
                    attend_out(a - 2)

            def out_weights_high(h, ks):
                k_ = ("out", h)
                act.wait_ge(slot_loaded[slot_of(k_)], 16 * turn_of(k_))
                w = slot[slot_of(k_)].rearrange("p (k n) -> p k n", k=KT)
                for k in ks:
                    sc.copy(w_out_high(h, k), w[:, k, :]).then_inc(oH_ready, 1)

            def merged_high(m):
                act.wait_ge(side_drained, side_no[("A", m)] + 1)
                sc.copy(mH[:, m, :], mergedT[:, m, :]).then_inc(mH_ready, 1)

            act.wait_ge(scores_ready, STEPS)
            out_weights_high(0, range(KT))
            merged_high(0)
            merged_high(1)
            act.wait_ge(unit_done, UNITS)
            out_weights_high(1, range(4))
            for m in range(2, KT):
                merged_high(m)
            act.wait_ge(side_done, len(SIDE))
            out_weights_high(1, range(4, KT))

            def square(t):
                act.wait_ge(yo_drained, TT + t + 1)
                if t == 0:
                    act.wait_ge(unit_done, UNITS)
                sc.activation(xn2[:, t, :], xs[:, t, :], ACT.Square,
                              accum_out=st[:, 8 + t:9 + t]).then_inc(x1_sq, 1)

            def modulate(t):
                act.wait_ge(h2T_psum, t + 1)
                if t == 0:
                    act.wait_ge(PT_ready, STEPS)
                if t >= 2:
                    act.wait_ge(logits_ready, t - 1)
                for k in range(1, KT, 2):
                    last = sc.activation(h2T[:, t % 2, k, :],
                                         bank[:, 3 + 2 * (t % 2), P * (k // 2):P * (k // 2 + 1)], ACT.Identity,
                                         bias=ab2[:, 1, k:k + 1], scale=ab2[:, 0, k:k + 1])
                last.then_inc(h2T_act, 1)

            for t in range(TT + 1):
                if t < TT:
                    square(t)
                if t >= 1:
                    modulate(t - 1)
            act.wait_ge(exp_in, 1)
            sc.activation(gexp, gdif, ACT.Exp).then_inc(exp_out, 1)
            act.wait_ge(exp_in, 2)
            sc.activation(edif, edif, ACT.Exp).then_inc(exp_out, 1)

            def modulate_gathered(n, turn):
                q = n + turn * (RING // 2)
                act.wait_ge(xt_ready, q + 1)
                if reached(n, turn, 1):
                    act.wait_ge(ab_done, q * 2)
                for k in range(KT // 2, KT):
                    last = sc.activation(xgT[:, k, :], bank[:, 1, P * (k % 4):P * (k % 4 + 1)], ACT.Identity,
                                         bias=ab2[:, 1, k:k + 1], scale=ab2[:, 0, k:k + 1])
                last.then_inc(xgT_act, 1)

            def step(n, turn):
                e, b = n + turn * RING, n % 2
                act.wait_ge(ab_done, e + 1)
                if reached(n, turn, 2):
                    act.wait_ge(st_done, e - 1)
                sc.copy(absb[:, b, :], bank[:, 2 + b, :]).then_inc(ab_drained, 1)
                if n % 2 and n < E - 1:
                    modulate_gathered((n + 1) // 2, turn)
                act.wait_ge(st_done, e + 1)
                if reached(n, turn, 2):
                    act.wait_ge(hid_ready, e - 1)
                sc.activation(th[:, b].rearrange("p f s -> p (f s)"), bank[:, 4 + b, 0:FT * SLOTS],
                              ACT.Tanh, scale=0.5).then_inc(th_ready, 1)

            act.wait_ge(yo_drained, 2 * TT)
            modulate_gathered(0, 0)
            all_experts(act, step)

            def overflow(b):
                act.wait_ge(x_ab, b + 1)
                sc.copy(absb[:, 0, :], bank[:, 2, :]).then_inc(x_ab_drained, 1)
                act.wait_ge(x_st, b + 1)
                sc.activation(th[:, 0].rearrange("p f s -> p (f s)"), bank[:, 4, 0:FT * SLOTS],
                              ACT.Tanh, scale=0.5).then_inc(x_th, 1)

            overflow_blocks(act, overflow)

        @block.vector
        def _(dve):
            v = nc.vector
            count = [0]

            def link(ins):
                count[0] += 1
                ins.then_inc(chain, 1)
                dve.wait_ge(chain, count[0])

            def ada(i, steps=range(4)):
                k = ADA[i]
                part, half = k[1], k[2]
                b = {2: 0, 3: 1, 4: 0, 5: 1}[part]
                w = slot[slot_of(k)].rearrange("p (k n) -> p k n", k=4)
                if steps[0] == 0:
                    dve.wait_ge(slot_loaded[slot_of(k)], 16 * turn_of(k))
                    if half == 0 and part == 4:
                        dve.wait_ge(side_done, 2)
                    if half == 0 and part == 5:
                        dve.wait_ge(side_done, side_no[("cols",)] + 1)
                for kk in steps:
                    cc = cols[:, C_, 4 * half + kk:4 * half + kk + 1]
                    if half == 0 and kk == 0:
                        ins = v.tensor_scalar(acc[:, b, :], w[:, kk, :], cc, None, ALU.mult)
                    else:
                        ins = v.scalar_tensor_tensor(out=acc[:, b, :], in0=w[:, kk, :], scalar=cc,
                                                     in1=acc[:, b, :], op0=ALU.mult, op1=ALU.add)
                    if kk < 3:
                        link(ins)
                if steps[-1] == 3:
                    ins.then_inc(ada_used, 1)
                    dve.wait_ge(ada_used, i + 1)

            dve.wait_ge(cact_ready, 1)
            link(v.scalar_tensor_tensor(out=cols[:, C_, :], in0=cth, scalar=1.0, in1=cols[:, C_, :],
                                        op0=ALU.add, op1=ALU.mult))
            ins = v.tensor_scalar(cols[:, C_, :], cols[:, C_, :], 0.5, None, ALU.mult)
            ins.then_inc(c_silu, 1)
            dve.wait_ge(c_silu, 1)
            dve.wait_ge(x_sq, TT)
            v.tensor_scalar(st[:, 4:8], st[:, 0:4], 1.0 / D, EPS, ALU.mult, ALU.add).then_inc(x_var, 1)
            dve.wait_ge(x_rstd, 1)
            for t in range(TT):
                v.tensor_scalar(xn[:, t, :], xs[:, t, :], st[:, 12 + t:13 + t], None, ALU.mult).then_inc(xn_ready, 1)
            dve.wait_ge(small_loaded, 16 * SMALL)
            link(v.tensor_scalar(qkg[:, 0:1], qkg[:, 0:1], HD ** -0.5, None, ALU.mult))

            def norm_cols(src, nrow, dst, jb_scale, jb_shift, done):
                link(v.tensor_tensor(dst[:, 1, :], src[:, 8:16], cols[:, BA + jb_shift, :], ALU.add))
                link(v.tensor_tensor(dst[:, 0, :], src[:, 0:8], cols[:, BA + jb_scale, :], ALU.add))
                v.scalar_tensor_tensor(out=dst[:, 0, :], in0=dst[:, 0, :], scalar=1.0, in1=cols[:, nrow, :],
                                       op0=ALU.add, op1=ALU.mult).then_inc(done, 1)

            for v_ in range(2):
                dve.wait_ge(ada_rows_done, 2 * v_ + 2)
                for r in (64 * v_, 64 * v_ + 32):
                    v.tensor_copy(rows[r:r + 1, :], bank[r:r + 1, 7, :]).then_inc(ada_rows_out, 1)
            dve.wait_ge(ada_cols_done, 1)
            norm_cols(bank[:, 6, :], N1, ab1, 1, 0, ab1_ready)
            dve.wait_ge(ab1_ready, 1)
            for k in range(0, KT, 2):
                dve.wait_ge(xT_ready, 4 if k < 6 else 8)
                v.tensor_scalar(hT[:, k, :], bank[:, k, :], ab1[:, 0, k:k + 1], ab1[:, 1, k:k + 1],
                                ALU.mult, ALU.add).then_inc(hT_dve, 1)

            def chunk_low(i, ks):
                w = slot[slot_of(IN[i])].rearrange("p (k n) -> p k n", k=KT)
                for k in ks:
                    dve.wait_ge(cH_ready, KT * (i - 1) + k + 1)
                    v.tensor_tensor(cL[:, k, :], w[:, k, :], cH[:, k, :].bitcast(F32),
                                    ALU.subtract).then_inc(cL_ready, 1)

            def weights_low(u):
                dve.wait_ge(wH_ready, u - U_P + 1)
                v.tensor_tensor(wL[:, u % 2], unit_weights(u), wH[:, u % 2].bitcast(F32),
                                ALU.subtract).then_inc(wL_ready, 1)

            def qk_norm(u):
                b = u % 2
                dve.wait_ge(qk_sq, u + 1)
                v.tensor_reduce(ss[:, b, 0, :], sqbuf.rearrange("p (h d) -> p h d", h=HEADS), AX.X,
                                ALU.add).then_inc(chain, 1)
                count[0] += 1
                dve.wait_ge(chain, count[0])
                v.tensor_scalar(ss[:, b, 0, :], ss[:, b, 0, :], 1.0 / HD, EPS, ALU.mult, ALU.add).then_inc(qk_var, 1)

            def qk_scale(u):
                b = u % 2
                dve.wait_ge(qk_rstd, u + 1)
                if u >= 2:
                    dve.wait_ge(qkT_ready, u - 1)
                v.tensor_tensor(qn[:, b, :].rearrange("p (h d) -> p h d", h=HEADS),
                                bank[:, u % 2, :].rearrange("p (h d) -> p h d", h=HEADS),
                                ss[:, b, 1, :].unsqueeze(2).broadcast_to([P, HEADS, HD]),
                                ALU.mult).then_inc(unit_drained_dve, 1)

            def qk_gain(u):
                dve.wait_ge(qkT_ready, u + 1)
                dst = (qT if u < 4 else kT)[:, :, P * (u % 4):P * (u % 4 + 1)]
                g = qkg[:, 0:1] if u < 4 else qkg[:, 1:2]
                v.tensor_scalar(dst, bank[:, 4 + u % 2, :].rearrange("p (j q) -> p j q", j=HP), g, None,
                                ALU.mult).then_inc(qkT_drained, 1)

            def attend_max(a):
                n = P * (a % TT + 1)
                o = 4 * (a % 2)
                dve.wait_ge(scores_ready, a + 1)
                link(v.tensor_reduce(st[:, 16 + o:18 + o], bank[:, 2:4, 0:n], AX.X, ALU.max))
                v.tensor_scalar(st[:, 18 + o:20 + o], st[:, 16 + o:18 + o], -1.0, None,
                                ALU.mult).then_inc(negmax_ready, 1)

            def attend_norm(a):
                n = P * (a % TT + 1)
                o = 4 * (a % 2)
                dve.wait_ge(probs_raw, 2 * a + 2)
                link(v.reciprocal(st[:, 30 + o:32 + o], st[:, 28 + o:30 + o]))
                for h in range(2):
                    last = v.tensor_scalar(probs[:, a % 2, h, 0:n], probs[:, a % 2, h, 0:n],
                                           st[:, 30 + o + h:31 + o + h], None, ALU.mult)
                last.then_inc(probs_ready, 1)

            def side(*k):
                n = side_no[k]
                b = side_bank(n)
                dve.wait_ge(side_done, n + 1)
                if k[0] in ("g1", "g2"):
                    g = (g1b if k[0] == "g1" else g2b)[:, CH * k[1]:CH * (k[1] + 1)]
                    dve.wait_ge(g_bias_loaded, 32)
                    v.tensor_tensor(g, bank[:, b, :], g, ALU.add).then_inc(side_drained, 1)
                elif k[0] == "cols":
                    norm_cols(bank[:, b, :], N2, ab2, 4, 3, side_drained)
                elif k[0] == "B":
                    m = k[1]
                    if m == 0:
                        dve.wait_ge(xT_ready, 8)
                        dve.wait_ge(late_loaded, 16 * LATE)
                        link(v.tensor_scalar(cols[:, PS, :], cols[:, PS, :], 0.5, None, ALU.mult))
                    dve.wait_ge(unit_drained_act, U_GP - U_V + m + 1)
                    link(v.tensor_scalar(mergedT[:, m, :], bank[:, b, :], cols[:, PS, m:m + 1], None, ALU.mult))
                    v.scalar_tensor_tensor(out=mergedT[:, m, :], in0=sg[:, m % 2, :], scalar=1.0,
                                           in1=mergedT[:, m, :], op0=ALU.add, op1=ALU.mult).then_inc(side_drained, 1)
                else:
                    m = k[1]
                    dve.wait_ge(unit_drained_act, U_GA - U_V + m + 1)
                    link(v.scalar_tensor_tensor(out=sg[:, m, :], in0=sg[:, m, :], scalar=1.0, in1=bank[:, b, :],
                                                op0=ALU.add, op1=ALU.mult))
                    v.scalar_tensor_tensor(out=mergedT[:, m, :], in0=sg[:, m, :], scalar=0.5, in1=mergedT[:, m, :],
                                           op0=ALU.mult, op1=ALU.add).then_inc(side_drained, 1)

            early, later = range(0, 2), range(2, 4)
            ADA_STEPS = {1: (0, early), 2: (1, early), 3: (2, early), 4: (2, later), 5: (3, early), 6: (3, later), 7: (4, early)}
            ADA_AT = {1: [(0, later)], 2: [(1, later)], 8: [(4, later), (5,)], 10: [(6,)], 11: [(7,)]}
            for u in range(UNITS):
                a = u - U_P
                if u == U_K - 1:
                    for k in range(KT):
                        if k < KT - 1:
                            dve.wait_ge(hT_used, k + 1)
                        else:
                            dve.wait_ge(unit_done, U_K)
                        dve.wait_ge(hH_ready, k + 1)
                        v.tensor_tensor(hL[:, k, :], hT[:, k, :], hH[:, k, :].bitcast(F32),
                                        ALU.subtract).then_inc(hL_ready, 1)
                if u == U_V - 1:
                    chunk_low(2, range(KT))
                if 0 <= a < STEPS:
                    attend_max(a)
                if 1 <= u <= 8:
                    qk_gain(u - 1)
                if u < U_V:
                    qk_norm(u)
                    if u in ADA_STEPS:
                        ada(*ADA_STEPS[u])
                    qk_scale(u)
                if u in (0, 1):
                    chunk_low(1, range(4 * u, 4 * u + 4))
                if u in (5, 7):
                    side("g1", u // 2 - 2)
                if u == 10:
                    side("cols")
                if u in (13, 15):
                    side("g2", u // 2 - 6)
                if U_GP + 2 <= u <= U_GA + 1:
                    side("B", u - 2 - U_GP)
                if U_P <= u + 1 < UNITS:
                    weights_low(u + 1)
                if 0 <= a < STEPS:
                    attend_norm(a)
                for steps in ADA_AT.get(u, ()):
                    ada(*steps)

            def out_weights_low(h, ks):
                w = slot[slot_of(("out", h))].rearrange("p (k n) -> p k n", k=KT)
                for k in ks:
                    dve.wait_ge(oH_ready, KT * h + k + 1)
                    v.tensor_tensor(oL[:, h, k, :], w[:, k, :], w_out_high(h, k).bitcast(F32),
                                    ALU.subtract).then_inc(oL_ready, 1)

            def merged_low(m):
                dve.wait_ge(mH_ready, m + 1)
                v.tensor_tensor(mL[:, m, :], mergedT[:, m, :], mH[:, m, :].bitcast(F32),
                                ALU.subtract).then_inc(mL_ready, 1)

            lows = {0: [(0, range(0, 4))], 1: [(0, range(4, 8))], 2: [0, 1], 3: [(1, range(0, 4))], 4: [2, 3],
                    5: [4], 6: [5], 7: [6, 7, (1, range(4, 8))]}
            for m in range(KT):
                side("A", m)
                for part in lows[m]:
                    if isinstance(part, tuple):
                        out_weights_low(*part)
                    else:
                        merged_low(part)

            def residual(t, h):
                n = t + TT * h
                dve.wait_ge(yo_done, n + 1)
                w = slice(CH * h, CH * (h + 1))
                tmp = acc[:, n % 2, w]
                if n >= 2:
                    dve.wait_ge(yo_drained, n - 1)
                link(v.tensor_tensor(tmp, bank[:, n % 2, :], g1b[:, w], ALU.mult))
                v.tensor_tensor(xs[:, t, w], tmp, xs[:, t, w], ALU.add).then_inc(yo_drained, 1)

            def modulate(t):
                dve.wait_ge(h2T_psum, t + 1)
                if t >= 2:
                    dve.wait_ge(logits_ready, t - 1)
                for k in range(0, KT, 2):
                    last = v.tensor_scalar(h2T[:, t % 2, k, :], bank[:, 2 + 2 * (t % 2), P * (k // 2):P * (k // 2 + 1)],
                                           ab2[:, 0, k:k + 1], ab2[:, 1, k:k + 1], ALU.mult, ALU.add)
                last.then_inc(h2T_dve, 1)

            for t in range(TT):
                residual(t, 0)
            for t in range(TT + 1):
                if t < TT:
                    residual(t, 1)
                if t >= 1:
                    modulate(t - 1)
                if t < TT:
                    dve.wait_ge(x1_sq, t + 1)
                    v.tensor_scalar(st[:, 40 + t:41 + t], st[:, 8 + t:9 + t], 1.0 / D, EPS, ALU.mult,
                                    ALU.add).then_inc(x1_var, 1)
                    dve.wait_ge(x1_rstd, t + 1)
                    v.tensor_scalar(xn2[:, t, :], xs[:, t, :], st[:, 44 + t:45 + t], None,
                                    ALU.mult).then_inc(xn2_ready, 1)

            dve.wait_ge(logits_ready, TT)
            dve.wait_ge(iotas_ready, 1)
            bc = lambda ap, shape, d: ap.unsqueeze(d).broadcast_to(shape)
            S4, S32 = [P, TT, NG], [P, TT, E]
            link(v.tensor_copy(lg, bank[:, 6, 0:TT * 36].rearrange("p (t n) -> p t n", t=TT)))
            gl, el = lg[:, :, 0:NG], lg[:, :, NG:NG + E]

            def first_max(vals, best, n, it, shape, eq, score, oh):
                link(v.tensor_reduce(best, vals, AX.X, ALU.max))
                link(v.tensor_tensor(eq, vals, bc(best, shape, 2), ALU.is_equal))
                link(v.tensor_tensor(eq, eq, it.unsqueeze(1).broadcast_to(shape), ALU.mult))
                link(v.tensor_reduce(score, eq, AX.X, ALU.max))
                link(v.tensor_tensor(oh, eq, bc(score, shape, 2), ALU.is_equal))

            first_max(gl, gbest, NG, iota_g, S4, geq, gscore, goh)
            v.tensor_tensor(gdif, gl, bc(gbest, S4, 2), ALU.subtract).then_inc(exp_in, 1)
            link(v.tensor_scalar(gpen, goh, -1.0, -NEG, ALU.add, ALU.mult))
            for t in range(TT):
                last = v.tensor_tensor(em[:, t, :].rearrange("p (g e) -> p g e", g=NG),
                                       el[:, t, :].rearrange("p (g e) -> p g e", g=NG),
                                       bc(gpen[:, t, :], [P, NG, EPG], 2), ALU.add)
            link(last)
            first_max(em, best1, E, iota_e, S32, eq1, score1, oh1)
            link(v.scalar_tensor_tensor(out=em.rearrange("p t e -> p (t e)"), in0=oh1.rearrange("p t e -> p (t e)"),
                                        scalar=10 * NEG, in1=em.rearrange("p t e -> p (t e)"),
                                        op0=ALU.mult, op1=ALU.add))
            first_max(em, best2, E, iota_e, S32, eq1, score1, oh2)
            v.tensor_tensor(maskm, oh1, oh2, ALU.add).then_inc(mask_ready, 1)
            v.tensor_tensor(edif, best2, best1, ALU.subtract).then_inc(exp_in, 1)
            v.tensor_copy(oh2b, oh2)
            link(v.tensor_tensor(maskf, oh1, oh2, ALU.add))
            dve.wait_ge(rank_ready, 1)
            link(v.tensor_copy(cnt, bank[:, 7, 128:160]))
            link(v.tensor_copy(rk.rearrange("p t e -> p (t e)"), bank[:, 7, 0:TT * E]))
            link(v.scalar_tensor_tensor(out=rm.rearrange("p t e -> p (t e)"), in0=rk.rearrange("p t e -> p (t e)"),
                                        scalar=1.0, in1=maskf.rearrange("p t e -> p (t e)"),
                                        op0=ALU.add, op1=ALU.mult))
            for t in range(TT):
                dve.wait_ge(xn2_stored[t], 16)

            def one_hot(g, ts):
                qs = IDX_GROUPS[g]
                es, n = slice(2 * qs[0], 2 * qs[-1] + 2), 2 * len(qs)
                for t in ts:
                    last = v.tensor_tensor(place[g][t], bc(rm[:, t, es], [P, n, SLOTS], 2),
                                           iota_s.unsqueeze(1).broadcast_to([P, n, SLOTS]), ALU.is_equal)
                if t == TT - 1:
                    last.then_inc(place_ready, 1)

            def indices(g):
                a, b = IDX_GROUPS[g][0], IDX_GROUPS[g][-1] + 1
                dve.wait_ge(idx_psum, g + 1)
                link(v.tensor_copy(slotv[:, a:b, :], idx_bank(g)[:, 4 * a:4 * b].rearrange("p (q c) -> p q c", c=4)))
                dst, tmp = tokg[:, a:b], tok1[:, a:b]
                link(v.tensor_tensor(tmp, slotv[:, a:b, 0], slotv[:, a:b, 1], ALU.add))
                link(v.tensor_scalar(dst, tmp, 0.0, float(OUT_OF_BOUNDS), ALU.is_equal, ALU.mult))
                link(v.scalar_tensor_tensor(out=dst, in0=dst, scalar=-1.0, in1=tmp, op0=ALU.add, op1=ALU.add))
                v.tensor_copy(gidx[:, a:b], tokg[:, a:b]).then_inc(idx_ready, 1)
                for x in range(2):
                    r = slice(SLOTS * x, SLOTS * (x + 1))
                    last = v.scalar_tensor_tensor(out=sidx[r, a:b], in0=tokg[r, a:b], scalar=2.0,
                                                  in1=slotv[r, a:b, 2 + x], op0=ALU.mult, op1=ALU.add)
                last.then_inc(sidx_ready, 1)

            one_hot(0, range(TT))
            indices(0)
            one_hot(1, range(0, 2))

            def modulate_gathered(n, turn):
                q = n + turn * (RING // 2)
                dve.wait_ge(xt_ready, q + 1)
                if reached(n, turn, 1):
                    dve.wait_ge(ab_done, q * 2)
                for k in range(KT // 2):
                    last = v.tensor_scalar(xgT[:, k, :], bank[:, k // 4, P * (k % 4):P * (k % 4 + 1)],
                                           ab2[:, 0, k:k + 1], ab2[:, 1, k:k + 1], ALU.mult, ALU.add)
                last.then_inc(xgT_ready, 1)

            def hidden(n, turn):
                e, b = n + turn * RING, n % 2
                dve.wait_ge(th_ready, e + 1)
                if reached(n, turn, 2):
                    dve.wait_ge(y_done, n // 2 + turn * (RING // 2))
                v.scalar_tensor_tensor(out=sl[:, b].rearrange("p f s -> p (f s)"),
                                       in0=th[:, b].rearrange("p f s -> p (f s)"), scalar=1.0,
                                       in1=bank[:, 4 + b, 0:FT * SLOTS], op0=ALU.add,
                                       op1=ALU.mult).then_inc(silu_ready, 1)
                dve.wait_ge(silu_ready, e + 1)
                v.scalar_tensor_tensor(out=hid[:, b].rearrange("p f s -> p (f s)"),
                                       in0=sl[:, b].rearrange("p f s -> p (f s)"), scalar=0.5,
                                       in1=bank[:, 4 + b, FT * SLOTS:2 * FT * SLOTS], op0=ALU.mult,
                                       op1=ALU.mult).then_inc(hid_ready, 1)

            def drain_y(n, turn):
                q = n + turn * (RING // 2)
                dve.wait_ge(y_done, q + 1)
                if reached(n, turn, 3):
                    dve.wait_ge(y_stored[n % 3], turn * 16 + 16 * (n // 3))
                for h in range(2):
                    w = slice(CH * h, CH * (h + 1))
                    last = v.tensor_tensor(ysb[n % 3][:, w], bank[:, 6 + h, :], g2b[:, w], ALU.mult)
                last.then_inc(y_drained, 1)

            def step(n, turn):
                if n % 2 == 0 and reached(n, turn, 2):
                    drain_y(n // 2 - 1, turn)
                if n % 2 and n < E - 1:
                    modulate_gathered((n + 1) // 2, turn)
                hidden(n, turn)

            modulate_gathered(0, 0)
            one_hot(1, range(2, TT))
            indices(1)
            dve.wait_ge(exp_out, 1)
            link(v.tensor_reduce(gsum, gexp, AX.X, ALU.add))
            link(v.reciprocal(gsum, gsum))
            dve.wait_ge(exp_out, 2)
            link(v.tensor_scalar(best1, edif, 1.0, None, ALU.add))
            link(v.reciprocal(best1, best1))
            link(v.tensor_tensor(cw[:, 0, :], best1, gsum, ALU.mult))
            link(v.tensor_tensor(cw[:, 1, :], cw[:, 0, :], edif, ALU.mult))

            def overflow_counts():
                link(v.tensor_scalar(nx[0], cnt, float(SLOTS), None, ALU.is_gt))
                for m in range(2, T // SLOTS):
                    link(v.scalar_tensor_tensor(out=nx[0], in0=cnt, scalar=float(SLOTS * m), in1=nx[0],
                                                op0=ALU.is_gt, op1=ALU.add))
                link(v.tensor_copy(nx[1], nx[0]))
                cur, s = 1, 1
                while s < E:
                    nxt = 3 - cur
                    v.tensor_copy(nx[nxt][:, 0:s], nx[cur][:, 0:s])
                    link(v.tensor_tensor(nx[nxt][:, s:E], nx[cur][:, s:E], nx[cur][:, 0:E - s], ALU.add))
                    cur, s = nxt, 2 * s
                incl = nx[cur]
                for h in range(2):
                    half = incl[:, E // 2 * h:E // 2 * (h + 1)]
                    S = [P, E // 2, MAXB]
                    link(v.tensor_tensor(xcmp, bc(half, S, 2), iota_b.unsqueeze(1).broadcast_to(S), ALU.is_le))
                    link(v.tensor_reduce(xsum[:, h, :], xcmp.rearrange("p e b -> p b e"), AX.X, ALU.add))
                link(v.tensor_tensor(xsum[:, 0, :], xsum[:, 0, :], xsum[:, 1, :], ALU.add))
                link(v.tensor_scalar(xsum[:, 0, :], xsum[:, 0, :], float(E - 1), None, ALU.min))
                v.tensor_copy(xtab[:, 0:MAXB], xsum[:, 0, :])
                link(v.tensor_copy(xtab[:, MAXB:MAXB + 1], incl[:, E - 1:E]))
                v.tensor_scalar(xbase[:, :], cnt[:, 0:1], 0.0, float(E * SLOTS - 1), ALU.mult,
                                ALU.add).then_inc(xtab_ready, 1)
                dve.wait_ge(xtab_ready, 1)
                link(v.tensor_tensor(cnt, incl, nx[0], ALU.subtract))
                link(v.tensor_scalar(cnt, cnt, float(SLOTS), float((E - 1) * SLOTS), ALU.mult, ALU.add))
                link(v.tensor_scalar(nx[cur], iota_e, -float(SLOTS), float(E * SLOTS), ALU.mult, ALU.add))
                e64 = nx[cur]
                link(v.tensor_tensor(cnt, cnt, e64, ALU.subtract))
                link(v.tensor_scalar(xem, rk, float(SLOTS), None, ALU.is_ge))
                link(v.tensor_tensor(xem, xem, cnt.unsqueeze(1).broadcast_to(S32), ALU.mult))
                link(v.tensor_tensor(rk, rk, e64.unsqueeze(1).broadcast_to(S32), ALU.add))
                link(v.tensor_tensor(rk, rk, xem, ALU.add))
                for j, oh in enumerate((oh1, oh2)):
                    link(v.tensor_tensor(xem, rk, oh, ALU.mult))
                    link(v.tensor_reduce(posf[:, j, :], xem, AX.X, ALU.add))

            all_experts(dve, step, overflow_counts)
            drain_y(PAIRS - 1, 0)

            def overflow(b):
                v.tensor_scalar(xrel[:, :], posf.rearrange("p j t -> p (j t)"), xbase[:, :], None,
                                ALU.subtract).then_inc(x_rel, 1)
                dve.wait_ge(x_rel, b + 1)
                v.tensor_tensor(xplace, bc(xrel[:, :], [P, 2 * TT, SLOTS], 2),
                                iota_s.unsqueeze(1).broadcast_to([P, 2 * TT, SLOTS]), ALU.is_equal).then_inc(x_place, 1)
                v.tensor_scalar(xbase[:, :], xbase[:, :], float(SLOTS), None, ALU.add).then_inc(x_base, 1)
                dve.wait_ge(x_base, b + 1)
                dve.wait_ge(x_idx_psum, b + 1)
                r = slice(0, SLOTS)
                v.tensor_copy(xv[r, 0:3], bank[r, 0, 0:3]).then_inc(x_steps, 1)
                dve.wait_ge(x_steps, 6 * b + 1)
                v.tensor_tensor(xv[r, 3:4], xv[r, 0:1], xv[r, 1:2], ALU.add).then_inc(x_steps, 1)
                dve.wait_ge(x_steps, 6 * b + 2)
                v.tensor_scalar(xv[r, 4:5], xv[r, 3:4], 0.0, float(OUT_OF_BOUNDS), ALU.is_equal,
                                ALU.mult).then_inc(x_steps, 1)
                dve.wait_ge(x_steps, 6 * b + 3)
                v.scalar_tensor_tensor(out=xv[r, 5:6], in0=xv[r, 4:5], scalar=-1.0, in1=xv[r, 3:4], op0=ALU.add,
                                       op1=ALU.add).then_inc(x_steps, 1)
                dve.wait_ge(x_steps, 6 * b + 4)
                v.tensor_copy(gidxx[r, :], xv[r, 5:6]).then_inc(x_steps, 1)
                v.scalar_tensor_tensor(out=sidxx[r, :], in0=xv[r, 5:6], scalar=2.0, in1=xv[r, 2:3], op0=ALU.mult,
                                       op1=ALU.add).then_inc(x_steps, 1)
                dve.wait_ge(x_steps, 6 * b + 6)
                v.tensor_copy(xv[r, 6:7], xv[r, 5:6]).then_inc(x_idx, 1)
                dve.wait_ge(x_rowsT, b + 1)
                for k in range(KT):
                    last = v.tensor_scalar(xgT[:, k, 0:SLOTS], bank[:, k // 4, P * (k % 4):P * (k % 4) + SLOTS],
                                           ab2[:, 0, k:k + 1], ab2[:, 1, k:k + 1], ALU.mult, ALU.add)
                last.then_inc(x_in, 1)
                dve.wait_ge(x_th, b + 1)
                v.scalar_tensor_tensor(out=sl[:, 0].rearrange("p f s -> p (f s)"),
                                       in0=th[:, 0].rearrange("p f s -> p (f s)"), scalar=1.0,
                                       in1=bank[:, 4, 0:FT * SLOTS], op0=ALU.add, op1=ALU.mult).then_inc(x_silu, 1)
                dve.wait_ge(x_silu, b + 1)
                v.scalar_tensor_tensor(out=hid[:, 0].rearrange("p f s -> p (f s)"),
                                       in0=sl[:, 0].rearrange("p f s -> p (f s)"), scalar=0.5,
                                       in1=bank[:, 4, FT * SLOTS:2 * FT * SLOTS], op0=ALU.mult,
                                       op1=ALU.mult).then_inc(x_hid, 1)
                dve.wait_ge(x_y, b + 1)
                for h in range(2):
                    w = slice(CH * h, CH * (h + 1))
                    last = v.tensor_tensor(ysb[0][r, w], bank[r, 6 + h, :], g2b[r, w], ALU.mult)
                last.then_inc(x_y_drained, 1)
                dve.wait_ge(x_stored, 16 * b + 16)

            dve.wait_ge(y_stored[0], 16 * len(range(0, PAIRS, 3)))
            overflow_blocks(dve, overflow)

            for n in range(2 * TT):
                t, w = n // 2, slice(CH * (n % 2), CH * (n % 2 + 1))
                dve.wait_ge(yg_loaded[n], 16)
                for j in range(2):
                    last = v.scalar_tensor_tensor(out=xs[:, t, w], in0=yg[:, t, j, w], scalar=cw[:, j, t:t + 1],
                                                  in1=xs[:, t, w], op0=ALU.mult, op1=ALU.add)
                    if j == 0:
                        link(last)
                last.then_inc(out_ready, 1)

        @block.gpsimd
        def _(pool):
            g = nc.gpsimd
            count = [0]

            def link(ins):
                count[0] += 1
                ins.then_inc(pool_link, 1)
                pool.wait_ge(pool_link, count[0])

            def fill_diagonal(tile, base, n):
                link(g.affine_select(out=tile, in_=tile, compare_op=ALU.not_equal, fill=1.0, base=base,
                                     pattern=[[-1, n]], channel_multiplier=1))

            link(g.memset(ident[:, :], 0.0))
            fill_diagonal(ident[:, :], 0, P)
            link(g.tensor_copy(identb[:, :], ident[:, :]))
            link(g.memset(fold[:, :], 0.0))
            fill_diagonal(fold[:, :], 0, SLOTS)
            fill_diagonal(fold[:, :], -SLOTS, SLOTS)
            g.memset(ones[:, :], 1.0)
            link(g.memset(onesb[:, :], 1.0))
            link(g.memset(maskb[:, :], 0.0))
            g.affine_select(out=maskb[:, :], in_=maskb[:, :], compare_op=ALU.is_ge, fill=NEG, base=0,
                            pattern=[[-1, P]], channel_multiplier=1)
            g.affine_select(out=lowb[:, :], in_=onesb[:, :], compare_op=ALU.is_gt, fill=0.0, base=0,
                            pattern=[[1, P]], channel_multiplier=-1)
            for j in range(16):
                g.memset(recip[:, j:j + 1], 1.0 / (j + 1))
            for t in range(TT):
                g.iota(tokc[:, t, 0:1], pattern=[[0, 1]], base=1, channel_multiplier=1,
                       allow_small_or_imprecise_dtypes=True)
                g.iota(tokc[:, t, 1:2], pattern=[[0, 1]], base=P * t, channel_multiplier=0,
                       allow_small_or_imprecise_dtypes=True)
            kw = dict(allow_small_or_imprecise_dtypes=True, channel_multiplier=0)
            g.iota(iota_g, pattern=[[-1, NG]], base=NG, **kw)
            g.iota(iota_e, pattern=[[-1, E]], base=E, **kw)
            g.iota(iota_b, pattern=[[1, MAXB]], base=0, **kw)
            g.iota(iota_s, pattern=[[1, SLOTS]], base=1, **kw).then_inc(iotas_ready, 1)
            link(g.memset(nhalf[:, :], -0.5))
            g.memset(gidxx[:, :], 2 * OUT_OF_BOUNDS)
            g.memset(sidxx[:, :], 2 * OUT_OF_BOUNDS).then_inc(consts_ready, 1)
            pool.wait_ge(x_var, 1)
            g.tensor_tensor(st[:, 12:16], st[:, 4:8], nhalf[:, 0:4], ALU.pow).then_inc(x_rstd, 1)
            pool.wait_ge(slot_loaded[0], 32)
            pool.dma_start(cols[:, PS, :], pool_scale.rearrange("b (m p) -> (b p) m", p=P),
                           allow_slow_non_contiguous=True).then_inc(late_loaded, 16)
            pool.dma_start(wr[:, :, 0:NG], w_router_g.rearrange("l (p k) n -> (l p) k n", k=KT)).then_inc(late_loaded, 16)
            pool.dma_start(wr[:, :, NG:NG + E], w_router_e.rearrange("l (p k) n -> (l p) k n", k=KT)).then_inc(late_loaded, 16)
            pool.dma_start(br[:, 0:NG], b_router_g).then_inc(late_loaded, 16)
            pool.dma_start(br[:, NG:NG + E], b_router_e).then_inc(late_loaded, 16)
            for u in range(U_V):
                pool.wait_ge(qk_var, u + 1)
                if u >= 2:
                    pool.wait_ge(unit_drained_dve, u - 1)
                g.tensor_tensor(ss[:, u % 2, 1, :], ss[:, u % 2, 0, :], nhalf[:, :], ALU.pow).then_inc(qk_rstd, 1)

            pool.wait_ge(ada_used, len(ADA))
            pool.dma_start(pw, w_pool.rearrange("l g c n -> (l c) g n")).then_inc(late_loaded, 16)
            for gi, w in enumerate(WINDOWS):
                pool.wait_ge(unit_drained_act, U_P - U_V + gi + 1)
                src, s, b = pT[:, gi, :], 1, 0
                while s < w:
                    dst = ptmp[b]
                    g.tensor_copy(dst[:, 0:s], src[:, 0:s])
                    link(g.tensor_tensor(dst[:, s:T], src[:, s:T], src[:, 0:T - s], ALU.add))
                    src, s, b = dst, 2 * s, 1 - b
                g.tensor_tensor(src[:, 0:w - 1], src[:, 0:w - 1], recip[:, 0:w - 1], ALU.mult)
                link(g.tensor_scalar(src[:, w - 1:T], src[:, w - 1:T], 1.0 / w, None, ALU.mult))
                g.tensor_tensor(pT[:, gi, :], src, pT[:, gi, :], ALU.subtract).then_inc(pooled, 1)
                pool.wait_ge(pooled, gi + 1)

            for t in range(TT):
                pool.wait_ge(x1_var, t + 1)
                g.tensor_tensor(st[:, 44 + t:45 + t], st[:, 40 + t:41 + t], nhalf[:, 0:1],
                                ALU.pow).then_inc(x1_rstd, 1)

            def gather(dst, ix, done):
                pool.indirect_dma_start(out=dst, out_offset=None, in_=xn2_d,
                                        in_offset=bass.IndirectOffsetOnAxis(ap=ix, axis=0),
                                        bounds_check=T - 1, oob_is_err=False).then_inc(done, 16)

            def scatter(src, ix, done):
                pool.indirect_dma_start(out=y_d, out_offset=bass.IndirectOffsetOnAxis(ap=ix, axis=0), in_=src,
                                        in_offset=None, bounds_check=2 * T - 1, oob_is_err=False).then_inc(done, 16)

            for t in range(TT):
                pool.wait_ge(xn2_stored[t], 16)
            for q in range(PAIRS + 5):
                if q >= 5:
                    if q == 5:
                        pool.wait_ge(sidx_ready, len(IDX_GROUPS))
                    pool.wait_ge(y_drained, q - 4)
                    scatter(ysb[(q - 5) % 3], sidx[:, q - 5:q - 4], y_stored[(q - 5) % 3])
                if q < PAIRS:
                    for g_, qs in enumerate(IDX_GROUPS):
                        if q == qs[0]:
                            pool.wait_ge(idx_ready, g_ + 1)
                    if q >= 3:
                        pool.wait_ge(xt_ready, q - 2)
                    gather(xg[:, q % 3, :], gidx[:, q:q + 1], xg_loaded[q % 3])

            def overflow(b):
                pool.wait_ge(x_idx, b + 1)
                pool.sem_inc(x_turns, 1)
                gather(xg[:, 0, :], gidxx[:, :], x_rows)
                pool.wait_ge(x_y_drained, b + 1)
                pool.sem_inc(x_turns, 1)
                scatter(ysb[0], sidxx[:, :], x_stored)
                pool.wait_ge(x_stored, 16 * b + 16)
                pool.sem_inc(x_turns, 1)

            overflow_blocks(pool, overflow)
            pool.sem_inc(overflow_done, 1)


_INS = ['x', 'c', 'w_ada', 'b_ada', 'norm1', 'w_in', 'q_norm', 'k_norm', 'w_attn_up', 'w_pool', 'pool_scale',
        'w_out', 'norm2', 'w_router_g', 'b_router_g', 'w_router_e', 'b_router_e', 'w1', 'w3', 'w2']


def kernel(**inputs):
    import numpy as _np
    import concourse.bacc as _bacc
    from concourse import mybir as _mybir
    from concourse.bass_utils import run_bass_kernel_spmd as _run

    nc = _bacc.Bacc("TRN2", target_bir_lowering=False, num_devices=1)
    arrays, args = {}, []
    for name in _INS:
        a = _np.ascontiguousarray(inputs[name])
        arrays[f"in_{name}_dram"] = a
        args.append(nc.dram_tensor(f"in_{name}_dram", a.shape, _mybir.dt.from_np(a.dtype), kind="ExternalInput").ap())
    args.append(nc.dram_tensor("out_0_dram", (1, T, D), F32, kind="ExternalOutput").ap())
    hybrid_trunk(nc, *args)
    r = _run(nc, [arrays], core_ids=[0])
    return r.results[0]["out_0_dram"]
```
